# Optimizing a Trainium2 kernel written in Bass

```python
import jax, jax.numpy as jnp
from jax import lax
import numpy as np

D_MODEL = 1024
BATCH = 1
SEQ = 1024
DEPTH = 2
DEC_BATCH = 8
DEC_SEQ = 4
PAST_LEN = 1024
PAGE_SIZE = 128

N_META = 16
N_A_LAYERS = (DEPTH + 1) // 2
N_C_LAYERS = DEPTH // 2
W_A = D_MODEL // 2
H_A = 8
DH_A = W_A // H_A
Q_BLOCK = 128
SB_BIAS_INIT = -6.0
W_B = D_MODEL // 2
POOL_WINDOWS = (2, 4, 8, 16)
POOL_GROUPS = len(POOL_WINDOWS)
POOL_GC = W_B // POOL_GROUPS
POOL_MAX = max(POOL_WINDOWS)
INNER_C = 2 * D_MODEL
H_C = 4
DH_C = INNER_C // H_C
CONV_W = 4
CHUNK = 128
EPS = 1e-6
F32 = jnp.float32

kernel_name = 'hybrid_stickbreak_pool_mlstm_decoder_step'

def rmsnorm(x, g):
    xf = x.astype(F32)
    y = xf * lax.rsqrt(jnp.mean(xf * xf, axis=-1, keepdims=True) + EPS)
    return (y * g.astype(F32)).astype(x.dtype)

def sb_block(q, k, v, bias, q_pos, k_pos):
    z = jnp.einsum('bqhd,bkhd->bhqk', q.astype(F32), k.astype(F32)) * (DH_A ** -0.5)
    z = z + bias.astype(F32)[None, :, None, None]
    mask = k_pos[None, :] < q_pos[:, None]
    lneg = jnp.where(mask, jax.nn.log_sigmoid(-z), 0.0)
    tail = lax.cumsum(lneg, axis=3, reverse=True) - lneg
    a = jnp.where(mask, jnp.exp(jax.nn.log_sigmoid(z) + tail), 0.0)
    return jnp.einsum('bhqk,bkhd->bqhd', a, v.astype(F32))

def sb_prompt(q, k, v, bias):
    B, L = q.shape[0], q.shape[1]
    pos = jnp.arange(L)
    o_meta = sb_block(q[:, :N_META], k[:, :N_META], v[:, :N_META], bias, pos[:N_META], pos[:N_META])
    nb = (L - N_META) // Q_BLOCK
    qb = jnp.moveaxis(q[:, N_META:].reshape(B, nb, Q_BLOCK, H_A, DH_A), 1, 0)
    pb = pos[N_META:].reshape(nb, Q_BLOCK)
    o_real = lax.map(lambda a: sb_block(a[0], k, v, bias, a[1], pos), (qb, pb))
    o_real = jnp.moveaxis(o_real, 0, 1).reshape(B, L - N_META, H_A, DH_A)
    return jnp.concatenate([o_meta, o_real], axis=1)

def pool_mix(u_ext, pos, w_pool, scale):
    P = POOL_MAX - 1
    B, Lx, _ = u_ext.shape
    T = Lx - P
    uf = u_ext.astype(F32)
    cs = jnp.concatenate([jnp.zeros((B, 1, W_B), F32), jnp.cumsum(uf, axis=1)], axis=1)
    means = []
    for g, w in enumerate(POOL_WINDOWS):
        c0 = g * POOL_GC
        win = cs[:, P + 1:P + 1 + T, c0:c0 + POOL_GC] - cs[:, P + 1 - w:P + 1 - w + T, c0:c0 + POOL_GC]
        cnt = jnp.minimum(w, pos + 1).astype(F32)
        means.append(win / cnt[None, :, None])
    mean = jnp.stack(means, axis=2)
    diff = mean - uf[:, P:].reshape(B, T, POOL_GROUPS, POOL_GC)
    y = jnp.einsum('btgc,gce->btge', diff, w_pool.astype(F32)).reshape(B, T, W_B)
    return y * scale.astype(F32)

def even_mixer(xn, pos, pool_prefix, sb_fn, w_in, w_out, sb_bias, w_pool, pool_scale):
    B, T, _ = xn.shape
    proj = xn @ w_in
    q = proj[..., 0:W_A].reshape(B, T, H_A, DH_A)
    k = proj[..., W_A:2 * W_A].reshape(B, T, H_A, DH_A)
    v = proj[..., 2 * W_A:3 * W_A].reshape(B, T, H_A, DH_A)
    g_a = proj[..., 3 * W_A:4 * W_A].astype(F32)
    u = proj[..., 4 * W_A:4 * W_A + W_B]
    g_b = proj[..., 4 * W_A + W_B:].astype(F32)
    o_a = sb_fn(q, k, v, sb_bias).reshape(B, T, W_A)
    u_ext = jnp.concatenate([pool_prefix.astype(u.dtype), u], axis=1)
    o_b = pool_mix(u_ext, pos, w_pool, pool_scale)
    mixed = jnp.concatenate([o_a * jax.nn.silu(g_a), o_b * jax.nn.silu(g_b)], axis=-1).astype(xn.dtype)
    return mixed @ w_out, k, v, u_ext[:, -(POOL_MAX - 1):]

def mlstm_chunk(C, n, m, q, k, v, logi, logf):
    C = C.astype(F32)
    n = n.astype(F32)
    m = m.astype(F32)
    T = q.shape[2]
    b = jnp.cumsum(logf, axis=-1)
    causal = jnp.tril(jnp.ones((T, T), dtype=bool))
    d = jnp.where(causal, b[..., :, None] - b[..., None, :] + logi[..., None, :], -jnp.inf)
    m_inter = b + m[..., None]
    m_t = jnp.maximum(m_inter, jnp.max(d, axis=-1))
    w_inter = jnp.exp(m_inter - m_t)
    s = jnp.einsum('bhtd,bhsd->bhts', q, k) * jnp.exp(d - m_t[..., None])
    num = w_inter[..., None] * jnp.einsum('bhtd,bhde->bhte', q, C) + jnp.einsum('bhts,bhse->bhte', s, v)
    den = w_inter * jnp.einsum('bhtd,bhd->bht', q, n) + jnp.sum(s, axis=-1)
    h = num / jnp.maximum(jnp.abs(den), jnp.exp(-m_t))[..., None]
    m_new = m_t[..., -1]
    w_s = jnp.exp(b[..., -1:] - b + logi - m_new[..., None])
    decay = jnp.exp(b[..., -1] + m - m_new)
    C_new = decay[..., None, None] * C + jnp.einsum('bhsd,bhse->bhde', k * w_s[..., None], v)
    n_new = decay[..., None] * n + jnp.einsum('bhs,bhsd->bhd', w_s, k)
    return h, C_new, n_new, m_new

def mlstm_prompt(state, q, k, v, logi, logf):
    B, H, L, _ = q.shape
    h_meta, C, n, m = mlstm_chunk(*state, q[:, :, :N_META], k[:, :, :N_META], v[:, :, :N_META],
                                  logi[:, :, :N_META], logf[:, :, :N_META])
    nc = (L - N_META) // CHUNK

    def to_chunks(a):
        a = a[:, :, N_META:]
        return jnp.moveaxis(a.reshape((B, H, nc, CHUNK) + a.shape[3:]), 2, 0)

    def step(carry, xs):
        h, C1, n1, m1 = mlstm_chunk(*carry, *xs)
        return (C1, n1, m1), h

    (C, n, m), hs = lax.scan(step, (C, n, m), tuple(to_chunks(a) for a in (q, k, v, logi, logf)))
    hs = jnp.moveaxis(hs, 0, 2).reshape(B, H, L - N_META, DH_C)
    return jnp.concatenate([h_meta, hs], axis=2), C, n, m

def mlstm_sample(state, q, k, v, logi, logf):
    return mlstm_chunk(*state, q, k, v, logi, logf)

def head_layernorm(h, g):
    mu = jnp.mean(h, axis=-1, keepdims=True)
    var = jnp.mean(jnp.square(h - mu), axis=-1, keepdims=True)
    hn = (h - mu) * lax.rsqrt(var + EPS)
    B, H, T, dh = h.shape
    return jnp.transpose(hn, (0, 2, 1, 3)).reshape(B, T, H * dh) * g.astype(F32)

def odd_mixer(xn, conv_prefix, state, scan_fn, w_in, b_gate, conv_w, conv_b, w_q, w_k, w_v, skip, on_g, w_out):
    B, T, _ = xn.shape
    proj = xn @ w_in
    xm = proj[..., :INNER_C]
    z = proj[..., INNER_C:2 * INNER_C].astype(F32)
    gates = (proj[..., 2 * INNER_C:] + b_gate).astype(F32)
    logi = jnp.transpose(gates[..., :H_C], (0, 2, 1))
    logf = jnp.transpose(jax.nn.log_sigmoid(gates[..., H_C:]), (0, 2, 1))
    xm_ext = jnp.concatenate([conv_prefix.astype(xm.dtype), xm], axis=1)
    conv = conv_b.astype(F32)
    for j in range(CONV_W):
        conv = conv + xm_ext[:, j:j + T].astype(F32) * conv_w[j].astype(F32)
    ca = jax.nn.silu(conv)
    ca_h = ca.reshape(B, T, H_C, DH_C)
    q = jnp.einsum('bthd,hde->bhte', ca_h, w_q.astype(F32))
    k = jnp.einsum('bthd,hde->bhte', ca_h, w_k.astype(F32)) * (DH_C ** -0.5)
    v = jnp.einsum('bthd,hde->bhte', xm.astype(F32).reshape(B, T, H_C, DH_C), w_v.astype(F32))
    h, C, n, m = scan_fn(state, q, k, v, logi, logf)
    out = (head_layernorm(h, on_g) + skip.astype(F32) * ca) * jax.nn.silu(z)
    return out.astype(xn.dtype) @ w_out, C, n, m, xm_ext[:, -(CONV_W - 1):]

def setup_inputs(seed: int = 0) -> dict:
    key = jax.random.key(seed)
    ks = jax.random.split(key, 32)
    n_pages = PAST_LEN // PAGE_SIZE
    n_used = DEC_BATCH * n_pages
    n_pool = n_used + max(1, n_used // 4)
    perm = jax.random.permutation(ks[0], n_pool)
    page_table = perm[:n_used].reshape(DEC_BATCH, n_pages).astype(jnp.int32)

    def nrm(k, shape, s):
        return jax.random.normal(k, shape, F32) * s

    b_i = nrm(ks[21], (N_C_LAYERS, H_C), 0.1)
    b_f = jnp.linspace(3.0, 6.0, H_C, dtype=F32)[None, :] + nrm(ks[22], (N_C_LAYERS, H_C), 0.1)
    return {
        'x_prompt': nrm(ks[1], (BATCH, SEQ, D_MODEL), 1.0),
        'x_sample': nrm(ks[2], (DEC_BATCH, DEC_SEQ, D_MODEL), 1.0),
        'cache_sb_k': nrm(ks[3], (N_A_LAYERS, n_pool, PAGE_SIZE, H_A, DH_A), 1.0),
        'cache_sb_v': nrm(ks[4], (N_A_LAYERS, n_pool, PAGE_SIZE, H_A, DH_A), 1.0),
        'page_table': page_table,
        'state_pool': nrm(ks[5], (N_A_LAYERS, DEC_BATCH, POOL_MAX - 1, W_B), 1.0),
        'state_C': nrm(ks[6], (N_C_LAYERS, DEC_BATCH, H_C, DH_C, DH_C), 0.02),
        'state_n': nrm(ks[7], (N_C_LAYERS, DEC_BATCH, H_C, DH_C), 0.1),
        'state_m': nrm(ks[8], (N_C_LAYERS, DEC_BATCH, H_C), 1.0),
        'state_conv': nrm(ks[9], (N_C_LAYERS, DEC_BATCH, CONV_W - 1, INNER_C), 1.0),
        'meta_tokens': nrm(ks[10], (N_META, D_MODEL), 1.0),
        'norm_g': 1.0 + nrm(ks[11], (DEPTH, D_MODEL), 0.02),
        'final_norm_g': 1.0 + nrm(ks[12], (D_MODEL,), 0.02),
        'w_in_a': nrm(ks[13], (N_A_LAYERS, D_MODEL, 4 * W_A + 2 * W_B), D_MODEL ** -0.5),
        'w_out_a': nrm(ks[14], (N_A_LAYERS, W_A + W_B, D_MODEL), (W_A + W_B) ** -0.5),
        'sb_bias': SB_BIAS_INIT + nrm(ks[28], (N_A_LAYERS, H_A), 0.1),
        'w_pool': nrm(ks[15], (N_A_LAYERS, POOL_GROUPS, POOL_GC, POOL_GC), POOL_GC ** -0.5),
        'pool_scale': 1.0 + nrm(ks[16], (N_A_LAYERS, W_B), 0.1),
        'w_in_c': nrm(ks[17], (N_C_LAYERS, D_MODEL, 2 * INNER_C + 2 * H_C), D_MODEL ** -0.5),
        'b_gate_c': jnp.concatenate([b_i, b_f], axis=-1),
        'conv_w': nrm(ks[18], (N_C_LAYERS, CONV_W, INNER_C), CONV_W ** -0.5),
        'conv_b': nrm(ks[19], (N_C_LAYERS, INNER_C), 0.02),
        'w_q': nrm(ks[20], (N_C_LAYERS, H_C, DH_C, DH_C), DH_C ** -0.5),
        'w_k': nrm(ks[23], (N_C_LAYERS, H_C, DH_C, DH_C), DH_C ** -0.5),
        'w_v': nrm(ks[24], (N_C_LAYERS, H_C, DH_C, DH_C), DH_C ** -0.5),
        'skip_c': 1.0 + nrm(ks[25], (N_C_LAYERS, INNER_C), 0.1),
        'outnorm_g': 1.0 + nrm(ks[26], (N_C_LAYERS, INNER_C), 0.02),
        'w_out_c': nrm(ks[27], (N_C_LAYERS, INNER_C, D_MODEL), INNER_C ** -0.5),
    }

def reference(x_prompt, x_sample, cache_sb_k, cache_sb_v, page_table, state_pool, state_C, state_n, state_m,
              state_conv, meta_tokens, norm_g, final_norm_g, w_in_a, w_out_a, sb_bias, w_pool, pool_scale, w_in_c,
              b_gate_c, conv_w, conv_b, w_q, w_k, w_v, skip_c, outnorm_g, w_out_c):
    Bp = x_prompt.shape[0]
    Bs, Ts, _ = x_sample.shape
    past = page_table.shape[1] * cache_sb_k.shape[2]
    meta = jnp.broadcast_to(meta_tokens.astype(x_prompt.dtype)[None], (Bp, N_META, D_MODEL))
    h_p = jnp.concatenate([meta, x_prompt], axis=1)
    h_s = x_sample
    pos_p = jnp.arange(h_p.shape[1])
    pos_s = past + jnp.arange(Ts)
    kpos_s = jnp.arange(past + Ts)
    sbk_p, sbv_p, sbk_s, sbv_s, pool_p, pool_s = [], [], [], [], [], []
    C_p, C_s, n_p, n_s, m_p, m_s, cv_p, cv_s = [], [], [], [], [], [], [], []
    for layer in range(DEPTH):
        if layer % 2 == 0:
            ie = layer // 2
            wa = (w_in_a[ie], w_out_a[ie], sb_bias[ie], w_pool[ie], pool_scale[ie])
            zeros_pool = jnp.zeros((Bp, POOL_MAX - 1, W_B), h_p.dtype)
            y, k, v, pst = even_mixer(rmsnorm(h_p, norm_g[layer]), pos_p, zeros_pool, sb_prompt, *wa)
            h_p = h_p + y
            sbk_p.append(k)
            sbv_p.append(v)
            pool_p.append(pst)
            k_past = cache_sb_k[ie][page_table].reshape(Bs, past, H_A, DH_A)
            v_past = cache_sb_v[ie][page_table].reshape(Bs, past, H_A, DH_A)

            def sb_sample(q, k, v, bias, k_past=k_past, v_past=v_past):
                k_all = jnp.concatenate([k_past.astype(k.dtype), k], axis=1)
                v_all = jnp.concatenate([v_past.astype(v.dtype), v], axis=1)
                return sb_block(q, k_all, v_all, bias, pos_s, kpos_s)

            y, k, v, pst = even_mixer(rmsnorm(h_s, norm_g[layer]), pos_s, state_pool[ie], sb_sample, *wa)
            h_s = h_s + y
            sbk_s.append(k)
            sbv_s.append(v)
            pool_s.append(pst)
        else:
            io = layer // 2
            wc = (w_in_c[io], b_gate_c[io], conv_w[io], conv_b[io], w_q[io], w_k[io], w_v[io],
                  skip_c[io], outnorm_g[io], w_out_c[io])
            init = (jnp.zeros((Bp, H_C, DH_C, DH_C), F32), jnp.zeros((Bp, H_C, DH_C), F32),
                    jnp.zeros((Bp, H_C), F32))
            zeros_conv = jnp.zeros((Bp, CONV_W - 1, INNER_C), h_p.dtype)
            y, C, n, m, cv = odd_mixer(rmsnorm(h_p, norm_g[layer]), zeros_conv, init, mlstm_prompt, *wc)
            h_p = h_p + y
            C_p.append(C)
            n_p.append(n)
            m_p.append(m)
            cv_p.append(cv)
            st = (state_C[io], state_n[io], state_m[io])
            y, C, n, m, cv = odd_mixer(rmsnorm(h_s, norm_g[layer]), state_conv[io], st, mlstm_sample, *wc)
            h_s = h_s + y
            C_s.append(C)
            n_s.append(n)
            m_s.append(m)
            cv_s.append(cv)
    y_prompt = rmsnorm(h_p, final_norm_g)[:, N_META:]
    y_sample = rmsnorm(h_s, final_norm_g)
    return (y_prompt, y_sample,
            jnp.stack(sbk_p), jnp.stack(sbv_p), jnp.stack(sbk_s), jnp.stack(sbv_s),
            jnp.stack(pool_p), jnp.stack(pool_s),
            jnp.stack(C_p), jnp.stack(C_s), jnp.stack(n_p), jnp.stack(n_s),
            jnp.stack(m_p), jnp.stack(m_s), jnp.stack(cv_p), jnp.stack(cv_s))


_drawn_inputs = setup_inputs


def setup_inputs(seed=0):
    import zlib

    import numpy as np

    out = dict(_drawn_inputs(seed))
    spreads = {}
    factors = {}
    for name, (base, spread) in spreads.items():
        noise = np.random.default_rng([zlib.crc32(name.encode()), seed]).standard_normal(out[name].shape)
        drawn = base * np.exp(spread * noise) if base else spread * noise
        out[name] = __import__('jax').numpy.asarray(drawn.astype(out[name].dtype))
    for name, factor in factors.items():
        out[name] = (out[name] * factor).astype(out[name].dtype)
    return out
```

```python
from contextlib import ExitStack

import concourse.bass as bass
import numpy as np
from concourse import mybir

F32 = mybir.dt.float32
F32R = mybir.dt.float32r
I32 = mybir.dt.int32
ALU = mybir.AluOpType
ACT = mybir.ActivationFunctionType

P = 128
D = 1024
KD = D // P
META = 16
SEQ = 1024
B = 8
TS = 4
NS = B * TS
PROMPT = META + SEQ
R8 = 64
S0 = 32
T = PROMPT + R8
SC = PROMPT + S0
NT = SEQ // P
EPS = 1e-6

WA = 512
HA = 8
DA = 64
PAIRS = HA // 2
PAST = 1024
PAGES = PAST // P
PW = (2, 4, 8, 16)
PRE = 15
UW = PRE + PROMPT + B * (PRE + TS)

HC = 4
DH = 512
KH = DH // P
INNER = HC * DH
CW = 4
CP = CW - 1
XW = CP + PROMPT + B * (CP + TS)
XS = CP + PROMPT
NEG = -1e30
BANK = 512
CHUNKS = ((0, 512), (512, 1024), (1024, T))

C_ID, C_STRICT, C_CAUSAL, C_BLOCK8, C_DEC, C_OWN, C_RCNT, C_ONE = 0, 128, 256, 384, 448, 512, 520, 584
C_W = 585
V_NORM, V_PSCALE, V_ROWS = 0, 16, 20
W_TAP, W_BIAS, W_SKIP, W_GAMMA, W_KINDS = 0, 4, 5, 6, 7


def constant_table():
    c = np.zeros((P, C_W), np.float32)
    r = np.arange(P)
    c[:, C_ID:C_ID + P] = np.eye(P)
    c[:, C_STRICT:C_STRICT + P] = np.where(r[None, :] < r[:, None], 0, NEG)
    c[:, C_CAUSAL:C_CAUSAL + P] = np.where(r[:, None] <= r[None, :], 0, NEG)
    s, t = np.meshgrid(np.arange(R8), np.arange(R8), indexing="ij")
    meta = (s < META) & (t < META) & (s <= t)
    own = (s >= S0) & (t >= S0) & (s // TS == t // TS) & (s <= t)
    c[:R8, C_BLOCK8:C_BLOCK8 + R8] = np.where(meta | own, 0, NEG)
    for g in range(2):
        b, q = r // 32 + 4 * g, r % TS
        k = np.arange(NS)
        ok = (k[None, :] // TS == b[:, None]) & (k[None, :] % TS < q[:, None])
        c[:, C_DEC + NS * g:C_DEC + NS * (g + 1)] = np.where(ok, 0, NEG)
    c[r, C_OWN + r % NS // TS] = 1
    for g, w in enumerate(PW):
        c[:, C_RCNT + 16 * g:C_RCNT + 16 * (g + 1)] = 1 / np.minimum(w, np.arange(16) + 1)
    c[:, C_ONE] = 1
    return c


def carry_table():
    c = np.ones((HC, T), np.float32)
    c[:, 0] = 0
    c[:, META:PROMPT:P] = 0
    c[:, PROMPT] = 0
    c[:, SC::TS] = 0
    return c


def tok(ap, i):
    return ap[:, META + P * i:META + P * (i + 1)] if i < NT else ap[:, PROMPT:T]


def pieces(a, b):
    while a < b:
        e = min(b, (a // BANK + 1) * BANK)
        yield a, e
        a = e


def chain(eng, sem):
    n = [0]

    def link(ins):
        n[0] += 1
        ins.then_inc(sem, 1)
        eng.wait_ge(sem, n[0])
    return link


class Space:

    def __init__(self, nc, ctx, stage):
        self.nc, self.ctx, self.stage, self.sems = nc, ctx, stage, []
        ctx.callback(self.clear)

    def clear(self):
        if self.sems:
            self.nc.clear_and_free_semaphores(self.sems)
            self.nc.all_engine_barrier()

    def sb(self, name, shape, dt=F32):
        return self.ctx.enter_context(self.nc.sbuf_tensor(f"{self.stage}_{name}", shape, dt))

    def ps(self, name, shape):
        return self.ctx.enter_context(self.nc.psum_tensor(f"{self.stage}_{name}", shape, F32))

    def sem(self, name):
        self.sems.append(self.nc.alloc_semaphore(name=f"{self.stage}_{name}"))
        return self.sems[-1]


def load_constants(nc, d, const, vcol, wcol, bias, prefT):
    with ExitStack() as ctx:
        s = Space(nc, ctx, "const")
        vrow = s.sb("vrow", [V_ROWS, P])
        wrow = s.sb("wrow", [W_KINDS * 16, P])
        prow = s.sb("prow", [B * PRE, WA])
        ps = s.ps("ps", [P, 3, BANK])
        landed, turned, done = s.sem("landed"), s.sem("turned"), s.sem("done")
        block = ctx.enter_context(nc.Block())
        n_loads = 9

        @block.sync
        def _(sp):
            sp.dma_start(const[:, :], d["consts"]).then_inc(landed, 16)
            sp.dma_start(vrow[V_NORM:V_NORM + 16, :], d["norm_g"].rearrange("l (k p) -> (l k) p", p=P)).then_inc(landed, 16)
            sp.dma_start(vrow[V_PSCALE:V_PSCALE + 4, :], d["pool_scale"].rearrange("l (k p) -> (l k) p", p=P)).then_inc(landed, 16)
            sp.dma_start(wrow[0:64, :], d["conv_w"].rearrange("l j (k p) -> (l j k) p", p=P)).then_inc(landed, 16)
            sp.dma_start(wrow[64:80, :], d["conv_b"].rearrange("l (k p) -> (l k) p", p=P)).then_inc(landed, 16)
            sp.dma_start(wrow[80:96, :], d["skip_c"].rearrange("l (k p) -> (l k) p", p=P)).then_inc(landed, 16)
            sp.dma_start(wrow[96:112, :], d["outnorm_g"].rearrange("l (k p) -> (l k) p", p=P)).then_inc(landed, 16)
            sp.dma_start(bias[:, :], d["sb_bias"].to_broadcast([P, HA])).then_inc(landed, 16)
            sp.dma_start(prow[:, :], d["state_pool"].rearrange("l b r c -> (l b r) c")).then_inc(landed, 16)

        @block.tensor
        def _(pe):
            pe.wait_ge(landed, 16 * n_loads)
            pe.transpose(ps[:, 0, 0:V_ROWS], vrow[:, :], const[0:V_ROWS, C_ID:C_ID + V_ROWS])
            pe.transpose(ps[:, 1, 0:112], wrow[:, :], const[0:112, C_ID:C_ID + 112])
            for g in range(4):
                last = pe.transpose(ps[:, 2, 120 * g:120 * (g + 1)], prow[:, P * g:P * (g + 1)], const[0:120, C_ID:C_ID + 120])
            last.then_inc(turned, 1)

        @block.vector
        def _(dve):
            dve.wait_ge(turned, 1)
            dve.tensor_copy(vcol[:, :], ps[:, 0, 0:V_ROWS])
            dve.tensor_copy(wcol[:, :, :], ps[:, 1, 0:112].rearrange("p (a k) -> p a k", a=W_KINDS))
            dve.tensor_copy(prefT[:, :, :], ps[:, 2, 0:480].rearrange("p (g r) -> p g r", g=4)).then_inc(done, 1)


def norm_stage(nc, d, stage, const, vcol, gcol, xnT, mixT, h_dram):
    with ExitStack() as ctx:
        s = Space(nc, ctx, stage)
        x = s.sb("x", [P, 2, D])
        h = s.sb("h", [P, 2, D]) if mixT is not None else x
        sq = s.sb("sq", [P, D])
        xn = s.sb("xn", [P, 2, D])
        stat = s.sb("stat", [P, 2, 2])
        wo = s.sb("wo", [P, KD, D]) if mixT is not None else None
        yp = s.ps("yp", [P, 2, 2, BANK])
        tp = s.ps("tp", [P, 2, 2, BANK])
        x_in = [s.sem("x_in0"), s.sem("x_in1")]
        wo_in, y_full, h_ready = s.sem("wo_in"), s.sem("y_full"), s.sem("h_ready")
        ss_ready, rstd_ready, xn_ready, xt_full, xt_done = (s.sem(n) for n in ("ss_ready", "rstd_ready", "xn_ready", "xt_full", "xt_done"))
        h_out = [s.sem("h_out0"), s.sem("h_out1")]
        msq_ready, rms_ready = s.sem("msq_ready"), s.sem("rms_ready")
        edge_zero = s.sem("edge_zero")
        block = ctx.enter_context(nc.Block())
        tiles = [(2 * m + q, q) for m in range(NT // 2) for q in range(2)]
        x_rows = d["x_prompt"].rearrange("b (i p) c -> (b i) p c", p=P)
        x_done = h_ready if mixT is not None else xn_ready

        @block.sync
        def _(sp):
            if mixT is not None:
                sp.dma_start(wo[:, :, :], d["w_out_a"].rearrange("l (k p) c -> p (l k) c", p=P)).then_inc(wo_in, 16)
            for q in range(2):
                sp.dma_start(x[:, q, :], x_rows[q]).then_inc(x_in[q], 16)
            with sp.Fori(1, NT // 2) as m:
                for q in range(2):
                    sp.wait_ge(x_done, 2 * m + q - 1)
                    sp.dma_start(x[:, q, :], x_rows[bass.ds(2 * m + q, 1)].rearrange("o p c -> (o p) c")).then_inc(x_in[q], 16)
            sp.wait_ge(x_done, NT - 1)
            sp.wait_ge(edge_zero, 1)
            sp.dma_start(x[0:META, 0, :], d["meta_tokens"]).then_inc(x_in[0], 16)
            sp.dma_start(x[S0:R8, 0, :], d["x_sample"].rearrange("b t c -> (b t) c")).then_inc(x_in[0], 16)
            if mixT is not None:
                sp.wait_ge(h_out[0], 16 * (NT // 2 + 1))
                sp.wait_ge(h_out[1], 16 * (NT // 2))

        @block.tensor
        def _(pe):
            def project(i, q):
                for half in range(2):
                    for k in range(KD):
                        rows = P if i < NT else R8
                        last = pe.matmul(yp[0:rows, q, half, :], tok(mixT[:, k, :], i), wo[:, k, BANK * half:BANK * (half + 1)],
                                         start=(k == 0), stop=(k == KD - 1))
                last.then_inc(y_full, 1)

            def turn(i, q):
                rows = P if i < NT else R8
                pe.wait_ge(xn_ready, i + 1)
                if i >= 2:
                    pe.wait_ge(xt_done, i - 1)
                for k in range(KD):
                    last = pe.transpose(tp[:, q, k // 4, P * (k % 4):P * (k % 4) + rows], xn[0:rows, q, P * k:P * (k + 1)],
                                        const[0:rows, C_ID:C_ID + rows])
                last.then_inc(xt_full, 1)

            if mixT is not None:
                pe.wait_ge(wo_in, 16)
                project(0, 0)
            for i in range(NT + 1):
                if mixT is not None and i < NT:
                    if i >= 1:
                        pe.wait_ge(h_ready, i)
                    project(i + 1, (i + 1) % 2)
                turn(i, i % 2)

        @block.scalar
        def _(act):
            for i in range(NT + 1):
                q, rows = i % 2, P if i < NT else R8
                if mixT is None:
                    act.wait_ge(x_in[q], 16 * (i // 2 + 1) + 16 * (i == NT))
                else:
                    act.wait_ge(h_ready, i + 1)
                act.activation(sq[0:rows, :], h[0:rows, q, :], ACT.Square, accum_out=stat[0:rows, q, 0:1]).then_inc(ss_ready, 1)
                act.wait_ge(msq_ready, i + 1)
                act.activation(stat[0:rows, q, 0:1], stat[0:rows, q, 1:2], ACT.Sqrt).then_inc(rms_ready, 1)
                act.wait_ge(rstd_ready, i + 1)
                if i >= 2:
                    act.wait_ge(xt_full, i - 1)
                act.activation(xn[0:rows, q, :], h[0:rows, q, :], ACT.Copy, scale=stat[0:rows, q, 1:2]).then_inc(xn_ready, 1)

        @block.vector
        def _(dve):
            def add(i):
                q, rows = i % 2, P if i < NT else R8
                if i >= 2:
                    dve.wait_ge(h_out[q], 16 * (i // 2))
                    dve.wait_ge(xn_ready, i - 1)
                dve.wait_ge(y_full, i + 1)
                dve.wait_ge(x_in[q], 16 * (i // 2 + 1) + 16 * (i == NT))
                dve.tensor_tensor(h[0:rows, q, :], x[0:rows, q, :], yp[0:rows, q, :, :].rearrange("p a n -> p (a n)"), ALU.add).then_inc(h_ready, 1)

            for i in range(NT + 1):
                q, rows = i % 2, P if i < NT else R8
                if i == NT:
                    dve.wait_ge(x_done, NT - 1)
                    dve.memset(x[0:R8, 0, :], 0.0).then_inc(edge_zero, 1)
                if mixT is not None:
                    add(i)
                dve.wait_ge(ss_ready, i + 1)
                dve.tensor_scalar(stat[0:rows, q, 1:2], stat[0:rows, q, 0:1], 1.0 / D, EPS, ALU.mult, ALU.add).then_inc(msq_ready, 1)
                dve.wait_ge(rms_ready, i + 1)
                dve.reciprocal(stat[0:rows, q, 1:2], stat[0:rows, q, 0:1]).then_inc(rstd_ready, 1)
                dve.wait_ge(xt_full, i + 1)
                for k in range(KD):
                    src, g = tp[:, q, k // 4, P * (k % 4):P * (k % 4 + 1)], vcol[:, gcol + k:gcol + k + 1]
                    if i < NT:
                        last = dve.tensor_scalar(xnT[:, k, META + P * i:META + P * (i + 1)], src, g, None, ALU.mult)
                    else:
                        dve.tensor_scalar(xnT[:, k, 0:META], src[:, 0:META], g, None, ALU.mult)
                        last = dve.tensor_scalar(xnT[:, k, PROMPT:T], src[:, 0:R8], g, None, ALU.mult)
                last.then_inc(xt_done, 1)

        if mixT is not None:
            @block.gpsimd
            def _(pool):
                for i in range(NT + 1):
                    q, rows = i % 2, P if i < NT else R8
                    pool.wait_ge(h_ready, i + 1)
                    pool.dma_start(h_dram[i, 0:rows], h[0:rows, q, :]).then_inc(h_out[q], 16)


def attention_pairs(nc, d, const, biasB, xnT, mixT, qS, kS, gS, vS):
    QT = NT + 1
    STEPS = 2 * QT
    full_blocks = [0] + [i + 1 for i in range(NT)]
    groups = [-(-(n + 1) // 4) for n in full_blocks]
    GP = 2 * sum(groups)
    NG = 2
    assert GP % NG == 0 and STEPS % 2 == 0
    keys = [META + P * n for n in full_blocks]

    with ExitStack() as ctx:
        s = Space(nc, ctx, "attn")
        w = s.sb("w", [P, 4, KD, P])
        qT, kT, ga = s.sb("qT", [P, T]), s.sb("kT", [P, T]), s.sb("ga", [P, T])
        v, kt = s.sb("v", [P, NT + 1, P]), s.sb("kt", [P, NT + 1, P])
        pos, neg, a = s.sb("pos", [P, 2, PROMPT]), s.sb("neg", [P, 2, PROMPT]), s.sb("a", [P, 2, PROMPT])
        rest = s.sb("rest", [P, 2, PROMPT + 1])
        aT = s.sb("aT", [P, 2, NT + 1, P])
        biasP = s.sb("biasP", [P, 2, 2])
        ps = s.ps("ps", [P, 8, BANK])
        w_in = [s.sem(f"w_in{u}") for u in range(4)]
        proj_full, proj_done, v_full, v_done, kt_full, kt_done, kv_out = (
            s.sem(n) for n in ("proj_full", "proj_done", "v_full", "v_done", "kt_full", "kt_done", "kv_out"))
        saved = s.sem("saved")
        z_full, sig_done, rest_done, a_done, t_full, t_done, o_full, o_done, b_done, b_neg = (
            s.sem(n) for n in ("z_full", "sig_done", "rest_done", "a_done", "t_full", "t_done", "o_full", "o_done", "b_done", "b_neg"))
        one_set, passed = s.sem("one_set"), s.sem("passed")
        block = ctx.enter_context(nc.Block())
        KV_DMAS = 6

        def gbase(j, t):
            return j * GP // 2 + sum(groups[:t])

        @block.sync
        def _(sp):
            cols = (0, WA, 3 * WA, 2 * WA)

            def load(p):
                for u in range(4):
                    if not isinstance(p, int):
                        if u < 3:
                            sp.wait_ge(proj_full, 3 * p - 2 + u)
                        else:
                            sp.wait_ge(v_full, 3 * p)
                    src = d["w_in_a"].rearrange("l (k p) c -> p (l k) c", p=P)
                    sp.dma_start(w[:, u], src[:, :, bass.ds(cols[u] + P * p, P)]).then_inc(w_in[u], 16)

            def store(p):
                sp.wait_ge(v_done, 3 * p + 3)
                sp.wait_ge(kt_done, 3 * p + 3)
                for src, pr, sa in ((kt, "out_kp", "out_ks"), (v, "out_vp", "out_vs")):
                    prompt = d[pr].rearrange("l b t h c -> (l b t) (h c)")
                    c = bass.ds(P * p, P)
                    sp.dma_start(prompt[META:PROMPT].rearrange("(i p) c -> p i c", p=P)[:, :, c], src[:, 0:NT, :]).then_inc(kv_out, 16)
                    sp.dma_start(prompt[0:META, c], src[0:META, NT, :]).then_inc(kv_out, 16)
                    sp.dma_start(d[sa].rearrange("l b t h c -> (l b t) (h c)")[:, c], src[S0:R8, NT, :]).then_inc(kv_out, 16)

            load(0)
            with sp.Fori(1, PAIRS) as p:
                store(p - 1)
                load(p)
            store(PAIRS - 1)
            sp.wait_ge(kv_out, 16 * KV_DMAS * PAIRS + 16)

        @block.tensor
        def _(pe):
            def wait_proj(u):
                pe.wait_ge(w_in[u], 16 * p + 16)

            def project(u, bank):
                wait_proj(u)
                for c, (c0, c1) in enumerate(CHUNKS):
                    for k in range(KD):
                        last = pe.matmul(ps[:, bank + c, 0:c1 - c0], w[:, u, k, :], xnT[:, k, c0:c1], start=(k == 0), stop=(k == KD - 1))
                last.then_inc(proj_full, 1)

            def scores(j, t):
                n = j * QT + t
                rows = R8 if t == 0 else P
                set_ = 2 * (n % 2)
                if n >= 2:
                    pe.wait_ge(sig_done, STEPS * p + n - 1)
                if t == 0:
                    pe.sem_inc(passed, 1)
                q = tok(qT, NT if t == 0 else t - 1)[DA * j:DA * (j + 1)]
                L = keys[t]
                mask = (L - P, L) if t else (0, META)
                if L > 2 * BANK and n >= 3:
                    pe.wait_ge(o_done, STEPS * p + n - 1)
                for c0, c1 in pieces(0, L):
                    out = ps[0:rows, set_ + c0 // BANK, 0:c1 - c0] if c0 < 2 * BANK else ps[0:rows, 6 + (n + 1) % 2, 0:META]
                    m0, m1 = max(c0, mask[0]), min(c1, mask[1])
                    last = pe.matmul(out, q, kT[DA * j:DA * (j + 1), c0:c1], start=True, stop=(m0 >= m1))
                    if m0 < m1:
                        last = pe.matmul(out[:, m0 - c0:m1 - c0], const[:, C_ID:C_ID + rows],
                                         const[:, C_STRICT + m0 - mask[0]:C_STRICT + m1 - mask[0]], start=False, stop=True)
                last.then_inc(z_full, 1)

            def turn(j, t):
                n = j * QT + t
                rows = META if t == 0 else P
                pe.wait_ge(a_done, STEPS * p + n + 1)
                order = list(range(full_blocks[t])) + [NT]
                for g in range(groups[t]):
                    u = gbase(j, t) + g
                    pe.wait_ge(t_done, GP * p + u + 1)
                    if t == 0:
                        pe.sem_inc(passed, 1)
                    for m, b in enumerate(order[4 * g:4 * g + 4]):
                        c0, c1 = (0, META) if b == NT else (META + P * b, META + P * (b + 1))
                        last = pe.transpose(ps[0:c1 - c0, 4 + u % NG, P * m:P * m + rows], a[0:rows, n % 2, c0:c1], const[0:rows, C_ID:C_ID + rows])
                    last.then_inc(t_full, 1)

            def weigh(j, t):
                n = j * QT + t
                rows = META if t == 0 else P
                pe.wait_ge(t_done, GP * p + gbase(j, t) + groups[t] + NG)
                if n >= 2:
                    pe.wait_ge(o_done, STEPS * p + n)
                out = ps[DA * j:DA * (j + 1), 6 + n % 2, 0:rows]
                for b in range(full_blocks[t]):
                    pe.matmul(out, v[:, b, DA * j:DA * (j + 1)], aT[:, n % 2, b, 0:rows], start=(b == 0), stop=False)
                pe.matmul(out, v[0:META, NT, DA * j:DA * (j + 1)], aT[0:META, n % 2, NT, 0:rows],
                          start=(full_blocks[t] == 0), stop=True).then_inc(o_full, 1)

            with pe.Fori(0, PAIRS) as p:
                pe.wait_ge(o_done, STEPS * p + 1)
                project(0, 0)
                project(1, 3)
                wait_proj(3)
                for g in range(3):
                    if g == 2:
                        pe.wait_ge(v_done, 3 * p + 1)
                    ids = range(4 * g, min(4 * g + 4, NT + 1))
                    for i in ids:
                        for k in range(KD):
                            rows = P if i < NT else R8
                            last = pe.matmul(ps[0:rows, 6 + g % 2, P * (i % 4):P * (i % 4 + 1)], tok(xnT[:, k, :], i), w[:, 3, k, :],
                                             start=(k == 0), stop=(k == KD - 1))
                    last.then_inc(v_full, 1)
                pe.wait_ge(proj_done, 3 * p + 1)
                project(2, 0)
                pe.wait_ge(proj_done, 3 * p + 2)
                for g in range(3):
                    for i in range(4 * g, min(4 * g + 4, NT + 1)):
                        rows = P if i < NT else R8
                        last = pe.transpose(ps[0:rows, 3 + g, P * (i % 4):P * (i % 4 + 1)], tok(kT, i), const[:, C_ID:C_ID + P])
                    last.then_inc(kt_full, 1)
                pe.wait_ge(proj_done, 3 * p + 3)
                pe.wait_ge(kt_done, 3 * p + 3)
                for n in range(STEPS + 2):
                    if n < STEPS:
                        scores(n // QT, n % QT)
                    if 1 <= n <= STEPS:
                        turn((n - 1) // QT, (n - 1) % QT)
                    if n >= 2:
                        weigh((n - 2) // QT, (n - 2) % QT)

        @block.scalar
        def _(act):
            act.sem_inc(t_done, NG)
            with act.Fori(0, PAIRS) as p:
                act.wait_ge(proj_full, 3 * p + 1)
                act.activation(qT[:, :], ps[:, 0:3, :].rearrange("p a n -> p (a n)")[:, 0:T], ACT.Copy, scale=DA ** -0.5).then_inc(proj_done, 1)
                act.wait_ge(proj_full, 3 * p + 2)
                act.activation(kT[:, :], ps[:, 3:6, :].rearrange("p a n -> p (a n)")[:, 0:T], ACT.Copy).then_inc(proj_done, 1)
                act.wait_ge(proj_full, 3 * p + 3)
                act.activation(ga[:, :], ps[:, 0:3, :].rearrange("p a n -> p (a n)")[:, 0:T], ACT.Silu).then_inc(proj_done, 1)
                act.wait_ge(b_done, 2 * p + 2)

                def sigmoids(n):
                    j, t = divmod(n, QT)
                    rows, L, set_ = META if t == 0 else P, keys[t], 2 * (n % 2)
                    act.wait_ge(z_full, STEPS * p + n + 1)
                    if n >= 2:
                        act.wait_ge(a_done, STEPS * p + n - 1)
                    z = ps[0:rows, set_:set_ + 2, :].rearrange("p a n -> p (a n)")[:, 0:min(L, 2 * BANK)]
                    parts = [(z, 0, min(L, 2 * BANK))]
                    if L > 2 * BANK:
                        parts.append((ps[0:rows, 6 + (n + 1) % 2, 0:META], 2 * BANK, L))
                    for zz, c0, c1 in parts:
                        act.activation(pos[0:rows, n % 2, c0:c1], zz, ACT.Sigmoid, bias=biasP[0:rows, 0, j:j + 1])
                        last = act.activation(neg[0:rows, n % 2, c0:c1], zz, ACT.Sigmoid, bias=biasP[0:rows, 1, j:j + 1], scale=-1.0)
                    last.then_inc(sig_done, 1)

                def copy_turned(n):
                    j, t = divmod(n, QT)
                    rows = META if t == 0 else P
                    if n >= 2:
                        act.wait_ge(o_full, STEPS * p + n - 1)
                    for g in range(groups[t]):
                        u = gbase(j, t) + g
                        act.wait_ge(t_full, GP * p + u + 1)
                        m = min(4, full_blocks[t] - 4 * g)
                        bank = ps[:, 4 + u % NG, :].rearrange("p (m r) -> p m r", r=P)
                        if m > 0:
                            last = act.activation(aT[:, n % 2, 4 * g:4 * g + m, :], bank[:, 0:m, :], ACT.Copy)
                        if g == groups[t] - 1:
                            last = act.activation(aT[0:META, n % 2, NT, 0:rows], bank[0:META, m, 0:rows], ACT.Copy)
                        last.then_inc(t_done, 1)

                for n in range(STEPS + 1):
                    if n < STEPS:
                        sigmoids(n)
                    if n >= 1:
                        copy_turned(n - 1)

        @block.vector
        def _(dve):
            dve.sem_inc(o_done, 1)
            dve.sem_inc(kv_out, 16)
            dve.memset(rest[:, :, :], 1.0).then_inc(one_set, 1)
            with dve.Fori(0, PAIRS) as p:
                dve.wait_ge(o_done, STEPS * p + 1)
                dve.wait_ge(kv_out, 16 * KV_DMAS * p + 16)
                for g in range(3):
                    dve.wait_ge(v_full, 3 * p + g + 1)
                    bank = ps[:, 6 + g % 2, :].rearrange("p (m r) -> p m r", r=P)
                    if g < 2:
                        dve.tensor_copy(v[:, 4 * g:4 * g + 4, :], bank).then_inc(v_done, 1)
                    else:
                        dve.tensor_scalar(vS[S0:R8, bass.ds(P * p, P)], ps[S0:R8, 6, 0:P], 1.0, None, ALU.mult)
                        dve.tensor_copy(v[0:R8, NT, :], bank[0:R8, 0, :]).then_inc(v_done, 1)
                for g in range(3):
                    dve.wait_ge(kt_full, 3 * p + g + 1)
                    bank = ps[:, 3 + g, :].rearrange("p (m r) -> p m r", r=P)
                    if g < 2:
                        dve.tensor_copy(kt[:, 4 * g:4 * g + 4, :], bank).then_inc(kt_done, 1)
                    else:
                        dve.tensor_copy(kt[0:R8, NT, :], bank[0:R8, 0, :]).then_inc(kt_done, 1)
                dve.wait_ge(proj_done, 3 * p + 3)
                for src, dst in ((qT, qS), (kT, kS), (ga, gS)):
                    dve.tensor_scalar(dst[:, bass.ds(p, 1), :].rearrange("p o n -> p (o n)"), src[:, SC:T], 1.0, None, ALU.mult).then_inc(saved, 1)
                pair_bias = biasB[:, bass.ds(2 * p, 2)]
                dve.tensor_scalar(biasP[:, 0, :], pair_bias, 1.0, None, ALU.mult).then_inc(b_done, 1)
                dve.tensor_scalar(biasP[:, 1, :], pair_bias, -1.0, None, ALU.mult).then_inc(b_done, 1)

                def weights(n):
                    j, t = divmod(n, QT)
                    rows, L = META if t == 0 else P, keys[t]
                    dve.wait_ge(sig_done, STEPS * p + n + 1)
                    if n == 0:
                        dve.wait_ge(one_set, 1)
                    if n >= 2:
                        dve.wait_ge(a_done, STEPS * p + n - 1)
                    dve.tensor_tensor_scan(rest[0:rows, n % 2, PROMPT - L:PROMPT][:, ::-1], neg[0:rows, n % 2, 0:L][:, ::-1],
                                           neg[0:rows, n % 2, 0:L][:, ::-1], 1.0, ALU.mult, ALU.bypass).then_inc(rest_done, 1)
                    dve.wait_ge(rest_done, STEPS * p + n + 1)
                    if n >= 2:
                        j2, t2 = divmod(n - 2, QT)
                        dve.wait_ge(t_full, GP * p + gbase(j2, t2) + groups[t2])
                    dve.tensor_tensor(a[0:rows, n % 2, 0:L], pos[0:rows, n % 2, 0:L], rest[0:rows, n % 2, PROMPT - L + 1:PROMPT + 1], ALU.mult).then_inc(a_done, 1)

                def output(n):
                    j, t = divmod(n, QT)
                    rows = META if t == 0 else P
                    c0 = PROMPT if t == 0 else META + P * (t - 1)
                    dve.wait_ge(o_full, STEPS * p + n + 1)
                    dve.tensor_tensor(mixT[DA * j:DA * (j + 1), bass.ds(p, 1), c0:c0 + rows].rearrange("p o n -> p (o n)"),
                                      ps[DA * j:DA * (j + 1), 6 + n % 2, 0:rows],
                                      ga[DA * j:DA * (j + 1), c0:c0 + rows], ALU.mult).then_inc(o_done, 1)

                for n in range(STEPS + 2):
                    if n < STEPS:
                        weights(n)
                    if n >= 2:
                        output(n - 2)


def pool_groups(nc, d, const, vcol, prefT, xnT, mixT, table, vp, v_in):
    with ExitStack() as ctx:
        s = Space(nc, ctx, "pool")
        w = s.sb("w", [P, 2, 2, KD, P])
        wp = s.sb("wp", [P, 4, P])
        u = s.sb("u", [P, 2, UW])
        un = s.sb("un", [P, 2, NS])
        win = s.sb("win", [P, 2, UW])
        gb = s.sb("gb", [P, 2, T])
        edge = s.sb("edge", [P, PRE])
        last_rows = s.sb("last_rows", [PRE, WA])
        new_rows = s.sb("new_rows", [NS, WA])
        ps = s.ps("ps", [P, 8, BANK])
        w_in = [s.sem("w_in0"), s.sem("w_in1")]
        table_in, wp_in, u_full, g_full, u_done, g_done, y_full, y_done, diff_done, link_s, rows_full, rows_done, out = (
            s.sem(n) for n in ("table_in", "wp_in", "u_full", "g_full", "u_done", "g_done", "y_full", "y_done", "diff_done", "link", "rows_full", "rows_done", "out"))
        block = ctx.enter_context(nc.Block())

        def sample_u(ap):
            return bass.AP(ap.tensor, ap.offset + PRE + PROMPT + PRE, [ap.ap[0], [PRE + TS, B], [1, TS]])

        @block.sync
        def _(sp):
            src = d["w_in_a"].rearrange("l (k p) c -> p (l k) c", p=P)
            sp.dma_start(wp[:, :, :], d["w_pool"].rearrange("l g c e -> c (l g) e")).then_inc(wp_in, 16)
            sp.dma_start(table[:, :], d["page_table"].rearrange("(o b) n -> o (b n)", o=1)).then_inc(table_in, 16)
            for g in range(4):
                if g == 2:
                    sp.wait_ge(table_in, 16)
                    for b in range(B // 2):
                        load_pages(sp, table, d["cache_sb_v"].rearrange("l n p h c -> (l n) p (h c)"), b, 0, PAGES, vp[:, b], v_in[b])
                if g >= 2:
                    sp.wait_ge(g_full, g - 1)
                for a in range(2):
                    c0 = 4 * WA + a * WA + P * g
                    sp.dma_start(w[:, g % 2, a], src[:, :, c0:c0 + P]).then_inc(w_in[g % 2], 16)
            old = d["state_pool"].rearrange("l b r c -> (l b) r c")
            new = d["out_pool_s"].rearrange("l b r c -> (l b) r c")
            sp.dma_start(new[:, 0:PRE - TS, :], old[:, TS:PRE, :]).then_inc(out, 16)
            sp.wait_ge(rows_done, 2)
            sp.dma_start(d["out_pool_p"].rearrange("l b r c -> (l b r) c"), last_rows[:, :]).then_inc(out, 16)
            sp.dma_start(new[:, PRE - TS:PRE, :], new_rows[:, :]).then_inc(out, 16)
            sp.wait_ge(out, 48)

        @block.tensor
        def _(pe):
            def project(g, a, bank, full):
                for c, (c0, c1) in enumerate(CHUNKS):
                    for k in range(KD):
                        last = pe.matmul(ps[:, bank + c, 0:c1 - c0], w[:, g % 2, a, k, :], xnT[:, k, c0:c1], start=(k == 0), stop=(k == KD - 1))
                last.then_inc(full, 1)

            for g in range(4):
                pe.wait_ge(w_in[g % 2], 32 * (g // 2 + 1))
                if g >= 1:
                    pe.wait_ge(y_done, g)
                project(g, 0, 0, u_full)
                if g >= 1:
                    pe.wait_ge(g_done, g)
                project(g, 1, 3, g_full)
                pe.wait_ge(u_done, g + 1)
                if g == 0:
                    pe.wait_ge(wp_in, 16)
                uu = u[:, g % 2, :]
                pe.transpose(ps[0:PRE, 6, P * g:P * (g + 1)], uu[:, PROMPT:PROMPT + PRE], const[:, C_ID:C_ID + P])
                pe.transpose(ps[0:NS, 7, P * g:P * (g + 1)], un[:, g % 2, :], const[:, C_ID:C_ID + P]).then_inc(rows_full, 1)
                pe.wait_ge(diff_done, g + 1)
                ww = win[:, 0, :]
                for c, (c0, c1) in enumerate(((0, 512), (512, 1024), (1024, PROMPT))):
                    pe.matmul(ps[:, c, 0:c1 - c0], wp[:, g, :], ww[:, PRE + c0:PRE + c1], start=True, stop=True)
                pe.matmul(ps[:, 2, META:2 * META], wp[:, g, :], ww[:, PRE:PRE + META], start=True, stop=True)
                pe.matmul(ps[:, 2, META + S0:META + R8], wp[:, g, :], sample_u(ww), start=True, stop=True).then_inc(y_full, 1)

        @block.scalar
        def _(act):
            for g in range(4):
                act.wait_ge(u_full, g + 1)
                uu = u[:, g % 2, :]
                act.activation(uu[:, PRE:PRE + PROMPT], ps[:, 0:3, :].rearrange("p a n -> p (a n)")[:, 0:PROMPT], ACT.Copy)
                act.activation(un[:, g % 2, :], ps[:, 2, META + S0:META + R8], ACT.Copy)
                act.activation(sample_u(uu), ps[:, 2, META + S0:META + R8].rearrange("p (b t) -> p b t", t=TS), ACT.Copy).then_inc(u_done, 1)
                act.wait_ge(g_full, g + 1)
                if g >= 2:
                    act.wait_ge(y_done, g - 1)
                act.activation(gb[:, g % 2, :], ps[:, 3:6, :].rearrange("p a n -> p (a n)")[:, 0:T], ACT.Silu).then_inc(g_done, 1)

        @block.vector
        def _(dve):
            link = chain(dve, link_s)
            link(dve.memset(u[:, :, 0:PRE], 0.0))
            link(dve.memset(mixT[:, :, PROMPT + META:SC], 0.0))
            for g, wd in enumerate(PW):
                uu = u[:, g % 2, :]
                pre = bass.AP(uu.tensor, uu.offset + PRE + PROMPT, [uu.ap[0], [PRE + TS, B], [1, PRE]])
                if g >= 1:
                    dve.wait_ge(y_full, g)
                link(dve.tensor_copy(pre, prefT[:, g, :].rearrange("p (b r) -> p b r", r=PRE)))
                dve.wait_ge(u_done, g + 1)
                src, step, side = uu, 1, 0
                while step < wd:
                    dst = win[:, side, :]
                    link(dve.tensor_tensor(dst[:, 2 * step - 1:UW], src[:, 2 * step - 1:UW], src[:, step - 1:UW - step], ALU.add))
                    src, step, side = dst, 2 * step, 1 - side
                n_edge = PRE
                link(dve.tensor_tensor(edge[:, :], src[:, PRE:PRE + n_edge], const[:, C_RCNT + 16 * g:C_RCNT + 16 * g + n_edge], ALU.mult))
                link(dve.scalar_tensor_tensor(win[:, 0, PRE:UW], src[:, PRE:UW], 1.0 / wd, uu[:, PRE:UW], ALU.mult, ALU.subtract))
                dve.tensor_tensor(win[:, 0, PRE:PRE + n_edge], edge[:, :], uu[:, PRE:PRE + n_edge], ALU.subtract).then_inc(diff_done, 1)
                dve.wait_ge(y_full, g + 1)
                dve.wait_ge(g_done, g + 1)
                for c0, c1 in ((0, PROMPT + META), (SC, T)):
                    last = dve.scalar_tensor_tensor(mixT[:, PAIRS + g, c0:c1], ps[:, 0:3, :].rearrange("p a n -> p (a n)")[:, c0:c1],
                                                    vcol[:, V_PSCALE + g:V_PSCALE + g + 1], gb[:, g % 2, c0:c1], ALU.mult, ALU.mult)
                last.then_inc(y_done, 1)
            dve.wait_ge(rows_full, 4)
            dve.tensor_copy(last_rows[:, :], ps[0:PRE, 6, :]).then_inc(rows_done, 1)
            dve.tensor_copy(new_rows[:, :], ps[0:NS, 7, :]).then_inc(rows_done, 1)


def load_pages(eng, table, cache, b, j0, n, dst, sem):
    for j in range(n):
        page = eng.value_load(table[0:1, PAGES * b + j0 + j:PAGES * b + j0 + j + 1], min_val=0, max_val=cache.shape[0] - 1)
        eng.dma_start(dst[:, j, :], cache[bass.ds(page, 1)].rearrange("o p c -> (o p) c")).then_inc(sem, 16)


def decode_attention(nc, d, const, xnT, mixT, qS, kS, gS, vS, table, vp, v_in):
    G, BG = 2, B // 2
    HALF = PAGES // 2
    LK = PAST + NS
    KS = 4
    units = [(b, f) for b in range(B) for f in range(2)]
    with ExitStack() as ctx:
        s = Space(nc, ctx, "dec")
        qB = s.sb("qB", [P, PAIRS, B, HA * TS])
        kp = xnT.rearrange("p k t -> p (k t)")[:, 0:KS * HALF * WA].rearrange("p (s j c) -> p s j c", s=KS, c=WA)
        kT = s.sb("kT", [P, 2, PAIRS, HALF * P])
        biasR = s.sb("biasR", [P, 2])
        zn = s.sb("zn", [P, NS])
        pos, neg, a = s.sb("pos", [P, LK]), s.sb("neg", [P, LK]), s.sb("a", [P, LK])
        rest = s.sb("rest", [P, LK + 1])
        aT = s.sb("aT", [P, PAGES, P])
        aN = s.sb("aN", [R8, P])
        oS = s.sb("oS", [P, WA])
        ps = s.ps("ps", [P, 8, BANK])
        bias_in, q_zero, q_set, bias_set = (s.sem(n) for n in ("bias_in", "q_zero", "q_set", "bias_set"))
        k_in = [s.sem(f"k_in{j}") for j in range(KS)]
        kt_full, kt_done, z_full, zn_set, sig_done, link_s, a_done, t_full, t_done, o_full, o_saved, ot_full, o_done = (
            s.sem(n) for n in ("kt_full", "kt_done", "z_full", "zn_set", "sig_done", "link", "a_done", "t_full", "t_done", "o_full", "o_saved", "ot_full", "o_done"))
        block = ctx.enter_context(nc.Block())

        @block.sync
        def _(sp):
            cache_k = d["cache_sb_k"].rearrange("l n p h c -> (l n) p (h c)")
            for u, (b, f) in enumerate(units):
                if u >= KS:
                    sp.wait_ge(z_full, u - KS + 1)
                load_pages(sp, table, cache_k, b, HALF * f, HALF, kp[:, u % KS], k_in[u % KS])

        @block.gpsimd
        def _(pool):
            pool.memset(qB[:, :, :, :], 0.0).then_inc(q_zero, 1)

        @block.tensor
        def _(pe):
            def turn_page(u, pg):
                n = HALF * u + pg
                if pg == 0:
                    pe.wait_ge(k_in[u % KS], 16 * HALF * (u // KS + 1))
                if n >= 2:
                    pe.wait_ge(kt_done, n - 1)
                for c in range(PAIRS):
                    last = pe.transpose(ps[:, 4 + n % 2, P * c:P * (c + 1)], kp[:, u % KS, pg, P * c:P * (c + 1)], const[:, C_ID:C_ID + P])
                last.then_inc(kt_full, 1)

            def scores(u):
                b, f = units[u]
                r = 32 * (b % BG)
                pe.wait_ge(kt_done, HALF * (u + 1))
                if u == 0:
                    pe.wait_ge(q_set, 1)
                if u == BG * 2:
                    pe.wait_ge(sig_done, 1)
                for c in range(PAIRS):
                    last = pe.matmul(ps[r:r + 32, f, :], qB[:, c, b, :], kT[:, u % 2, c, :], start=(c == 0), stop=(c == PAIRS - 1))
                if f == 1:
                    for c in range(PAIRS):
                        last = pe.matmul(ps[r:r + 32, 2, 0:NS], qB[:, c, b, :], kS[:, c, :], start=(c == 0), stop=(c == PAIRS - 1))
                last.then_inc(z_full, 1)

            def turn_weights(g):
                pe.wait_ge(a_done, g + 1)
                for m in range(3):
                    n = 3 * g + m
                    if n >= 1:
                        pe.wait_ge(t_done, n)
                    if m < 2:
                        for j in range(4):
                            last = pe.transpose(ps[:, 6, P * j:P * (j + 1)], a[:, P * (4 * m + j):P * (4 * m + j + 1)], const[:, C_ID:C_ID + P])
                    else:
                        last = pe.transpose(ps[0:NS, 6, 0:P], a[:, PAST:LK], const[:, C_ID:C_ID + P])
                    last.then_inc(t_full, 1)

            def output(b):
                g, bb = divmod(b, BG)
                if bb == 0:
                    pe.wait_ge(t_done, 3 * (g + 1))
                    if g >= 1:
                        pe.wait_ge(o_saved, g)
                    pe.matmul(ps[:, 7, :], aN[S0:R8, :], vS[S0:R8, :], start=True, stop=False)
                pe.wait_ge(v_in[bb], 16 * PAGES * (g + 1))
                r = 32 * bb
                for j in range(PAGES):
                    last = pe.matmul(ps[r:r + 32, 7, :], aT[:, j, r:r + 32], vp[:, bb, j, :], start=False, stop=(j == PAGES - 1))
                last.then_inc(o_full, 1)

            def turn_output(g):
                pe.wait_ge(o_saved, g + 1)
                if g >= 1:
                    pe.wait_ge(o_done, g)
                for c in range(PAIRS):
                    last = pe.transpose(ps[:, 3, P * c:P * (c + 1)], oS[:, P * c:P * (c + 1)], const[:, C_ID:C_ID + P])
                last.then_inc(ot_full, 1)

            for u in range(2 * B):
                for pg in range(HALF):
                    turn_page(u, pg)
                scores(u)
                if u == 2 * BG:
                    turn_weights(0)
                elif 2 * BG < u <= 3 * BG:
                    output(u - 2 * BG - 1)
                elif u == 3 * BG + 1:
                    turn_output(0)
            turn_weights(1)
            for b in range(BG, B):
                output(b)
            turn_output(1)

        @block.scalar
        def _(act):
            for b in range(BG):
                for h in range(HA):
                    r = 32 * b + TS * h
                    act.dma_start(biasR[r:r + TS, 0:1], d["sb_bias"][:, h:h + 1].to_broadcast([TS, 1])).then_inc(bias_in, 16)
            cache_v = d["cache_sb_v"].rearrange("l n p h c -> (l n) p (h c)")
            act.wait_ge(bias_set, 1)
            for g in range(G):
                act.wait_ge(z_full, 2 * BG * (g + 1))
                if g >= 1:
                    act.wait_ge(a_done, g)
                z = ps[:, 0:2, :].rearrange("p a n -> p (a n)")
                act.activation(pos[:, 0:PAST], z, ACT.Sigmoid, bias=biasR[:, 0:1])
                act.activation(neg[:, 0:PAST], z, ACT.Sigmoid, bias=biasR[:, 1:2], scale=-1.0)
                act.wait_ge(zn_set, g + 1)
                act.activation(pos[:, PAST:LK], zn[:, :], ACT.Sigmoid, bias=biasR[:, 0:1])
                act.activation(neg[:, PAST:LK], zn[:, :], ACT.Sigmoid, bias=biasR[:, 1:2], scale=-1.0).then_inc(sig_done, 1)
                for m in range(3):
                    act.wait_ge(t_full, 3 * g + m + 1)
                    if g >= 1 and m == 0:
                        act.wait_ge(o_full, BG * g)
                    if m < 2:
                        act.activation(aT[:, 4 * m:4 * m + 4, :], ps[:, 6, :].rearrange("p (j r) -> p j r", r=P), ACT.Copy).then_inc(t_done, 1)
                    else:
                        act.activation(aN[S0:R8, :], ps[0:NS, 6, 0:P], ACT.Copy).then_inc(t_done, 1)
                for b in range(BG * (g + 1), B):
                    act.wait_ge(o_full, b - BG + 1)
                    load_pages(act, table, cache_v, b, 0, PAGES, vp[:, b % BG], v_in[b % BG])

        @block.vector
        def _(dve):
            link = chain(dve, link_s)
            dve.wait_ge(q_zero, 1)
            for c in range(PAIRS):
                for j in range(2):
                    dst = qB[DA * j:DA * (j + 1), c, :, 8 * c + TS * j:8 * c + TS * (j + 1)]
                    last = dve.tensor_copy(dst, qS[DA * j:DA * (j + 1), c, :].rearrange("p (b t) -> p b t", t=TS))
            last.then_inc(q_set, 1)
            dve.wait_ge(bias_in, 16 * BG * HA)
            dve.tensor_scalar(biasR[:, 1:2], biasR[:, 0:1], -1.0, None, ALU.mult).then_inc(bias_set, 1)
            def copy_keys(u):
                for pg in range(HALF):
                    n = HALF * u + pg
                    dve.wait_ge(kt_full, n + 1)
                    if u >= 2 and pg == 0:
                        dve.wait_ge(z_full, u - 1)
                    dve.tensor_copy(kT[:, u % 2, :, P * pg:P * (pg + 1)], ps[:, 4 + n % 2, :].rearrange("p (c r) -> p c r", r=P)).then_inc(kt_done, 1)

            def weights(g):
                dve.wait_ge(z_full, 2 * BG * (g + 1))
                if g >= 1:
                    dve.wait_ge(sig_done, g)
                dve.tensor_tensor(zn[:, :], ps[:, 2, 0:NS], const[:, C_DEC + NS * g:C_DEC + NS * (g + 1)], ALU.add).then_inc(zn_set, 1)
                if g == 0:
                    link(dve.memset(rest[:, LK:LK + 1], 1.0))
                dve.wait_ge(sig_done, g + 1)
                link(dve.tensor_tensor_scan(rest[:, 0:LK][:, ::-1], neg[:, ::-1], neg[:, ::-1], 1.0, ALU.mult, ALU.bypass))
                if g >= 1:
                    dve.wait_ge(t_full, 3 * g)
                dve.tensor_tensor(a[:, :], pos[:, :], rest[:, 1:LK + 1], ALU.mult).then_inc(a_done, 1)

            def save(g):
                dve.wait_ge(o_full, BG * (g + 1))
                dve.tensor_copy(oS[:, :], ps[:, 7, :]).then_inc(o_saved, 1)

            def outputs(g):
                dve.wait_ge(ot_full, g + 1)
                for c in range(PAIRS):
                    for j in range(2):
                        r = slice(DA * j, DA * (j + 1))
                        rows = ps[r, 3, P * c:P * (c + 1)].rearrange("p (b x) -> p b x", b=BG)[:, :, 8 * c + TS * j:8 * c + TS * (j + 1)]
                        c0 = TS * BG * g
                        last = dve.tensor_tensor(mixT[r, c, SC + c0:SC + c0 + TS * BG].rearrange("p (b t) -> p b t", t=TS), rows,
                                                 gS[r, c, c0:c0 + TS * BG].rearrange("p (b t) -> p b t", t=TS), ALU.mult)
                last.then_inc(o_done, 1)

            for u in range(2 * BG):
                copy_keys(u)
            weights(0)
            for u in range(2 * BG, 4 * BG):
                copy_keys(u)
                if u == 3 * BG:
                    save(0)
            outputs(0)
            weights(1)
            save(1)
            outputs(1)


_OUTS = {
    "out_yp": (1, SEQ, D), "out_ys": (B, TS, D),
    "out_kp": (1, 1, PROMPT, HA, DA), "out_vp": (1, 1, PROMPT, HA, DA),
    "out_ks": (1, B, TS, HA, DA), "out_vs": (1, B, TS, HA, DA),
    "out_pool_p": (1, 1, PRE, WA), "out_pool_s": (1, B, PRE, WA),
    "out_C_p": (1, 1, HC, DH, DH), "out_C_s": (1, B, HC, DH, DH),
    "out_n_p": (1, 1, HC, DH), "out_n_s": (1, B, HC, DH),
    "out_m_p": (1, 1, HC), "out_m_s": (1, B, HC),
    "out_conv_p": (1, 1, CP, INNER), "out_conv_s": (1, B, CP, INNER),
}
_RETURNS = ("out_yp", "out_ys", "out_kp", "out_vp", "out_ks", "out_vs", "out_pool_p", "out_pool_s", "out_C_p", "out_C_s",
            "out_n_p", "out_n_s", "out_m_p", "out_m_s", "out_conv_p", "out_conv_s")


Q_G, Q_INTER, Q_FLOOR, Q_STATE = range(4)


def gate_stage(nc, d, const, xnT, cols, decay8, preC, gate_dram):
    with ExitStack() as ctx:
        s = Space(nc, ctx, "gate")
        wg = s.sb("wg", [P, KD, S0 + HC])
        gb = s.sb("gb", [HC, 2])
        m0 = s.sb("m0", [HC, B])
        carry = s.sb("carry", [HC, T])
        li, f, e, lf, b, m, u, mp = (s.sb(n, [HC, T]) for n in ("li", "f", "e", "lf", "b", "m", "u", "mp"))
        q = s.sb("q", [HC, 4, T])
        dec = s.sb("dec", [HC, NT + 1 + B])
        crow = s.sb("crow", [B * CP, INNER])
        ps = s.ps("ps", [P, 8, BANK])
        landed, zeroed, g_full, raw, vs, act_s, rows_set, t_full, done, out = (
            s.sem(n) for n in ("landed", "zeroed", "g_full", "raw", "vs", "act_s", "rows_set", "t_full", "done", "out"))
        pre_done = s.sem("pre_done")
        block = ctx.enter_context(nc.Block())

        @block.gpsimd
        def _(pool):
            pool.memset(wg[:, :, :], 0.0).then_inc(zeroed, 1)

        @block.sync
        def _(sp):
            w = d["w_in_c"].rearrange("l (k p) c -> p (l k) c", p=P)
            with nc.allow_non_contiguous_dma(reason="gate weights, biases and states are a few words per row"):
                sp.wait_ge(zeroed, 1)
                for g in range(2):
                    c0 = 2 * INNER + HC * g
                    sp.dma_start(wg[:, :, S0 * g:S0 * g + HC], w[:, :, c0:c0 + HC]).then_inc(landed, 16)
                    sp.dma_start(gb[:, g:g + 1], d["b_gate_c"][:, HC * g:HC * (g + 1)].rearrange("l h -> h l")).then_inc(landed, 16)
                sp.dma_start(m0[:, :], d["state_m"].rearrange("l b h -> h (l b)")).then_inc(landed, 16)
                sp.dma_start(carry[:, :], d["carry"]).then_inc(landed, 16)
                sp.dma_start(crow[:, :], d["state_conv"].rearrange("l b r c -> (l b r) c")).then_inc(landed, 16)
                sp.wait_ge(rows_set, 3)
                sp.dma_start(gate_dram[:, 0:T], u[:, :]).then_inc(out, 16)
                sp.dma_start(gate_dram[:, T:T + NT + 1 + B], dec[:, :]).then_inc(out, 16)
                sp.dma_start(d["out_m_p"].rearrange("l b h -> h (l b)"), m[:, PROMPT - 1:PROMPT]).then_inc(out, 16)
                sp.dma_start(d["out_m_s"].rearrange("l b h -> h (l b)"), m[:, SC + TS - 1:T:TS]).then_inc(out, 16)
                sp.wait_ge(out, 64)

        @block.tensor
        def _(pe):
            pe.wait_ge(landed, 16 * 7)
            for c, (c0, c1) in enumerate(CHUNKS):
                for k in range(KD):
                    last = pe.matmul(ps[0:S0 + HC, c, 0:c1 - c0], wg[:, k, :], xnT[:, k, c0:c1], start=(k == 0), stop=(k == KD - 1))
            last.then_inc(g_full, 1)
            for j in range(16):
                last = pe.transpose(ps[:, 4, 24 * j:24 * (j + 1)], crow[:, P * j:P * (j + 1)], const[0:24, C_ID:C_ID + 24])
            last.then_inc(t_full, 1)
            pe.wait_ge(rows_set, 3)
            for i in range(NT + 1):
                rows = P if i < NT else R8
                for n in range(4):
                    pe.transpose(ps[0:rows, 5, 16 * i + HC * n:16 * i + HC * (n + 1)], tok(q[:, n, :], i), const[0:HC, C_ID:C_ID + HC])
            pe.transpose(ps[0:B, 6, 0:HC], dec[:, NT + 1:NT + 1 + B], const[0:HC, C_ID:C_ID + HC]).then_inc(t_full, 1)

        @block.scalar
        def _(act):
            act.wait_ge(landed, 16 * 7)
            act.wait_ge(g_full, 1)
            flat = ps[:, 0:3, :].rearrange("p a n -> p (a n)")
            act.activation(li[:, :], flat[0:HC, 0:T], ACT.Identity, bias=gb[:, 0:1]).then_inc(raw, 1)
            act.activation(f[:, :], flat[S0:S0 + HC, 0:T], ACT.Identity, bias=gb[:, 1:2]).then_inc(raw, 1)
            act.wait_ge(vs, 1)
            act.activation(e[:, :], e[:, :], ACT.Exp, scale=-1.0).then_inc(act_s, 1)
            act.wait_ge(act_s, 1)
            act.activation(e[:, :], e[:, :], ACT.Ln, bias=const[0:HC, C_ONE:C_ONE + 1]).then_inc(act_s, 1)
            act.wait_ge(rows_set, 2)
            act.activation(q[:, Q_FLOOR, :], m[:, :], ACT.Exp, scale=-1.0).then_inc(act_s, 1)
            act.activation(q[:, Q_INTER, :], q[:, Q_INTER, :], ACT.Exp).then_inc(act_s, 1)
            act.activation(q[:, Q_STATE, :], q[:, Q_STATE, :], ACT.Exp).then_inc(act_s, 1)
            act.activation(dec[:, :], dec[:, :], ACT.Exp).then_inc(act_s, 1)
            act.wait_ge(act_s, 6)
            act.sem_inc(rows_set, 0 + 1)

        @block.vector
        def _(dve):
            link = chain(dve, vs)
            dve.wait_ge(raw, 2)
            link(dve.scalar_tensor_tensor(e[:, :], f[:, :], -1.0, f[:, :], ALU.mult, ALU.max))
            dve.wait_ge(act_s, 2)
            link(dve.scalar_tensor_tensor(lf[:, :], f[:, :], 0.0, e[:, :], ALU.min, ALU.subtract))
            link(dve.tensor_tensor_scan(b[:, :], carry[:, :], lf[:, :], 0.0, ALU.mult, ALU.add))
            dve.tensor_tensor_scan(m[:, 0:PROMPT], lf[:, 0:PROMPT], li[:, 0:PROMPT], 0.0, ALU.add, ALU.max)
            dve.tensor_tensor_scan(m[:, PROMPT:SC], lf[:, PROMPT:SC], li[:, PROMPT:SC], 0.0, ALU.add, ALU.max)
            for j in range(B):
                c = slice(SC + TS * j, SC + TS * (j + 1))
                last = dve.tensor_tensor_scan(m[:, c], lf[:, c], li[:, c], m0[:, j:j + 1], ALU.add, ALU.max)
            link(last)
            link(dve.tensor_tensor(u[:, :], b[:, :], m[:, :], ALU.subtract))
            link(dve.tensor_tensor(q[:, Q_G, :], li[:, :], b[:, :], ALU.subtract))

            def spread(dst, src, c0, step, n, width, first):
                a, z = dst[:, c0:c0 + 1], src[:, first:first + 1]
                link(dve.tensor_copy(bass.AP(a.tensor, a.offset, [a.ap[0], [step, n], [1, width]]),
                                     bass.AP(z.tensor, z.offset, [z.ap[0], [step, n], [0, width]])))

            link(dve.memset(mp[:, :], 0.0))
            spread(mp, m, META, P, NT, P, META - 1)
            a = mp[:, SC:SC + 1]
            z = m0[:, 0:1]
            link(dve.tensor_copy(bass.AP(a.tensor, a.offset, [a.ap[0], [TS, B], [1, TS]]), bass.AP(z.tensor, z.offset, [z.ap[0], [1, B], [0, TS]])))
            link(dve.tensor_tensor(q[:, Q_INTER, :], u[:, :], mp[:, :], ALU.add))
            spread(mp, u, 0, P, 1, META, META - 1)
            spread(mp, u, META, P, NT, P, META + P - 1)
            spread(mp, u, PROMPT, P, 1, S0, PROMPT + META - 1)
            spread(mp, u, SC, TS, B, TS, SC + TS - 1)
            link(dve.tensor_tensor(q[:, Q_STATE, :], q[:, Q_G, :], mp[:, :], ALU.add))
            link(dve.tensor_scalar(q[:, Q_STATE, :], q[:, Q_STATE, :], 0.0, None, ALU.min))
            link(dve.tensor_copy(dec[:, 0:NT + 1], q[:, Q_INTER, META - 1:PROMPT:P]))
            link(dve.tensor_copy(dec[:, NT + 1:NT + 1 + B], q[:, Q_INTER, SC + TS - 1:T:TS]))
            dve.sem_inc(rows_set, 2)
            dve.wait_ge(t_full, 1)
            dve.tensor_copy(preC[:, :, :], ps[:, 4, 0:384].rearrange("p (k r) -> p k r", r=24)).then_inc(pre_done, 1)
            dve.wait_ge(t_full, 2)
            n = 16 * NT
            dve.tensor_copy(cols[:, 0:NT], ps[:, 5, 0:n].rearrange("p (i n h) -> p i n h", i=NT, n=4))
            dve.tensor_copy(cols[0:R8, NT], ps[0:R8, 5, n:n + 16].rearrange("p (n h) -> p n h", n=4))
            dve.tensor_copy(decay8[:, :], ps[0:B, 6, 0:HC]).then_inc(done, 1)


def head_loop(nc, d, const, wcol, cols, decay8, preC, gate_dram, h_dram, xnT):
    NP = 16
    NV = NT + 1 + 2
    NCH = NT + 1
    assert B <= NT
    NKV = KH * (1 + B + NT)
    NY = 2 * (NT + 1)
    YB = 3
    GW = T + NT + 1 + B
    with ExitStack() as ctx:
        s = Space(nc, ctx, "head")
        w = s.sb("w", [P, 3, KH, DH])
        xq = s.sb("xq", [P, KH, T])
        ca = s.sb("ca", [P, KH, T])
        kz = s.sb("kz", [P, KH, T])
        hT = s.sb("hT", [P, KH, T])
        v = s.sb("v", [P, NT + 1, DH])
        C = s.sb("C", [P, KH, DH])
        Cs = s.sb("Cs", [P, 2, KH, DH])
        x8 = s.sb("x8", [P, KH, R8])
        xc = s.sb("xc", [P, KH, B * CP])
        qm = s.sb("qm", [P, KH, B, NS])
        kw = hT[:, 3, 0:2 * DH].rearrange("p (j c) -> p j c", j=2)
        ks, vs = s.sb("ks", [P, DH], F32R), s.sb("vs", [P, DH], F32R)
        kb = s.sb("kb", [P, 2, DH], F32R)
        t1 = hT[:, 2, 0:DH]
        arg, ex, sT = s.sb("arg", [P, P]), s.sb("ex", [P, P]), s.sb("sT", [P, 2, P])
        ub = s.sb("ub", [P, GW])
        ys = s.sb("ys", [P, YB, DH])
        crow = s.sb("crow", [R8, DH])
        nrow = s.sb("nrow", [B, DH])
        n0 = s.sb("n0", [P, KH, B])
        n = s.sb("n", [P, KH])
        hv = s.sb("hv", [P, W_KINDS, KH])
        hc = s.sb("hc", [P, NT + 1, 4])
        d8 = s.sb("d8", [B, 1])
        bn = s.sb("bn", [P, NT + 1, 6])
        mv = s.sb("mv", [P, NT + 1, 2])
        den, r1, r2 = s.sb("den", [P, NT + 1]), s.sb("r1", [P, NT + 1]), s.sb("r2", [P, NT + 1])
        ps = s.ps("ps", [P, 8, BANK])
        w_in = [s.sem(f"w_in{j}") for j in range(3)]
        ub_in, n_in, n_out = s.sem("ub_in"), s.sem("n_in"), s.sem("n_out")
        cs_in, cs_out = [s.sem("cs_in0"), s.sem("cs_in1")], [s.sem("cs_out0"), s.sem("cs_out1")]
        y_in, y_out = [s.sem(f"y_in{j}") for j in range(YB)], [s.sem(f"y_out{j}") for j in range(YB)]
        rows_out, cp_out = s.sem("rows_out"), s.sem("cp_out")
        proj_full, proj_done, pads, conv0, conv, ca_done, v_full, v_done, skipped = (
            s.sem(x) for x in ("proj_full", "proj_done", "pads", "conv0", "conv", "ca_done", "v_full", "v_done", "skipped"))
        s_full, s_done, arg_done, ex_done, kt_full, kt_done, i_full, i_done, h_full, h_done = (
            s.sem(x) for x in ("s_full", "s_done", "arg_done", "ex_done", "kt_full", "kt_done", "i_full", "i_done", "h_full", "h_done"))
        kv_full, kv_done, n_done, kb_done, n0_full, n0_done, ns_full, ns_done, qm_done = (
            s.sem(x) for x in ("kv_full", "kv_done", "n_done", "kb_done", "n0_full", "n0_done", "ns_full", "ns_done", "qm_done"))
        var_done, root_done, scale_done, hn_done, ht_full, ht_done, out_done, y_full, y_done = (
            s.sem(x) for x in ("var_done", "root_done", "scale_done", "hn_done", "ht_full", "ht_done", "out_done", "y_full", "y_done"))
        all_stored = s.sem("all_stored")
        vs_done, kh_done, ks_done, e_done = (s.sem(x) for x in ("vs_done", "kh_done", "ks_done", "e_done"))
        vec, head_set, zero_set, passed = s.sem("vec"), s.sem("head_set"), s.sem("zero_set"), s.sem("passed")
        block = ctx.enter_context(nc.Block())
        X_, K_, Q_, Z_ = 0, 4, 8, 12

        def flat(b0, b1, c0, c1, rows=P):
            return ps[0:rows, b0:b1, :].rearrange("p a n -> p (a n)")[:, c0:c1]

        def kv_unit(c, m):
            if c == -1:
                return m
            return KH * (2 + 2 * c[1]) + m if isinstance(c, tuple) else KH * (1 + 2 * c) + m

        def met(eng, sem, value):
            eng.wait_ge(sem, value)
            eng.sem_inc(passed, 1)

        @block.sync
        def _(sp):
            win = d["w_in_c"].rearrange("l (k p) c -> p (l k) c", p=P)
            wo = d["w_out_c"].rearrange("l (k p) c -> p (l k) c", p=P)

            def unit(slot, src):
                sp.dma_start(w[:, slot], src).then_inc(w_in[slot], 16)

            def first(e):
                later = not isinstance(e, int)
                if later:
                    met(sp, proj_full, NP * e)
                unit(0, win[:, 0:KH, bass.ds(DH * e, DH)])
                if later:
                    met(sp, y_full, NY * e - NT - 1)
                unit(1, win[:, KH:KD, bass.ds(DH * e, DH)])
                if later:
                    met(sp, h_done, NCH * e)
                sp.dma_start(ub[:, :], gate_dram[bass.ds(e, 1)].to_broadcast([P, GW])).then_inc(ub_in, 16)
                if later:
                    met(sp, n_out, 16 * e)
                sp.dma_start(nrow[:, :], d["state_n"].rearrange("l b h c -> (l b) (h c)")[:, bass.ds(DH * e, DH)]).then_inc(n_in, 16)
                if later:
                    met(sp, y_full, NY * e)
                unit(2, d["w_v"].rearrange("l h (k p) c -> (l h) p k c", p=P)[bass.ds(e, 1)].rearrange("o p k c -> (o p) k c"))

            def rest(e):
                def square(name):
                    return d[name].rearrange("l h (k p) c -> (l h) p k c", p=P)[bass.ds(e, 1)].rearrange("o p k c -> (o p) k c")
                met(sp, proj_full, NP * e + K_)
                unit(0, square("w_k"))
                unit(1, square("w_q"))
                met(sp, v_full, NV * e + NT + 1)
                unit(2, win[:, 0:KH, bass.ds(INNER + DH * e, DH)])
                met(sp, proj_full, NP * e + Q_)
                unit(0, win[:, KH:KD, bass.ds(INNER + DH * e, DH)])
                met(sp, ns_done, e + 1)
                sp.dma_start(d["out_n_s"].rearrange("l b h c -> (l b) (h c)")[:, bass.ds(DH * e, DH)], nrow[:, :]).then_inc(n_out, 16)
                met(sp, proj_full, NP * e + Z_)
                unit(1, wo[:, bass.ds(KH * e, KH), 0:DH])
                met(sp, proj_full, NP * e + NP)
                unit(2, wo[:, bass.ds(KH * e, KH), DH:D])

            first(0)
            with sp.Fori(0, HC - 1) as e:
                rest(e)
                first(e + 1)
            rest(HC - 1)
            met(sp, n_out, 16 * HC)

        @block.gpsimd
        def _(pool):
            with pool.Fori(0, HC) as e:
                old = d["state_C"].rearrange("l b h (k p) c -> (l b) h p k c", p=P)
                new = d["out_C_s"].rearrange("l b h (k p) c -> (l b) h p k c", p=P)

                def state(t, b):
                    return t[b][bass.ds(e, 1)].rearrange("o p k c -> (o p) k c")

                def load(b):
                    pool.dma_start(Cs[:, b % 2], state(old, b)).then_inc(cs_in[b % 2], 16)

                for b in range(2):
                    load(b)
                met(pool, v_done, NV * e + NV)
                cc = bass.ds(DH * e, DH)
                pool.dma_start(d["out_conv_s"].rearrange("l b r c -> (l b r) c")[:, cc], crow[0:B * CP, :]).then_inc(rows_out, 16)
                pool.dma_start(d["out_conv_p"].rearrange("l b r c -> (l b r) c")[:, cc], crow[S0:S0 + CP, :]).then_inc(rows_out, 16)
                for b in range(B):
                    met(pool, kv_done, NKV * e + kv_unit(("s", b), KH - 1) + 1)
                    pool.dma_start(state(new, b), Cs[:, b % 2]).then_inc(cs_out[b % 2], 16)
                    if b + 2 < B:
                        met(pool, cs_out[b % 2], 64 * e + 16 * (b // 2) + 16)
                        load(b + 2)
                met(pool, h_done, NCH * e + NCH)
                pool.dma_start(d["out_C_p"].rearrange("l b h (k p) c -> (l b h) p k c", p=P)[bass.ds(e, 1)].rearrange("o p k c -> (o p) k c"),
                               C[:, :, :]).then_inc(cp_out, 16)
                with nc.allow_non_contiguous_dma(reason="512 words"):
                    for m in range(KH):
                        pool.dma_start(d["out_n_p"].rearrange("l b h (k p o) -> (l b h) p k o", p=P, o=1)[bass.ds(e, 1), :, m]
                                       .rearrange("a p o -> (a p) o"), n[:, m:m + 1]).then_inc(cp_out, 16)

                def tile(u):
                    half, i = divmod(u, NT + 1)
                    rows = P if i < NT else R8
                    return h_dram[i, 0:rows, DH * half:DH * (half + 1)], ys[0:rows, u % YB, :]

                for u in range(NY + 1):
                    if u < NY:
                        src, dst = tile(u)
                        per = NY // YB
                        if u >= YB:
                            met(pool, y_out[u % YB], 16 * per * e + 16 * (u // YB))
                        pool.dma_start(dst, src).then_inc(y_in[u % YB], 16)
                    if u >= 1:
                        dst, src = tile(u - 1)
                        met(pool, y_done, NY * e + u + 1)
                        pool.dma_start(dst, src).then_inc(y_out[(u - 1) % YB], 16)
                for j in range(2):
                    met(pool, cs_out[j], 64 * e + 64)
                for j in range(YB):
                    met(pool, y_out[j], 16 * (NY // YB) * (e + 1))
                met(pool, rows_out, 32 * e + 32)
                met(pool, cp_out, 80 * e + 80)
                pool.sem_inc(all_stored, 1)

        @block.tensor
        def _(pe):
            def landed(slot, k):
                pe.wait_ge(w_in[slot], 16 * 3 * e + 16 * (k + 1))

            def project(j, lhs, rhs, kk):
                if j % 4 >= 2 or j >= 4:
                    pe.wait_ge(proj_done, NP * e + j - 1)
                for c, (c0, c1) in enumerate(CHUNKS):
                    for k in range(kk):
                        last = pe.matmul(ps[:, 3 * (j % 2) + c, 0:c1 - c0], lhs(k, j % 4), rhs[:, k, c0:c1], start=(k == 0), stop=(k == kk - 1))
                last.then_inc(proj_full, 1)

            def scores(i):
                x = 0 if i == NT else i + 1
                rows = P if i < NT else R8
                if x >= 1:
                    pe.wait_ge(s_done, NCH * e + x)
                if x == 1:
                    pe.wait_ge(ns_done, e + 1)
                for k in range(KH):
                    last = pe.matmul(ps[0:rows, 4, 0:rows], tok(kz[:, k, :], i), tok(xq[:, k, :], i), start=(k == 0), stop=(k == KH - 1))
                last.then_inc(s_full, 1)
                if x >= 1:
                    pe.wait_ge(kt_done, NCH * e + x)
                for k in range(KH):
                    last = pe.transpose(ps[0:rows, 5, P * k:P * (k + 1)], tok(kz[:, k, :], i), const[:, C_ID:C_ID + P])
                last.then_inc(kt_full, 1)

            def state_products(c, lhs, rhs):
                for m in range(KH):
                    u = kv_unit(c, m)
                    if u >= 2:
                        pe.wait_ge(kv_done, NKV * e + u - 1)
                    pe.matmul(ps[:, 2 + u % 2, :], lhs[:, P * m:P * (m + 1)], rhs, start=True, stop=True).then_inc(kv_full, 1)

            def one(r0, r1):
                return const[r0:r1, C_ONE:C_ONE + 1]

            with pe.Fori(0, HC) as e:
                pe.wait_ge(y_done, NY * e + 1)
                landed(0, 0)
                landed(1, 0)
                for m in range(4):
                    project(X_ + m, lambda k, t: w[:, k // KH, k % KH, P * t:P * (t + 1)], xnT, KD)
                pe.wait_ge(proj_done, NP * e + K_)
                landed(2, 0)
                for i in range(NT + 1):
                    if i >= 2:
                        pe.wait_ge(v_done, NV * e + i - 1)
                    rows = P if i < NT else R8
                    for k in range(KH):
                        x = xq[:, k, CP + META + P * i:CP + META + P * (i + 1)] if i < NT else x8[:, k, :]
                        last = pe.matmul(ps[0:rows, 6 + i % 2, :], x, w[:, 2, k, :], start=(k == 0), stop=(k == KH - 1))
                    last.then_inc(v_full, 1)
                for j, (rows, src) in enumerate(((CP, lambda k: xq[:, k, XS - CP:XS]), (B * CP, lambda k: xc[:, k, :]))):
                    pe.wait_ge(v_done, NV * e + NT + j)
                    pe.sem_inc(passed, 1)
                    for k in range(KH):
                        last = pe.transpose(ps[0:rows, 7 - j, P * k:P * (k + 1)], src(k), const[:, C_ID:C_ID + P])
                    last.then_inc(v_full, 1)
                pe.wait_ge(ca_done, KH * e + KH)
                landed(0, 1)
                for m in range(4):
                    project(K_ + m, lambda k, t: w[:, 0, k, P * t:P * (t + 1)], ca, KH)
                landed(1, 1)
                for m in range(4):
                    project(Q_ + m, lambda k, t: w[:, 1, k, P * t:P * (t + 1)], ca, KH)
                pe.wait_ge(proj_done, NP * e + Z_)
                pe.wait_ge(v_done, NV * e + NV)

                scores(NT)
                pe.wait_ge(n_in, 16 * e + 16)
                pe.sem_inc(passed, 1)
                for k in range(KH):
                    last = pe.transpose(ps[:, 7, B * k:B * (k + 1)], nrow[:, P * k:P * (k + 1)], const[0:B, C_ID:C_ID + B])
                last.then_inc(n0_full, 1)
                pe.wait_ge(kt_done, NCH * e + 1)
                pe.wait_ge(s_done, NCH * e + 1)
                pe.sem_inc(passed, 1)
                pe.matmul(ps[0:R8, 1, :], sT[0:R8, 0, 0:R8], v[0:R8, NT, :], start=True, stop=True)
                pe.matmul(ps[0:R8, 6, 1:2], sT[0:R8, 0, 0:R8], one(0, R8), start=True, stop=True)
                pe.wait_ge(n0_done, e + 1)
                pe.wait_ge(qm_done, e + 1)
                pe.sem_inc(passed, 1)
                for b in range(B):
                    for k in range(KH):
                        pe.matmul(ps[S0:R8, 6, 0:1], qm[:, k, b, :], n0[:, k, b:b + 1], start=(b == 0 and k == 0), stop=(b == B - 1 and k == KH - 1))
                for m in range(KH):
                    last = pe.matmul(ps[:, 6, 2 + m:3 + m], kw[0:META, 0, P * m:P * (m + 1)], one(0, META), start=True, stop=True)
                last.then_inc(h_full, 1)
                pe.matmul(ps[0:B, 4, :], const[S0:R8, C_OWN:C_OWN + B], kw[S0:R8, 0, :], start=True, stop=True).then_inc(ns_full, 1)
                state_products(-1, kw[0:META, 0, :], v[0:META, NT, :])

                def sample(b):
                    pe.wait_ge(cs_in[b % 2], 64 * e + 16 * (b // 2) + 16)
                    pe.sem_inc(passed, 1)
                    for k in range(KH):
                        last = pe.matmul(ps[S0:R8, 7, :], qm[:, k, b, :], Cs[:, b % 2, k, :], start=(b == 0 and k == 0), stop=(b == B - 1 and k == KH - 1))
                    if b == B - 1:
                        last.then_inc(i_full, 1)
                    if b == 0:
                        pe.wait_ge(vs_done, e + 1)
                    pe.wait_ge(kb_done, B * e + b + 1)
                    state_products(("s", b), kb[:, b % 2, :], vs[:, :])

                for c in range(NT):
                    x = c + 1
                    scores(c)
                    if c >= 1:
                        pe.wait_ge(i_done, NCH * e + c)
                    for k in range(KH):
                        pe.wait_ge(kv_done, NKV * e + (kv_unit(c - 1, k)) + 1)
                        last = pe.matmul(ps[:, 0, :], tok(xq[:, k, :], c), C[:, k, :], start=(k == 0), stop=(k == KH - 1))
                    last.then_inc(i_full, 1)
                    if c == 0:
                        pe.wait_ge(e_done, e + 1)
                    else:
                        pe.wait_ge(h_done, NCH * e + c)
                    for k in range(KH):
                        pe.matmul(ps[:, 6, 0:1], tok(xq[:, k, :], c), n[:, k:k + 1], start=(k == 0), stop=(k == KH - 1))
                    pe.wait_ge(s_done, NCH * e + x + 1)
                    pe.matmul(ps[:, 1, :], sT[:, x % 2, :], v[:, c, :], start=True, stop=True)
                    pe.matmul(ps[:, 6, 1:2], sT[:, x % 2, :], one(0, P), start=True, stop=True)
                    pe.wait_ge(kt_done, NCH * e + x + 1)
                    for m in range(KH):
                        last = pe.matmul(ps[:, 6, 2 + m:3 + m], kw[:, x % 2, P * m:P * (m + 1)], one(0, P), start=True, stop=True)
                    last.then_inc(h_full, 1)
                    state_products(c, kw[:, x % 2, :], v[:, c, :])
                    if c < B:
                        sample(c)

                pe.wait_ge(h_done, NCH * e + NT)
                pe.wait_ge(kv_done, NKV * (e + 1))
                landed(2, 1)
                landed(0, 2)
                zw = (lambda k, t: w[:, 2 if k < KH else 0, k % KH, P * t:P * (t + 1)])
                project(Z_, zw, xnT, KD)
                for i in range(NT + 1):
                    rows = P if i < NT else R8
                    pe.wait_ge(hn_done, NCH * e + i + 1)
                    if i >= 2:
                        pe.wait_ge(ht_done, NCH * e + i - 1)
                    if i == NT:
                        pe.sem_inc(passed, 1)
                    for k in range(KH):
                        last = pe.transpose(ps[:, 6 + i % 2, P * k:P * k + rows], v[0:rows, i, P * k:P * (k + 1)], const[0:rows, C_ID:C_ID + rows])
                    last.then_inc(ht_full, 1)
                for m in range(1, 4):
                    project(Z_ + m, zw, xnT, KD)

                pe.wait_ge(proj_done, NP * e + NP)
                pe.wait_ge(out_done, e + 1)
                for u in range(NY):
                    half, i = divmod(u, NT + 1)
                    rows = P if i < NT else R8
                    if i == 0:
                        landed(1 + half, 2)
                    if u >= 4:
                        pe.wait_ge(y_done, NY * e + u - 2)
                    for k in range(KH):
                        last = pe.matmul(ps[0:rows, u % 4, :], tok(hT[:, k, :], i), w[:, 1 + half, k, :], start=(k == 0), stop=(k == KH - 1))
                    last.then_inc(y_full, 1)

        @block.scalar
        def _(act):
            act.wait_ge(zero_set, 1)
            with act.Fori(0, HC) as e:
                for m in range(4):
                    act.wait_ge(proj_full, NP * e + X_ + m + 1)
                    if m == 0:
                        act.wait_ge(pads, e + 1)
                    b0 = 3 * (m % 2)
                    act.activation(xq[:, m, CP:CP + PROMPT], flat(b0, b0 + 3, 0, PROMPT), ACT.Copy)
                    new = flat(b0, b0 + 3, SC, T).rearrange("p (b t) -> p b t", t=TS)
                    a = xq[:, m, XS + CP:XS + CP + 1]
                    act.activation(bass.AP(a.tensor, a.offset, [a.ap[0], [CP + TS, B], [1, TS]]), new, ACT.Copy)
                    act.activation(xc[:, m, :].rearrange("p (b t) -> p b t", t=CP), new[:, :, TS - CP:TS], ACT.Copy)
                    act.activation(x8[:, m, :], flat(b0, b0 + 3, PROMPT, T), ACT.Copy).then_inc(proj_done, 1)
                    act.wait_ge(proj_done, NP * e + m + 1)
                    if m >= 2:
                        act.wait_ge(ca_done, KH * e + m - 1)
                    act.activation(hT[:, m % 2, 0:XW - CP], xq[:, m, 0:XW - CP], ACT.Identity,
                                   bias=hv[:, W_BIAS, m:m + 1], scale=hv[:, W_TAP, m:m + 1]).then_inc(conv0, 1)

                    def silu(m):
                        act.wait_ge(conv, 3 * KH * e + 3 * m + 3)
                        c = hT[:, m % 2, :]
                        act.activation(ca[:, m, 0:PROMPT], c[:, 0:PROMPT], ACT.Silu)
                        act.activation(ca[:, m, PROMPT:PROMPT + META], c[:, 0:META], ACT.Silu)
                        a = c[:, XS:XS + 1]
                        act.activation(ca[:, m, SC:T].rearrange("p (b t) -> p b t", t=TS),
                                       bass.AP(a.tensor, a.offset, [a.ap[0], [CP + TS, B], [1, TS]]), ACT.Silu).then_inc(ca_done, 1)
                    if m >= 1:
                        silu(m - 1)
                silu(3)
                for j in range(K_, Z_):
                    act.wait_ge(proj_full, NP * e + j + 1)
                    b0 = 3 * (j % 2)
                    dst, scale = (kz, DH ** -0.5) if j < Q_ else (xq, 1.0)
                    act.activation(dst[:, j % 4, :], flat(b0, b0 + 3, 0, T), ACT.Copy, scale=scale).then_inc(proj_done, 1)
                for k in range(KH):
                    last = act.activation(ca[:, k, :], ca[:, k, :], ACT.Copy, scale=hv[:, W_SKIP, k:k + 1])
                last.then_inc(skipped, 1)

                def exponent(x, rows):
                    act.wait_ge(arg_done, NCH * e + x + 1)
                    act.activation(ex[0:rows, 0:rows], arg[0:rows, 0:rows], ACT.Exp).then_inc(ex_done, 1)

                exponent(0, R8)
                act.wait_ge(kt_full, NCH * e + 1)
                act.activation(kw[S0:R8, 0, :], ps[S0:R8, 5, :], ACT.Copy, scale=hc[S0:R8, NT, Q_STATE:Q_STATE + 1])
                act.activation(kw[0:META, 0, :], ps[0:META, 5, :], ACT.Copy, scale=hc[0:META, NT, Q_STATE:Q_STATE + 1]).then_inc(kt_done, 1)
                act.wait_ge(kt_done, NCH * e + 1)
                for q in range(2):
                    last = act.activation(ks[NS * q:NS * (q + 1), :], kw[S0:R8, 0, :], ACT.Copy)
                last.then_inc(kh_done, 1)
                for c in range(NT):
                    x = c + 1
                    exponent(x, P)
                    act.wait_ge(kt_full, NCH * e + x + 1)
                    if c >= 1:
                        act.wait_ge(kv_full, NKV * e + kv_unit(c - 2, KH - 1) + 1)
                    act.activation(kw[:, x % 2, :], ps[:, 5, :], ACT.Copy, scale=hc[:, c, Q_STATE:Q_STATE + 1]).then_inc(kt_done, 1)
                    if c < B:
                        if c == 0:
                            act.wait_ge(ks_done, e + 1)
                        if c >= 2:
                            act.wait_ge(kv_full, NKV * e + kv_unit(("s", c - 2), KH - 1) + 1)
                        act.activation(kb[:, c % 2, :], ks[:, :], ACT.Copy, scale=const[:, C_OWN + c:C_OWN + c + 1]).then_inc(kb_done, 1)
                    act.wait_ge(i_full, NCH * e + x)
                    if c >= 1:
                        act.wait_ge(h_done, NCH * e + c)
                    act.activation(t1, ps[:, 0, :], ACT.Copy, scale=hc[:, c, Q_INTER:Q_INTER + 1]).then_inc(i_done, 1)
                act.wait_ge(i_full, NCH * e + NCH)
                act.wait_ge(h_done, NCH * e + NT)
                act.activation(t1[S0:R8, :], ps[S0:R8, 7, :], ACT.Copy, scale=hc[S0:R8, NT, Q_INTER:Q_INTER + 1]).then_inc(i_done, 1)
                act.wait_ge(var_done, e + 1)
                act.activation(r2[:, :], r2[:, :], ACT.Sqrt).then_inc(root_done, 1)
                act.wait_ge(scale_done, e + 1)
                for i in range(NT + 1):
                    rows = P if i < NT else R8
                    act.activation(v[0:rows, i, :], v[0:rows, i, :], ACT.Identity, scale=r1[0:rows, i:i + 1], bias=r2[0:rows, i:i + 1]).then_inc(hn_done, 1)
                for m in range(4):
                    act.wait_ge(proj_full, NP * e + Z_ + m + 1)
                    b0 = 3 * (m % 2)
                    act.activation(kz[:, m, :], flat(b0, b0 + 3, 0, T), ACT.Silu).then_inc(proj_done, 1)

        @block.vector
        def _(dve):
            V = 22
            dve.memset(ca[:, :, PROMPT + META:SC], 0.0)
            dve.memset(den[:, :], 1.0)
            dve.memset(hc[:, :, :], 1.0)
            dve.memset(mv[:, :, :], 0.0)
            dve.memset(qm[:, :, :, :], 0.0).then_inc(zero_set, 1)
            for sem, k in ((y_done, 1), (all_stored, 1)):
                dve.sem_inc(sem, k)
            dve.wait_ge(zero_set, 1)
            with dve.Fori(0, HC) as e:
                count = [0]

                def link(ins):
                    count[0] += 1
                    ins.then_inc(vec, 1)
                    dve.wait_ge(vec, V * e + count[0])

                dve.wait_ge(y_done, NY * e + 1)
                dve.tensor_scalar(hv[:, :, :], wcol[:, :, bass.ds(KH * e, KH)], 1.0, None, ALU.mult)
                dve.tensor_scalar(hc[:, 0:NT, :], cols[:, 0:NT, :, bass.ds(e, 1)].rearrange("p i n o -> p i (n o)"), 1.0, None, ALU.mult)
                dve.tensor_scalar(hc[0:R8, NT, :], cols[0:R8, NT, :, bass.ds(e, 1)].rearrange("p n o -> p (n o)"), 1.0, None, ALU.mult)
                dve.tensor_scalar(d8[:, :], decay8[:, bass.ds(e, 1)], 1.0, None, ALU.mult).then_inc(head_set, 1)
                dve.wait_ge(head_set, e + 1)
                dve.memset(xq[:, :, 0:CP], 0.0)
                for k in range(KH):
                    a = xq[:, k, XS:XS + 1]
                    last = dve.tensor_scalar(bass.AP(a.tensor, a.offset, [a.ap[0], [CP + TS, B], [1, CP]]),
                                             preC[:, bass.ds(KH * e + k, 1), :].rearrange("p o (b r) -> p (o b) r", r=CP), 1.0, None, ALU.mult)
                last.then_inc(pads, 1)
                for m in range(KH):
                    dve.wait_ge(conv0, KH * e + m + 1)
                    c = hT[:, m % 2, 0:XW - CP]
                    for j in range(1, CW):
                        dve.scalar_tensor_tensor(c, xq[:, m, j:j + XW - CP], hv[:, W_TAP + j, m:m + 1], c, ALU.mult, ALU.add).then_inc(conv, 1)
                        if j < CW - 1:
                            dve.wait_ge(conv, 3 * KH * e + 3 * m + j)
                for i in range(NT + 1):
                    rows = P if i < NT else R8
                    dve.wait_ge(v_full, NV * e + i + 1)
                    dve.tensor_copy(v[0:rows, i, :], ps[0:rows, 6 + i % 2, :]).then_inc(v_done, 1)
                dve.wait_ge(all_stored, e + 1)
                dve.wait_ge(v_full, NV * e + NT + 2)
                dve.tensor_copy(crow[S0:S0 + CP, :], ps[0:CP, 7, :]).then_inc(v_done, 1)
                dve.wait_ge(v_full, NV * e + NT + 3)
                dve.tensor_copy(crow[0:B * CP, :], ps[0:B * CP, 6, :]).then_inc(v_done, 1)

                dve.wait_ge(ub_in, 16 * e + 16)

                def log_weights(x, rows, c0, g, mask):
                    if x >= 1:
                        dve.wait_ge(ex_done, NCH * e + x)
                    dve.scalar_tensor_tensor(arg[0:rows, 0:rows], ub[0:rows, c0:c0 + rows], g, const[0:rows, mask:mask + rows],
                                             ALU.add, ALU.min).then_inc(arg_done, 1)

                def weigh(x, rows):
                    dve.wait_ge(ex_done, NCH * e + x + 1)
                    dve.wait_ge(s_full, NCH * e + x + 1)
                    dve.tensor_tensor(sT[0:rows, x % 2, 0:rows], ps[0:rows, 4, 0:rows], ex[0:rows, 0:rows], ALU.mult).then_inc(s_done, 1)

                def chunk_weights(c):
                    log_weights(c + 1, P, META + P * c, hc[:, c, Q_G:Q_G + 1], C_CAUSAL)

                log_weights(0, R8, PROMPT, hc[0:R8, NT, Q_G:Q_G + 1], C_BLOCK8)
                dve.wait_ge(proj_done, NP * e + Z_)
                for k in range(KH):
                    a = qm[:, k, 0, 0:1]
                    last = dve.tensor_copy(bass.AP(a.tensor, a.offset, [a.ap[0], [NS + TS, B], [1, TS]]), xq[:, k, SC:T].rearrange("p (b t) -> p b t", t=TS))
                last.then_inc(qm_done, 1)
                weigh(0, R8)
                chunk_weights(0)
                dve.wait_ge(v_done, NV * e + NT + 1)
                for q in (2, 0, 1):
                    last = dve.tensor_copy(vs[NS * q:NS * (q + 1), :], v[S0:R8, NT, :])
                link(last)
                link(dve.tensor_tensor(vs[S0:R8, :], v[S0:R8, NT, :], vs[S0:R8, :].bitcast(F32), ALU.subtract))
                dve.tensor_copy(vs[96:P, :], vs[S0:R8, :]).then_inc(vs_done, 1)
                dve.wait_ge(kh_done, e + 1)
                link(dve.tensor_tensor(ks[R8:96, :], kw[S0:R8, 0, :], ks[S0:R8, :].bitcast(F32), ALU.subtract))
                dve.tensor_copy(ks[96:P, :], ks[R8:96, :]).then_inc(ks_done, 1)
                dve.wait_ge(n0_full, e + 1)
                dve.tensor_copy(n0[:, :, :], ps[:, 7, 0:KH * B].rearrange("p (k b) -> p k b", b=B)).then_inc(n0_done, 1)
                dve.wait_ge(h_full, NCH * e + 1)
                dve.tensor_copy(n[:, :], ps[:, 6, 2:2 + KH]).then_inc(n_done, 1)
                dve.wait_ge(ns_full, e + 1)
                dve.scalar_tensor_tensor(nrow[:, :], nrow[:, :], d8[:, 0:1], ps[0:B, 4, :], ALU.mult, ALU.add).then_inc(ns_done, 1)
                for m in range(KH):
                    dve.wait_ge(kv_full, NKV * e + m + 1)
                    dve.tensor_copy(C[:, m, :], ps[:, 2 + m % 2, :]).then_inc(kv_done, 1)
                dve.tensor_copy(v[0:R8, NT, :], ps[0:R8, 1, :])
                dve.tensor_copy(den[0:S0, NT:NT + 1], ps[0:S0, 6, 1:2])
                dve.tensor_copy(r1[S0:R8, NT:NT + 1], ps[S0:R8, 6, 1:2])
                link(dve.tensor_scalar(r2[S0:R8, NT:NT + 1], ps[S0:R8, 6, 0:1], hc[S0:R8, NT, Q_INTER:Q_INTER + 1], None, ALU.mult))
                dve.tensor_tensor(den[S0:R8, NT:NT + 1], r2[S0:R8, NT:NT + 1], r1[S0:R8, NT:NT + 1], ALU.add).then_inc(e_done, 1)
                for c in range(NT):
                    x = c + 1
                    weigh(x, P)
                    if c + 1 < NT:
                        chunk_weights(c + 1)
                    for m in range(KH):
                        u = kv_unit(c, m)
                        dve.wait_ge(kv_full, NKV * e + u + 1)
                        dve.scalar_tensor_tensor(C[:, m, :], C[:, m, :], ub[:, T + 1 + c:T + 2 + c], ps[:, 2 + u % 2, :], ALU.mult, ALU.add).then_inc(kv_done, 1)
                    for m in range(KH if c < B else 0):
                        u = kv_unit(("s", c), m)
                        dve.wait_ge(kv_full, NKV * e + u + 1)
                        dve.scalar_tensor_tensor(Cs[:, c % 2, m, :], Cs[:, c % 2, m, :], ub[:, T + NT + 1 + c:T + NT + 2 + c],
                                                 ps[:, 2 + u % 2, :], ALU.mult, ALU.add).then_inc(kv_done, 1)
                    dve.wait_ge(i_done, NCH * e + x)
                    dve.scalar_tensor_tensor(n[:, :], n[:, :], ub[:, T + 1 + c:T + 2 + c], ps[:, 6, 2:2 + KH], ALU.mult, ALU.add)
                    dve.tensor_tensor(v[:, c, :], t1, ps[:, 1, :], ALU.add)
                    dve.tensor_copy(r1[:, c:c + 1], ps[:, 6, 1:2])
                    link(dve.tensor_scalar(r2[:, c:c + 1], ps[:, 6, 0:1], hc[:, c, Q_INTER:Q_INTER + 1], None, ALU.mult))
                    dve.tensor_tensor(den[:, c:c + 1], r2[:, c:c + 1], r1[:, c:c + 1], ALU.add).then_inc(h_done, 1)
                    dve.wait_ge(h_done, NCH * e + x)
                    dve.bn_stats(bn[:, c, :], v[:, c, :])
                dve.wait_ge(i_done, NCH * e + NCH)
                dve.tensor_tensor(v[S0:R8, NT, :], v[S0:R8, NT, :], t1[S0:R8, :], ALU.add).then_inc(h_done, 1)
                dve.wait_ge(h_done, NCH * e + NCH)
                last = dve.bn_stats(bn[0:R8, NT, :], v[0:R8, NT, :])
                link(last)
                dve.sem_inc(passed, 1)
                for i in range(NT + 1):
                    rows = P if i < NT else R8
                    last = dve.bn_aggr(mv[0:rows, i, :], bn[0:rows, i, :])
                link(last)
                link(dve.scalar_tensor_tensor(den[:, :], den[:, :], -1.0, den[:, :], ALU.mult, ALU.max))
                link(dve.tensor_tensor(den[:, :], den[:, :], hc[:, :, Q_FLOOR:Q_FLOOR + 1].rearrange("p i o -> p (i o)"), ALU.max))
                link(dve.reciprocal(r1[:, :], den[:, :]))
                link(dve.tensor_tensor(r2[:, :], r1[:, :], r1[:, :], ALU.mult))
                link(dve.tensor_tensor(r2[:, :], r2[:, :], mv[:, :, 1], ALU.mult))
                dve.tensor_scalar(r2[:, :], r2[:, :], EPS, None, ALU.add).then_inc(var_done, 1)
                dve.wait_ge(root_done, e + 1)
                link(dve.reciprocal(den[:, :], r2[:, :]))
                link(dve.tensor_tensor(r1[:, :], r1[:, :], den[:, :], ALU.mult))
                dve.scalar_tensor_tensor(r2[:, :], mv[:, :, 0], -1.0, r1[:, :], ALU.mult, ALU.mult).then_inc(scale_done, 1)
                for i in range(NT + 1):
                    rows = P if i < NT else R8
                    dve.wait_ge(ht_full, NCH * e + i + 1)
                    src = ps[:, 6 + i % 2, :].rearrange("p (k r) -> p k r", r=P)[:, :, 0:rows]
                    c0 = META + P * i if i < NT else PROMPT
                    dve.tensor_copy(hT[:, :, c0:c0 + rows], src).then_inc(ht_done, 1)
                dve.wait_ge(skipped, e + 1)
                dve.wait_ge(ht_done, NCH * e + NCH)
                H = slice(META, T)
                for k in range(KH):
                    last = dve.scalar_tensor_tensor(hT[:, k, H], hT[:, k, H], hv[:, W_GAMMA, k:k + 1], ca[:, k, H], ALU.mult, ALU.add)
                link(last)
                for k in range(KH):
                    dve.wait_ge(proj_done, NP * e + Z_ + k + 1)
                    last = dve.tensor_tensor(hT[:, k, H], hT[:, k, H], kz[:, k, H], ALU.mult)
                last.then_inc(out_done, 1)
                for u in range(NY):
                    rows = P if u % (NT + 1) < NT else R8
                    dve.wait_ge(y_full, NY * e + u + 1)
                    dve.wait_ge(y_in[u % YB], 16 * (NY // YB) * e + 16 * (u // YB) + 16)
                    dve.tensor_tensor(ys[0:rows, u % YB, :], ys[0:rows, u % YB, :], ps[0:rows, u % 4, :], ALU.add).then_inc(y_done, 1)
                assert count[0] == V, count[0]


def final_stage(nc, d, h_dram):
    with ExitStack() as ctx:
        s = Space(nc, ctx, "fin")
        h, sq, xn, y = s.sb("h", [P, 2, D]), s.sb("sq", [P, D]), s.sb("xn", [P, 2, D]), s.sb("y", [P, 2, D])
        g = s.sb("g", [P, D])
        stat = s.sb("stat", [P, 2, 2])
        h_in, y_out = [s.sem("h_in0"), s.sem("h_in1")], [s.sem("y_out0"), s.sem("y_out1")]
        g_in, ss_ready, msq_ready, rms_ready, rstd_ready, xn_ready, y_ready = (
            s.sem(n) for n in ("g_in", "ss_ready", "msq_ready", "rms_ready", "rstd_ready", "xn_ready", "y_ready"))
        block = ctx.enter_context(nc.Block())
        rows_of = [P] * NT + [R8]

        @block.sync
        def _(sp):
            sp.dma_start(g[:, :], d["final_norm_g"].rearrange("(o c) -> o c", o=1).to_broadcast([P, D])).then_inc(g_in, 16)
            for i in range(NT + 1):
                if i >= 2:
                    sp.wait_ge(xn_ready, i - 1)
                sp.dma_start(h[0:rows_of[i], i % 2, :], h_dram[i, 0:rows_of[i]]).then_inc(h_in[i % 2], 16)

        @block.gpsimd
        def _(pool):
            yp = d["out_yp"].rearrange("b (i p) c -> (b i) p c", p=P)
            for i in range(NT + 1):
                pool.wait_ge(y_ready, i + 1)
                if i < NT:
                    pool.dma_start(yp[i], y[:, i % 2, :]).then_inc(y_out[i % 2], 16)
                else:
                    pool.dma_start(d["out_ys"].rearrange("b t c -> (b t) c"), y[S0:R8, i % 2, :]).then_inc(y_out[i % 2], 16)
            pool.wait_ge(y_out[0], 16 * (NT // 2 + 1))
            pool.wait_ge(y_out[1], 16 * (NT // 2))

        @block.scalar
        def _(act):
            for i in range(NT + 1):
                q, rows = i % 2, rows_of[i]
                act.wait_ge(h_in[q], 16 * (i // 2 + 1))
                act.activation(sq[0:rows, :], h[0:rows, q, :], ACT.Square, accum_out=stat[0:rows, q, 0:1]).then_inc(ss_ready, 1)
                act.wait_ge(msq_ready, i + 1)
                act.activation(stat[0:rows, q, 0:1], stat[0:rows, q, 1:2], ACT.Sqrt).then_inc(rms_ready, 1)
                act.wait_ge(rstd_ready, i + 1)
                if i >= 2:
                    act.wait_ge(y_ready, i - 1)
                act.activation(xn[0:rows, q, :], h[0:rows, q, :], ACT.Copy, scale=stat[0:rows, q, 1:2]).then_inc(xn_ready, 1)

        @block.vector
        def _(dve):
            dve.wait_ge(g_in, 16)
            for i in range(NT + 1):
                q, rows = i % 2, rows_of[i]
                dve.wait_ge(ss_ready, i + 1)
                dve.tensor_scalar(stat[0:rows, q, 1:2], stat[0:rows, q, 0:1], 1.0 / D, EPS, ALU.mult, ALU.add).then_inc(msq_ready, 1)
                dve.wait_ge(rms_ready, i + 1)
                dve.reciprocal(stat[0:rows, q, 1:2], stat[0:rows, q, 0:1]).then_inc(rstd_ready, 1)
                dve.wait_ge(xn_ready, i + 1)
                if i >= 2:
                    dve.wait_ge(y_out[q], 16 * (i // 2))
                dve.tensor_tensor(y[0:rows, q, :], xn[0:rows, q, :], g[0:rows, :], ALU.mult).then_inc(y_ready, 1)


def program(nc, d, h_dram, gate_dram):
    with ExitStack() as ctx:
        s = Space(nc, ctx, "all")
        const = s.sb("const", [P, C_W])
        vcol, wcol, biasB = s.sb("vcol", [P, V_ROWS]), s.sb("wcol", [P, W_KINDS, 16]), s.sb("biasB", [P, HA])
        xnT = s.sb("xnT", [P, KD, T])
        with ExitStack() as ctx0:
            s0 = Space(nc, ctx0, "even")
            mixT = s0.sb("mixT", [P, KD, T])
            prefT = s0.sb("prefT", [P, 4, B * PRE])
            qS, kS, gS = (s0.sb(n, [P, PAIRS, NS]) for n in ("qS", "kS", "gS"))
            vS = s0.sb("vS", [R8, WA])
            load_constants(nc, d, const, vcol, wcol, biasB, prefT)
            norm_stage(nc, d, "norm0", const, vcol, V_NORM, xnT, None, None)
            attention_pairs(nc, d, const, biasB, xnT, mixT, qS, kS, gS, vS)
            with ExitStack() as ctx2:
                s2 = Space(nc, ctx2, "paged")
                table = s2.sb("table", [1, B * PAGES], I32)
                vp = s2.sb("vp", [P, B // 2, PAGES, WA])
                v_in = [s2.sem(f"v_in{j}") for j in range(B // 2)]
                pool_groups(nc, d, const, vcol, prefT, xnT, mixT, table, vp, v_in)
                decode_attention(nc, d, const, xnT, mixT, qS, kS, gS, vS, table, vp, v_in)
            norm_stage(nc, d, "norm1", const, vcol, V_NORM + KD, xnT, mixT, h_dram)
        with ExitStack() as ctx1:
            s1 = Space(nc, ctx1, "odd")
            cols = s1.sb("cols", [P, NT + 1, 4, HC])
            decay8 = s1.sb("decay8", [B, HC])
            preC = s1.sb("preC", [P, INNER // P, B * CP])
            gate_stage(nc, d, const, xnT, cols, decay8, preC, gate_dram)
            head_loop(nc, d, const, wcol, cols, decay8, preC, gate_dram, h_dram, xnT)
        final_stage(nc, d, h_dram)


def kernel(**inputs):
    import concourse.bacc as _bacc
    from concourse.bass_utils import run_bass_kernel_spmd as _run

    nc = _bacc.Bacc("TRN2", target_bir_lowering=False, num_devices=1)
    arrays = {n: np.ascontiguousarray(a) for n, a in inputs.items()}
    arrays["consts"], arrays["carry"] = constant_table(), carry_table()
    d = {n: nc.dram_tensor(f"in_{n}", a.shape, mybir.dt.from_np(a.dtype), kind="ExternalInput").ap() for n, a in arrays.items()}
    d.update({n: nc.dram_tensor(n, shape, F32, kind="ExternalOutput").ap() for n, shape in _OUTS.items()})
    h_dram = nc.dram_tensor("h_dram", (NT + 1, P, D), F32, kind="Internal").ap()
    gate_dram = nc.dram_tensor("gate_dram", (HC, T + NT + 1 + B), F32, kind="Internal").ap()
    program(nc, d, h_dram, gate_dram)
    r = _run(nc, [{f"in_{n}": a for n, a in arrays.items()}], core_ids=[0]).results[0]
    return tuple(r[n] for n in _RETURNS)
```

```python
from contextlib import ExitStack

import concourse.bass as bass
import numpy as np
from concourse import mybir

F32 = mybir.dt.float32
F32R = mybir.dt.float32r
I32 = mybir.dt.int32
ALU = mybir.AluOpType
ACT = mybir.ActivationFunctionType

P = 128
D = 1024
KD = D // P
META = 16
SEQ = 1024
B = 8
TS = 4
NS = B * TS
PROMPT = META + SEQ
R8 = 64
S0 = 32
T = PROMPT + R8
SC = PROMPT + S0
NT = SEQ // P
EPS = 1e-6

WA = 512
HA = 8
DA = 64
PAIRS = HA // 2
PAST = 1024
PAGES = PAST // P
PW = (2, 4, 8, 16)
PRE = 15
UW = PRE + PROMPT + B * (PRE + TS)

HC = 4
DH = 512
KH = DH // P
INNER = HC * DH
CW = 4
CP = CW - 1
XW = CP + PROMPT + B * (CP + TS)
XS = CP + PROMPT
NEG = -1e30
BANK = 512
CHUNKS = ((0, 512), (512, 1024), (1024, T))

C_ID, C_STRICT, C_CAUSAL, C_BLOCK8, C_DEC, C_OWN, C_RCNT, C_ONE = 0, 128, 256, 384, 448, 512, 520, 584
C_W = 585
V_NORM, V_PSCALE, V_ROWS = 0, 16, 20
W_TAP, W_BIAS, W_SKIP, W_GAMMA, W_KINDS = 0, 4, 5, 6, 7


def constant_table():
    c = np.zeros((P, C_W), np.float32)
    r = np.arange(P)
    c[:, C_ID:C_ID + P] = np.eye(P)
    c[:, C_STRICT:C_STRICT + P] = np.where(r[None, :] < r[:, None], 0, NEG)
    c[:, C_CAUSAL:C_CAUSAL + P] = np.where(r[:, None] <= r[None, :], 0, NEG)
    s, t = np.meshgrid(np.arange(R8), np.arange(R8), indexing="ij")
    meta = (s < META) & (t < META) & (s <= t)
    own = (s >= S0) & (t >= S0) & (s // TS == t // TS) & (s <= t)
    c[:R8, C_BLOCK8:C_BLOCK8 + R8] = np.where(meta | own, 0, NEG)
    for g in range(2):
        b, q = r // 32 + 4 * g, r % TS
        k = np.arange(NS)
        ok = (k[None, :] // TS == b[:, None]) & (k[None, :] % TS < q[:, None])
        c[:, C_DEC + NS * g:C_DEC + NS * (g + 1)] = np.where(ok, 0, NEG)
    c[r, C_OWN + r % NS // TS] = 1
    for g, w in enumerate(PW):
        c[:, C_RCNT + 16 * g:C_RCNT + 16 * (g + 1)] = 1 / np.minimum(w, np.arange(16) + 1)
    c[:, C_ONE] = 1
    return c


def carry_table():
    c = np.ones((HC, T), np.float32)
    c[:, 0] = 0
    c[:, META:PROMPT:P] = 0
    c[:, PROMPT] = 0
    c[:, SC::TS] = 0
    return c


def tok(ap, i):
    return ap[:, META + P * i:META + P * (i + 1)] if i < NT else ap[:, PROMPT:T]


def pieces(a, b):
    while a < b:
        e = min(b, (a // BANK + 1) * BANK)
        yield a, e
        a = e


def chain(eng, sem):
    n = [0]

    def link(ins):
        n[0] += 1
        ins.then_inc(sem, 1)
        eng.wait_ge(sem, n[0])
    return link


class Space:

    def __init__(self, nc, ctx, stage):
        self.nc, self.ctx, self.stage, self.sems, self.place = nc, ctx, stage, [], {}
        ctx.callback(self.clear)

    def clear(self):
        if self.sems:
            self.nc.clear_and_free_semaphores(self.sems)
            self.nc.all_engine_barrier()

    def sb(self, name, shape, dt=F32):
        self.place[name] = -(-self.nc.sbuf_base // 32) * 32
        return self.ctx.enter_context(self.nc.sbuf_tensor(f"{self.stage}_{name}", shape, dt))

    def over(self, old, name, shape, dt):
        return self.nc.alloc_sbuf_tensor_at(f"{self.stage}_{name}", shape, dt, offset=self.place[old])

    def ps(self, name, shape):
        return self.ctx.enter_context(self.nc.psum_tensor(f"{self.stage}_{name}", shape, F32))

    def sem(self, name):
        self.sems.append(self.nc.alloc_semaphore(name=f"{self.stage}_{name}"))
        return self.sems[-1]


def load_constants(nc, d, const, vcol, wcol, bias, prefT):
    with ExitStack() as ctx:
        s = Space(nc, ctx, "const")
        vrow = s.sb("vrow", [V_ROWS, P])
        wrow = s.sb("wrow", [W_KINDS * 16, P])
        prow = s.sb("prow", [B * PRE, WA])
        ps = s.ps("ps", [P, 3, BANK])
        landed, turned, done = s.sem("landed"), s.sem("turned"), s.sem("done")
        block = ctx.enter_context(nc.Block())
        n_loads = 9

        @block.sync
        def _(sp):
            sp.dma_start(const[:, :], d["consts"]).then_inc(landed, 16)
            sp.dma_start(vrow[V_NORM:V_NORM + 16, :], d["norm_g"].rearrange("l (k p) -> (l k) p", p=P)).then_inc(landed, 16)
            sp.dma_start(vrow[V_PSCALE:V_PSCALE + 4, :], d["pool_scale"].rearrange("l (k p) -> (l k) p", p=P)).then_inc(landed, 16)
            sp.dma_start(wrow[0:64, :], d["conv_w"].rearrange("l j (k p) -> (l j k) p", p=P)).then_inc(landed, 16)
            sp.dma_start(wrow[64:80, :], d["conv_b"].rearrange("l (k p) -> (l k) p", p=P)).then_inc(landed, 16)
            sp.dma_start(wrow[80:96, :], d["skip_c"].rearrange("l (k p) -> (l k) p", p=P)).then_inc(landed, 16)
            sp.dma_start(wrow[96:112, :], d["outnorm_g"].rearrange("l (k p) -> (l k) p", p=P)).then_inc(landed, 16)
            sp.dma_start(bias[:, :], d["sb_bias"].to_broadcast([P, HA])).then_inc(landed, 16)
            sp.dma_start(prow[:, :], d["state_pool"].rearrange("l b r c -> (l b r) c")).then_inc(landed, 16)

        @block.tensor
        def _(pe):
            pe.wait_ge(landed, 16 * n_loads)
            pe.transpose(ps[:, 0, 0:V_ROWS], vrow[:, :], const[0:V_ROWS, C_ID:C_ID + V_ROWS])
            pe.transpose(ps[:, 1, 0:112], wrow[:, :], const[0:112, C_ID:C_ID + 112])
            for g in range(4):
                last = pe.transpose(ps[:, 2, 120 * g:120 * (g + 1)], prow[:, P * g:P * (g + 1)], const[0:120, C_ID:C_ID + 120])
            last.then_inc(turned, 1)

        @block.vector
        def _(dve):
            dve.wait_ge(turned, 1)
            dve.tensor_copy(vcol[:, :], ps[:, 0, 0:V_ROWS])
            dve.tensor_copy(wcol[:, :, :], ps[:, 1, 0:112].rearrange("p (a k) -> p a k", a=W_KINDS))
            dve.tensor_copy(prefT[:, :, :], ps[:, 2, 0:480].rearrange("p (g r) -> p g r", g=4)).then_inc(done, 1)


def norm_stage(nc, d, stage, const, vcol, gcol, xnT, mixT, h_dram):
    with ExitStack() as ctx:
        s = Space(nc, ctx, stage)
        XS = 4
        x = s.sb("x", [P, XS, D])
        h = s.sb("h", [P, 2, D]) if mixT is not None else x
        sq = s.sb("sq", [P, D])
        xn = s.sb("xn", [P, 2, D])
        stat = s.sb("stat", [P, 2, 2])
        wo = s.sb("wo", [P, KD, D]) if mixT is not None else None
        yp = s.ps("yp", [P, 2, 2, BANK])
        tp = s.ps("tp", [P, 2, 2, BANK])
        x_in = [s.sem(f"x_in{j}") for j in range(XS)]
        assert NT % XS == 0
        hs = 2 if mixT is not None else XS
        wo_in, y_full, h_ready = s.sem("wo_in"), s.sem("y_full"), s.sem("h_ready")
        ss_ready, rstd_ready, xn_ready, xt_full, xt_done = (s.sem(n) for n in ("ss_ready", "rstd_ready", "xn_ready", "xt_full", "xt_done"))
        h_out = [s.sem("h_out0"), s.sem("h_out1")]
        msq_ready, rms_ready = s.sem("msq_ready"), s.sem("rms_ready")
        edge_zero = s.sem("edge_zero")
        block = ctx.enter_context(nc.Block())
        x_rows = d["x_prompt"].rearrange("b (i p) c -> (b i) p c", p=P)
        x_done = h_ready if mixT is not None else xn_ready

        @block.sync
        def _(sp):
            if mixT is not None:
                sp.dma_start(wo[:, :, :], d["w_out_a"].rearrange("l (k p) c -> p (l k) c", p=P)).then_inc(wo_in, 16)
            for i in range(NT):
                if i >= XS:
                    sp.wait_ge(x_done, i - XS + 1)
                sp.dma_start(x[:, i % XS, :], x_rows[i]).then_inc(x_in[i % XS], 16)
            sp.wait_ge(x_done, NT - XS + 1)
            sp.wait_ge(edge_zero, 1)
            sp.dma_start(x[0:META, 0, :], d["meta_tokens"]).then_inc(x_in[0], 16)
            sp.dma_start(x[S0:R8, 0, :], d["x_sample"].rearrange("b t c -> (b t) c")).then_inc(x_in[0], 16)
            if mixT is not None:
                sp.wait_ge(h_out[0], 16 * (NT // 2 + 1))
                sp.wait_ge(h_out[1], 16 * (NT // 2))

        @block.tensor
        def _(pe):
            def project(i, q):
                for half in range(2):
                    for k in range(KD):
                        rows = P if i < NT else R8
                        last = pe.matmul(yp[0:rows, q, half, :], tok(mixT[:, k, :], i), wo[:, k, BANK * half:BANK * (half + 1)],
                                         start=(k == 0), stop=(k == KD - 1))
                last.then_inc(y_full, 1)

            def turn(i, q):
                rows = P if i < NT else R8
                pe.wait_ge(xn_ready, i + 1)
                if i >= 2:
                    pe.wait_ge(xt_done, i - 1)
                for k in range(KD):
                    last = pe.transpose(tp[:, q, k // 4, P * (k % 4):P * (k % 4) + rows], xn[0:rows, q, P * k:P * (k + 1)],
                                        const[0:rows, C_ID:C_ID + rows])
                last.then_inc(xt_full, 1)

            if mixT is not None:
                pe.wait_ge(wo_in, 16)
                project(0, 0)
            for i in range(NT + 1):
                if mixT is not None and i < NT:
                    if i >= 1:
                        pe.wait_ge(h_ready, i)
                    project(i + 1, (i + 1) % 2)
                turn(i, i % 2)

        @block.scalar
        def _(act):
            def squares(i):
                q, rows = i % 2, P if i < NT else R8
                if mixT is None:
                    act.wait_ge(x_in[i % XS], 16 * (i // XS + 1) + 16 * (i == NT))
                else:
                    act.wait_ge(h_ready, i + 1)
                act.activation(sq[0:rows, :], h[0:rows, i % hs, :], ACT.Square, accum_out=stat[0:rows, q, 0:1]).then_inc(ss_ready, 1)

            def root(i):
                q, rows = i % 2, P if i < NT else R8
                act.wait_ge(msq_ready, i + 1)
                act.activation(stat[0:rows, q, 0:1], stat[0:rows, q, 1:2], ACT.Sqrt).then_inc(rms_ready, 1)

            def normalise(i):
                q, rows = i % 2, P if i < NT else R8
                act.wait_ge(rstd_ready, i + 1)
                if i >= 2:
                    act.wait_ge(xt_full, i - 1)
                act.activation(xn[0:rows, q, :], h[0:rows, i % hs, :], ACT.Copy, scale=stat[0:rows, q, 1:2]).then_inc(xn_ready, 1)

            squares(0)
            for i in range(NT + 1):
                root(i)
                if mixT is None and i < NT:
                    squares(i + 1)
                normalise(i)
                if mixT is not None and i < NT:
                    squares(i + 1)

        @block.vector
        def _(dve):
            def clear_edge():
                dve.wait_ge(x_done, NT - XS + 1)
                dve.memset(x[0:R8, 0, :], 0.0).then_inc(edge_zero, 1)

            def add(i):
                q, rows = i % 2, P if i < NT else R8
                if i >= 2:
                    dve.wait_ge(h_out[q], 16 * (i // 2))
                    dve.wait_ge(xn_ready, i - 1)
                dve.wait_ge(y_full, i + 1)
                dve.wait_ge(x_in[i % XS], 16 * (i // XS + 1) + 16 * (i == NT))
                dve.tensor_tensor(h[0:rows, q, :], x[0:rows, i % XS, :], yp[0:rows, q, :, :].rearrange("p a n -> p (a n)"), ALU.add).then_inc(h_ready, 1)

            def mean(i):
                q, rows = i % 2, P if i < NT else R8
                dve.wait_ge(ss_ready, i + 1)
                dve.tensor_scalar(stat[0:rows, q, 1:2], stat[0:rows, q, 0:1], 1.0 / D, EPS, ALU.mult, ALU.add).then_inc(msq_ready, 1)

            def invert(i):
                q, rows = i % 2, P if i < NT else R8
                dve.wait_ge(rms_ready, i + 1)
                dve.reciprocal(stat[0:rows, q, 1:2], stat[0:rows, q, 0:1]).then_inc(rstd_ready, 1)

            def evacuate(i):
                q = i % 2
                dve.wait_ge(xt_full, i + 1)
                for k in range(KD):
                    src, g = tp[:, q, k // 4, P * (k % 4):P * (k % 4 + 1)], vcol[:, gcol + k:gcol + k + 1]
                    if i < NT:
                        last = dve.tensor_scalar(xnT[:, k, META + P * i:META + P * (i + 1)], src, g, None, ALU.mult)
                    else:
                        dve.tensor_scalar(xnT[:, k, 0:META], src[:, 0:META], g, None, ALU.mult)
                        last = dve.tensor_scalar(xnT[:, k, PROMPT:T], src[:, 0:R8], g, None, ALU.mult)
                last.then_inc(xt_done, 1)

            if mixT is None:
                mean(0)
                for i in range(NT + 1):
                    invert(i)
                    if i == NT - XS + 1:
                        clear_edge()
                    if i < NT:
                        mean(i + 1)
                    if i >= 1:
                        evacuate(i - 1)
                evacuate(NT)
            else:
                for i in range(NT + 1):
                    if i == NT - XS + 1:
                        clear_edge()
                    add(i)
                    mean(i)
                    invert(i)
                    evacuate(i)

        if mixT is not None:
            @block.gpsimd
            def _(pool):
                for i in range(NT + 1):
                    q, rows = i % 2, P if i < NT else R8
                    pool.wait_ge(h_ready, i + 1)
                    pool.dma_start(h_dram[i, 0:rows], h[0:rows, q, :]).then_inc(h_out[q], 16)


def attention_pairs(nc, d, const, biasB, xnT, mixT, qS, kS, gS, vS):
    QT = NT + 1
    STEPS = 2 * QT
    full_blocks = [0] + [i + 1 for i in range(NT)]
    groups = [-(-(n + 1) // 4) for n in full_blocks]
    GP = 2 * sum(groups)
    order = [(n % 2, NT - n // 2 if n % 2 == 0 else n // 2) for n in range(STEPS)]
    NG = 2
    assert GP % NG == 0 and STEPS % 2 == 0
    keys = [META + P * n for n in full_blocks]

    with ExitStack() as ctx:
        s = Space(nc, ctx, "attn")
        w = s.sb("w", [P, 4, KD, P])
        qT, kT, ga = s.sb("qT", [P, T]), s.sb("kT", [P, T]), s.sb("ga", [P, T])
        v, kt = s.sb("v", [P, NT + 1, P]), s.sb("kt", [P, NT + 1, P])
        pos, neg, a = s.sb("pos", [P, 2, PROMPT]), s.sb("neg", [P, 2, PROMPT]), s.sb("a", [P, 3, PROMPT])
        rest = s.sb("rest", [P, 2, PROMPT + 1])
        aT = s.sb("aT", [P, 2, NT + 1, P])
        biasP = s.sb("biasP", [P, 2, 2])
        ps = s.ps("ps", [P, 8, BANK])
        w_in = [s.sem(f"w_in{u}") for u in range(4)]
        proj_full, proj_done, v_full, v_done, kt_full, kt_done, kv_out = (
            s.sem(n) for n in ("proj_full", "proj_done", "v_full", "v_done", "kt_full", "kt_done", "kv_out"))
        saved = s.sem("saved")
        z_full, sig_done, rest_done, a_done, t_full, t_done, o_full, o_done, b_done, b_neg = (
            s.sem(n) for n in ("z_full", "sig_done", "rest_done", "a_done", "t_full", "t_done", "o_full", "o_done", "b_done", "b_neg"))
        one_set, passed = s.sem("one_set"), s.sem("passed")
        block = ctx.enter_context(nc.Block())
        KV_DMAS = 6

        def gbase(n):
            return sum(groups[t] for _, t in order[:n])

        @block.sync
        def _(sp):
            cols = (0, WA, 3 * WA, 2 * WA)

            def load(p):
                for u in range(4):
                    if not isinstance(p, int):
                        if u < 3:
                            sp.wait_ge(proj_full, 3 * p - 2 + u)
                        else:
                            sp.wait_ge(v_full, 3 * p)
                    src = d["w_in_a"].rearrange("l (k p) c -> p (l k) c", p=P)
                    sp.dma_start(w[:, u], src[:, :, bass.ds(cols[u] + P * p, P)]).then_inc(w_in[u], 16)

            def store(p):
                sp.wait_ge(v_done, 3 * p + 3)
                sp.wait_ge(kt_done, 3 * p + 3)
                for src, pr, sa in ((kt, "out_kp", "out_ks"), (v, "out_vp", "out_vs")):
                    prompt = d[pr].rearrange("l b t h c -> (l b t) (h c)")
                    c = bass.ds(P * p, P)
                    sp.dma_start(prompt[META:PROMPT].rearrange("(i p) c -> p i c", p=P)[:, :, c], src[:, 0:NT, :]).then_inc(kv_out, 16)
                    sp.dma_start(prompt[0:META, c], src[0:META, NT, :]).then_inc(kv_out, 16)
                    sp.dma_start(d[sa].rearrange("l b t h c -> (l b t) (h c)")[:, c], src[S0:R8, NT, :]).then_inc(kv_out, 16)

            load(0)
            with sp.Fori(1, PAIRS) as p:
                store(p - 1)
                load(p)
            store(PAIRS - 1)
            sp.wait_ge(kv_out, 16 * KV_DMAS * PAIRS + 16)

        @block.tensor
        def _(pe):
            def wait_proj(u):
                pe.wait_ge(w_in[u], 16 * p + 16)

            def project(u, bank):
                wait_proj(u)
                for c, (c0, c1) in enumerate(CHUNKS):
                    for k in range(KD):
                        last = pe.matmul(ps[:, bank + c, 0:c1 - c0], w[:, u, k, :], xnT[:, k, c0:c1], start=(k == 0), stop=(k == KD - 1))
                last.then_inc(proj_full, 1)

            def scores(n):
                j, t = order[n]
                rows = R8 if t == 0 else P
                set_ = 2 * (n % 2)
                if n >= 2:
                    pe.wait_ge(sig_done, STEPS * p + n - 1)
                if t == 0:
                    pe.sem_inc(passed, 1)
                q = tok(qT, NT if t == 0 else t - 1)[DA * j:DA * (j + 1)]
                L = keys[t]
                mask = (L - P, L) if t else (0, META)
                if L > 2 * BANK and n >= 4:
                    pe.wait_ge(o_done, STEPS * p + n - 2)
                for c0, c1 in pieces(0, L):
                    out = ps[0:rows, set_ + c0 // BANK, 0:c1 - c0] if c0 < 2 * BANK else ps[0:rows, 6 + n % 2, 0:META]
                    m0, m1 = max(c0, mask[0]), min(c1, mask[1])
                    last = pe.matmul(out, q, kT[DA * j:DA * (j + 1), c0:c1], start=True, stop=(m0 >= m1))
                    if m0 < m1:
                        last = pe.matmul(out[:, m0 - c0:m1 - c0], const[:, C_ID:C_ID + rows],
                                         const[:, C_STRICT + m0 - mask[0]:C_STRICT + m1 - mask[0]], start=False, stop=True)
                last.then_inc(z_full, 1)

            def turn(n):
                j, t = order[n]
                rows = META if t == 0 else P
                pe.wait_ge(a_done, STEPS * p + n + 1)
                blocks = list(range(full_blocks[t])) + [NT]
                for g in range(groups[t]):
                    u = gbase(n) + g
                    pe.wait_ge(t_done, GP * p + u + 1)
                    if t == 0:
                        pe.sem_inc(passed, 1)
                    for m, b in enumerate(blocks[4 * g:4 * g + 4]):
                        c0, c1 = (0, META) if b == NT else (META + P * b, META + P * (b + 1))
                        last = pe.transpose(ps[0:c1 - c0, 4 + u % NG, P * m:P * m + rows], a[0:rows, n % 3, c0:c1], const[0:rows, C_ID:C_ID + rows])
                    last.then_inc(t_full, 1)

            def weigh(n):
                j, t = order[n]
                rows = META if t == 0 else P
                pe.wait_ge(t_done, GP * p + gbase(n + 1) + NG)
                if n >= 2:
                    pe.wait_ge(o_done, STEPS * p + n)
                if n + 2 < STEPS and keys[order[n + 2][1]] > 2 * BANK:
                    pe.wait_ge(sig_done, STEPS * p + n + 3)
                out = ps[DA * j:DA * (j + 1), 6 + n % 2, 0:rows]
                for b in range(full_blocks[t]):
                    pe.matmul(out, v[:, b, DA * j:DA * (j + 1)], aT[:, n % 2, b, 0:rows], start=(b == 0), stop=False)
                pe.matmul(out, v[0:META, NT, DA * j:DA * (j + 1)], aT[0:META, n % 2, NT, 0:rows],
                          start=(full_blocks[t] == 0), stop=True).then_inc(o_full, 1)

            with pe.Fori(0, PAIRS) as p:
                pe.wait_ge(o_done, STEPS * p + 1)
                project(0, 0)
                project(1, 3)
                wait_proj(3)
                for g in range(3):
                    if g == 2:
                        pe.wait_ge(v_done, 3 * p + 1)
                    ids = range(4 * g, min(4 * g + 4, NT + 1))
                    for i in ids:
                        for k in range(KD):
                            rows = P if i < NT else R8
                            last = pe.matmul(ps[0:rows, 6 + g % 2, P * (i % 4):P * (i % 4 + 1)], tok(xnT[:, k, :], i), w[:, 3, k, :],
                                             start=(k == 0), stop=(k == KD - 1))
                    last.then_inc(v_full, 1)
                pe.wait_ge(proj_done, 3 * p + 1)
                project(2, 0)
                pe.wait_ge(proj_done, 3 * p + 2)
                for g in range(3):
                    for i in range(4 * g, min(4 * g + 4, NT + 1)):
                        rows = P if i < NT else R8
                        last = pe.transpose(ps[0:rows, 3 + g, P * (i % 4):P * (i % 4 + 1)], tok(kT, i), const[:, C_ID:C_ID + P])
                    last.then_inc(kt_full, 1)
                pe.wait_ge(proj_done, 3 * p + 3)
                pe.wait_ge(kt_done, 3 * p + 3)
                for n in range(STEPS + 3):
                    if n < STEPS:
                        scores(n)
                    if 2 <= n <= STEPS + 1:
                        turn(n - 2)
                    if n >= 3:
                        weigh(n - 3)

        @block.scalar
        def _(act):
            act.sem_inc(t_done, NG)
            with act.Fori(0, PAIRS) as p:
                act.wait_ge(proj_full, 3 * p + 1)
                act.activation(qT[:, :], ps[:, 0:3, :].rearrange("p a n -> p (a n)")[:, 0:T], ACT.Copy, scale=DA ** -0.5).then_inc(proj_done, 1)
                act.wait_ge(proj_full, 3 * p + 2)
                act.activation(kT[:, :], ps[:, 3:6, :].rearrange("p a n -> p (a n)")[:, 0:T], ACT.Copy).then_inc(proj_done, 1)
                act.wait_ge(proj_full, 3 * p + 3)
                act.activation(ga[:, :], ps[:, 0:3, :].rearrange("p a n -> p (a n)")[:, 0:T], ACT.Silu).then_inc(proj_done, 1)
                act.wait_ge(b_done, 2 * p + 2)

                def sigmoids(n):
                    j, t = order[n]
                    rows, L, set_ = META if t == 0 else P, keys[t], 2 * (n % 2)
                    act.wait_ge(z_full, STEPS * p + n + 1)
                    if n >= 2:
                        act.wait_ge(a_done, STEPS * p + n - 1)
                    z = ps[0:rows, set_:set_ + 2, :].rearrange("p a n -> p (a n)")[:, 0:min(L, 2 * BANK)]
                    parts = [(z, 0, min(L, 2 * BANK))]
                    if L > 2 * BANK:
                        parts.append((ps[0:rows, 6 + n % 2, 0:META], 2 * BANK, L))
                    for zz, c0, c1 in parts:
                        act.activation(pos[0:rows, n % 2, c0:c1], zz, ACT.Sigmoid, bias=biasP[0:rows, 0, j:j + 1])
                        last = act.activation(neg[0:rows, n % 2, c0:c1], zz, ACT.Sigmoid, bias=biasP[0:rows, 1, j:j + 1], scale=-1.0)
                    last.then_inc(sig_done, 1)

                def copy_turned(n):
                    j, t = order[n]
                    rows = META if t == 0 else P
                    if n >= 2:
                        act.wait_ge(o_full, STEPS * p + n - 1)
                    for g in range(groups[t]):
                        u = gbase(n) + g
                        act.wait_ge(t_full, GP * p + u + 1)
                        m = min(4, full_blocks[t] - 4 * g)
                        bank = ps[:, 4 + u % NG, :].rearrange("p (m r) -> p m r", r=P)
                        if m > 0:
                            last = act.activation(aT[:, n % 2, 4 * g:4 * g + m, :], bank[:, 0:m, :], ACT.Copy)
                        if g == groups[t] - 1:
                            last = act.activation(aT[0:META, n % 2, NT, 0:rows], bank[0:META, m, 0:rows], ACT.Copy)
                        last.then_inc(t_done, 1)

                for n in range(STEPS + 2):
                    if n < STEPS:
                        sigmoids(n)
                    if n >= 2:
                        copy_turned(n - 2)

        @block.vector
        def _(dve):
            dve.sem_inc(o_done, 1)
            dve.sem_inc(kv_out, 16)
            dve.memset(rest[:, :, :], 1.0).then_inc(one_set, 1)
            with dve.Fori(0, PAIRS) as p:
                dve.wait_ge(o_done, STEPS * p + 1)
                dve.wait_ge(kv_out, 16 * KV_DMAS * p + 16)
                for g in range(3):
                    dve.wait_ge(v_full, 3 * p + g + 1)
                    bank = ps[:, 6 + g % 2, :].rearrange("p (m r) -> p m r", r=P)
                    if g < 2:
                        dve.tensor_copy(v[:, 4 * g:4 * g + 4, :], bank).then_inc(v_done, 1)
                    else:
                        dve.tensor_scalar(vS[S0:R8, bass.ds(P * p, P)], ps[S0:R8, 6, 0:P], 1.0, None, ALU.mult)
                        dve.tensor_copy(v[0:R8, NT, :], bank[0:R8, 0, :]).then_inc(v_done, 1)
                for g in range(3):
                    dve.wait_ge(kt_full, 3 * p + g + 1)
                    bank = ps[:, 3 + g, :].rearrange("p (m r) -> p m r", r=P)
                    if g < 2:
                        dve.tensor_copy(kt[:, 4 * g:4 * g + 4, :], bank).then_inc(kt_done, 1)
                    else:
                        dve.tensor_copy(kt[0:R8, NT, :], bank[0:R8, 0, :]).then_inc(kt_done, 1)
                dve.wait_ge(proj_done, 3 * p + 3)
                for src, dst in ((qT, qS), (kT, kS), (ga, gS)):
                    dve.tensor_scalar(dst[:, bass.ds(p, 1), :].rearrange("p o n -> p (o n)"), src[:, SC:T], 1.0, None, ALU.mult).then_inc(saved, 1)
                pair_bias = biasB[:, bass.ds(2 * p, 2)]
                dve.tensor_scalar(biasP[:, 0, :], pair_bias, 1.0, None, ALU.mult).then_inc(b_done, 1)
                dve.tensor_scalar(biasP[:, 1, :], pair_bias, -1.0, None, ALU.mult).then_inc(b_done, 1)

                def weights(n):
                    j, t = order[n]
                    rows, L = META if t == 0 else P, keys[t]
                    dve.wait_ge(sig_done, STEPS * p + n + 1)
                    if n == 0:
                        dve.wait_ge(one_set, 1)
                    if n >= 2:
                        dve.wait_ge(a_done, STEPS * p + n - 1)
                    dve.tensor_tensor_scan(rest[0:rows, n % 2, PROMPT - L:PROMPT][:, ::-1], neg[0:rows, n % 2, 0:L][:, ::-1],
                                           neg[0:rows, n % 2, 0:L][:, ::-1], 1.0, ALU.mult, ALU.bypass).then_inc(rest_done, 1)
                    dve.wait_ge(rest_done, STEPS * p + n + 1)
                    if n >= 3:
                        dve.wait_ge(t_full, GP * p + gbase(n - 2))
                    dve.tensor_tensor(a[0:rows, n % 3, 0:L], pos[0:rows, n % 2, 0:L], rest[0:rows, n % 2, PROMPT - L + 1:PROMPT + 1], ALU.mult).then_inc(a_done, 1)

                def output(n):
                    j, t = order[n]
                    rows = META if t == 0 else P
                    c0 = PROMPT if t == 0 else META + P * (t - 1)
                    dve.wait_ge(o_full, STEPS * p + n + 1)
                    dve.tensor_tensor(mixT[DA * j:DA * (j + 1), bass.ds(p, 1), c0:c0 + rows].rearrange("p o n -> p (o n)"),
                                      ps[DA * j:DA * (j + 1), 6 + n % 2, 0:rows],
                                      ga[DA * j:DA * (j + 1), c0:c0 + rows], ALU.mult).then_inc(o_done, 1)

                for n in range(STEPS + 3):
                    if n < STEPS:
                        weights(n)
                    if n >= 3:
                        output(n - 3)


def pool_groups(nc, d, const, vcol, prefT, xnT, mixT, table, vp, v_in):
    with ExitStack() as ctx:
        s = Space(nc, ctx, "pool")
        w = s.sb("w", [P, 2, 2, KD, P])
        wp = s.sb("wp", [P, 4, P])
        u = s.sb("u", [P, 2, UW])
        un = s.sb("un", [P, 2, NS])
        win = s.sb("win", [P, 2, UW])
        gb = s.sb("gb", [P, 2, T])
        edge = s.sb("edge", [P, PRE])
        last_rows = s.sb("last_rows", [PRE, WA])
        new_rows = s.sb("new_rows", [NS, WA])
        ps = s.ps("ps", [P, 8, BANK])
        w_in = [s.sem("w_in0"), s.sem("w_in1")]
        table_in, wp_in, u_full, g_full, u_done, g_done, y_full, y_done, diff_done, link_s, rows_full, rows_done, out = (
            s.sem(n) for n in ("table_in", "wp_in", "u_full", "g_full", "u_done", "g_done", "y_full", "y_done", "diff_done", "link", "rows_full", "rows_done", "out"))
        block = ctx.enter_context(nc.Block())

        def sample_u(ap):
            return bass.AP(ap.tensor, ap.offset + PRE + PROMPT + PRE, [ap.ap[0], [PRE + TS, B], [1, TS]])

        @block.sync
        def _(sp):
            src = d["w_in_a"].rearrange("l (k p) c -> p (l k) c", p=P)
            sp.dma_start(wp[:, :, :], d["w_pool"].rearrange("l g c e -> c (l g) e")).then_inc(wp_in, 16)
            sp.dma_start(table[:, :], d["page_table"].rearrange("(o b) n -> o (b n)", o=1)).then_inc(table_in, 16)
            for g in range(4):
                if g == 2:
                    sp.wait_ge(table_in, 16)
                    for b in range(B // 2):
                        load_pages(sp, table, d["cache_sb_v"].rearrange("l n p h c -> (l n) p (h c)"), b, 0, PAGES, vp[:, b], v_in[b])
                if g >= 2:
                    sp.wait_ge(g_full, g - 1)
                for a in range(2):
                    c0 = 4 * WA + a * WA + P * g
                    sp.dma_start(w[:, g % 2, a], src[:, :, c0:c0 + P]).then_inc(w_in[g % 2], 16)
            old = d["state_pool"].rearrange("l b r c -> (l b) r c")
            new = d["out_pool_s"].rearrange("l b r c -> (l b) r c")
            sp.dma_start(new[:, 0:PRE - TS, :], old[:, TS:PRE, :]).then_inc(out, 16)
            sp.wait_ge(rows_done, 2)
            sp.dma_start(d["out_pool_p"].rearrange("l b r c -> (l b r) c"), last_rows[:, :]).then_inc(out, 16)
            sp.dma_start(new[:, PRE - TS:PRE, :], new_rows[:, :]).then_inc(out, 16)
            sp.wait_ge(out, 48)

        @block.tensor
        def _(pe):
            def project(g, a, bank, full):
                for c, (c0, c1) in enumerate(CHUNKS):
                    for k in range(KD):
                        last = pe.matmul(ps[:, bank + c, 0:c1 - c0], w[:, g % 2, a, k, :], xnT[:, k, c0:c1], start=(k == 0), stop=(k == KD - 1))
                last.then_inc(full, 1)

            for g in range(4):
                pe.wait_ge(w_in[g % 2], 32 * (g // 2 + 1))
                if g >= 1:
                    pe.wait_ge(y_done, g)
                project(g, 0, 0, u_full)
                if g >= 1:
                    pe.wait_ge(g_done, g)
                project(g, 1, 3, g_full)
                pe.wait_ge(u_done, g + 1)
                if g == 0:
                    pe.wait_ge(wp_in, 16)
                uu = u[:, g % 2, :]
                pe.transpose(ps[0:PRE, 6, P * g:P * (g + 1)], uu[:, PROMPT:PROMPT + PRE], const[:, C_ID:C_ID + P])
                pe.transpose(ps[0:NS, 7, P * g:P * (g + 1)], un[:, g % 2, :], const[:, C_ID:C_ID + P]).then_inc(rows_full, 1)
                pe.wait_ge(diff_done, g + 1)
                ww = win[:, 0, :]
                for c, (c0, c1) in enumerate(((0, 512), (512, 1024), (1024, PROMPT))):
                    pe.matmul(ps[:, c, 0:c1 - c0], wp[:, g, :], ww[:, PRE + c0:PRE + c1], start=True, stop=True)
                pe.matmul(ps[:, 2, META:2 * META], wp[:, g, :], ww[:, PRE:PRE + META], start=True, stop=True)
                pe.matmul(ps[:, 2, META + S0:META + R8], wp[:, g, :], sample_u(ww), start=True, stop=True).then_inc(y_full, 1)

        @block.scalar
        def _(act):
            for g in range(4):
                act.wait_ge(u_full, g + 1)
                uu = u[:, g % 2, :]
                act.activation(uu[:, PRE:PRE + PROMPT], ps[:, 0:3, :].rearrange("p a n -> p (a n)")[:, 0:PROMPT], ACT.Copy)
                act.activation(un[:, g % 2, :], ps[:, 2, META + S0:META + R8], ACT.Copy)
                act.activation(sample_u(uu), ps[:, 2, META + S0:META + R8].rearrange("p (b t) -> p b t", t=TS), ACT.Copy).then_inc(u_done, 1)
                act.wait_ge(g_full, g + 1)
                if g >= 2:
                    act.wait_ge(y_done, g - 1)
                act.activation(gb[:, g % 2, :], ps[:, 3:6, :].rearrange("p a n -> p (a n)")[:, 0:T], ACT.Silu).then_inc(g_done, 1)

        @block.vector
        def _(dve):
            link = chain(dve, link_s)
            link(dve.memset(u[:, :, 0:PRE], 0.0))
            link(dve.memset(mixT[:, :, PROMPT + META:SC], 0.0))
            for g, wd in enumerate(PW):
                uu = u[:, g % 2, :]
                pre = bass.AP(uu.tensor, uu.offset + PRE + PROMPT, [uu.ap[0], [PRE + TS, B], [1, PRE]])
                if g >= 1:
                    dve.wait_ge(y_full, g)
                link(dve.tensor_copy(pre, prefT[:, g, :].rearrange("p (b r) -> p b r", r=PRE)))
                dve.wait_ge(u_done, g + 1)
                src, step, side = uu, 1, 0
                while step < wd:
                    dst = win[:, side, :]
                    link(dve.tensor_tensor(dst[:, 2 * step - 1:UW], src[:, 2 * step - 1:UW], src[:, step - 1:UW - step], ALU.add))
                    src, step, side = dst, 2 * step, 1 - side
                n_edge = PRE
                link(dve.tensor_tensor(edge[:, :], src[:, PRE:PRE + n_edge], const[:, C_RCNT + 16 * g:C_RCNT + 16 * g + n_edge], ALU.mult))
                link(dve.scalar_tensor_tensor(win[:, 0, PRE:UW], src[:, PRE:UW], 1.0 / wd, uu[:, PRE:UW], ALU.mult, ALU.subtract))
                dve.tensor_tensor(win[:, 0, PRE:PRE + n_edge], edge[:, :], uu[:, PRE:PRE + n_edge], ALU.subtract).then_inc(diff_done, 1)
                dve.wait_ge(y_full, g + 1)
                dve.wait_ge(g_done, g + 1)
                for c0, c1 in ((0, PROMPT + META), (SC, T)):
                    last = dve.scalar_tensor_tensor(mixT[:, PAIRS + g, c0:c1], ps[:, 0:3, :].rearrange("p a n -> p (a n)")[:, c0:c1],
                                                    vcol[:, V_PSCALE + g:V_PSCALE + g + 1], gb[:, g % 2, c0:c1], ALU.mult, ALU.mult)
                last.then_inc(y_done, 1)
            dve.wait_ge(rows_full, 4)
            dve.tensor_copy(last_rows[:, :], ps[0:PRE, 6, :]).then_inc(rows_done, 1)
            dve.tensor_copy(new_rows[:, :], ps[0:NS, 7, :]).then_inc(rows_done, 1)


def load_pages(eng, table, cache, b, j0, n, dst, sem):
    for j in range(n):
        page = eng.value_load(table[0:1, PAGES * b + j0 + j:PAGES * b + j0 + j + 1], min_val=0, max_val=cache.shape[0] - 1)
        eng.dma_start(dst[:, j, :], cache[bass.ds(page, 1)].rearrange("o p c -> (o p) c")).then_inc(sem, 16)


def decode_attention(nc, d, const, xnT, mixT, qS, kS, gS, vS, table, vp, v_in):
    G, BG = 2, B // 2
    HALF = PAGES // 2
    LK = PAST + NS
    KS = 4
    units = [(b, f) for b in range(B) for f in range(2)]
    with ExitStack() as ctx:
        s = Space(nc, ctx, "dec")
        qB = s.sb("qB", [P, PAIRS, B, HA * TS])
        kp = xnT.rearrange("p k t -> p (k t)")[:, 0:KS * HALF * WA].rearrange("p (s j c) -> p s j c", s=KS, c=WA)
        kT = s.sb("kT", [P, 2, PAIRS, HALF * P])
        biasR = s.sb("biasR", [P, 2])
        zn = s.sb("zn", [P, NS])
        pos, neg, a = s.sb("pos", [P, LK]), s.sb("neg", [P, LK]), s.sb("a", [P, LK])
        rest = s.sb("rest", [P, LK + 1])
        aT = s.sb("aT", [P, PAGES, P])
        aN = s.sb("aN", [R8, P])
        oS = s.sb("oS", [P, WA])
        ps = s.ps("ps", [P, 8, BANK])
        bias_in, q_zero, q_set, bias_set = (s.sem(n) for n in ("bias_in", "q_zero", "q_set", "bias_set"))
        k_in = [s.sem(f"k_in{j}") for j in range(KS)]
        kt_full, kt_done, z_full, zn_set, sig_done, link_s, a_done, t_full, t_done, o_full, o_saved, ot_full, o_done = (
            s.sem(n) for n in ("kt_full", "kt_done", "z_full", "zn_set", "sig_done", "link", "a_done", "t_full", "t_done", "o_full", "o_saved", "ot_full", "o_done"))
        block = ctx.enter_context(nc.Block())

        @block.sync
        def _(sp):
            cache_k = d["cache_sb_k"].rearrange("l n p h c -> (l n) p (h c)")
            for u, (b, f) in enumerate(units):
                if u >= KS:
                    sp.wait_ge(z_full, u - KS + 1)
                load_pages(sp, table, cache_k, b, HALF * f, HALF, kp[:, u % KS], k_in[u % KS])

        @block.gpsimd
        def _(pool):
            pool.memset(qB[:, :, :, :], 0.0).then_inc(q_zero, 1)

        @block.tensor
        def _(pe):
            def turn_page(u, pg):
                n = HALF * u + pg
                if pg == 0:
                    pe.wait_ge(k_in[u % KS], 16 * HALF * (u // KS + 1))
                if n >= 2:
                    pe.wait_ge(kt_done, n - 1)
                for c in range(PAIRS):
                    last = pe.transpose(ps[:, 4 + n % 2, P * c:P * (c + 1)], kp[:, u % KS, pg, P * c:P * (c + 1)], const[:, C_ID:C_ID + P])
                last.then_inc(kt_full, 1)

            def scores(u):
                b, f = units[u]
                r = 32 * (b % BG)
                pe.wait_ge(kt_done, HALF * (u + 1))
                if u == 0:
                    pe.wait_ge(q_set, 1)
                if u == BG * 2:
                    pe.wait_ge(sig_done, 1)
                for c in range(PAIRS):
                    last = pe.matmul(ps[r:r + 32, f, :], qB[:, c, b, :], kT[:, u % 2, c, :], start=(c == 0), stop=(c == PAIRS - 1))
                if f == 1:
                    for c in range(PAIRS):
                        last = pe.matmul(ps[r:r + 32, 2, 0:NS], qB[:, c, b, :], kS[:, c, :], start=(c == 0), stop=(c == PAIRS - 1))
                last.then_inc(z_full, 1)

            def turn_weights(g):
                pe.wait_ge(a_done, g + 1)
                for m in range(3):
                    n = 3 * g + m
                    if n >= 1:
                        pe.wait_ge(t_done, n)
                    if m < 2:
                        for j in range(4):
                            last = pe.transpose(ps[:, 6, P * j:P * (j + 1)], a[:, P * (4 * m + j):P * (4 * m + j + 1)], const[:, C_ID:C_ID + P])
                    else:
                        last = pe.transpose(ps[0:NS, 6, 0:P], a[:, PAST:LK], const[:, C_ID:C_ID + P])
                    last.then_inc(t_full, 1)

            def output(b):
                g, bb = divmod(b, BG)
                if bb == 0:
                    pe.wait_ge(t_done, 3 * (g + 1))
                    if g >= 1:
                        pe.wait_ge(o_saved, g)
                    pe.matmul(ps[:, 7, :], aN[S0:R8, :], vS[S0:R8, :], start=True, stop=False)
                pe.wait_ge(v_in[bb], 16 * PAGES * (g + 1))
                r = 32 * bb
                for j in range(PAGES):
                    last = pe.matmul(ps[r:r + 32, 7, :], aT[:, j, r:r + 32], vp[:, bb, j, :], start=False, stop=(j == PAGES - 1))
                last.then_inc(o_full, 1)

            def turn_output(g):
                pe.wait_ge(o_saved, g + 1)
                if g >= 1:
                    pe.wait_ge(o_done, g)
                for c in range(PAIRS):
                    last = pe.transpose(ps[:, 3, P * c:P * (c + 1)], oS[:, P * c:P * (c + 1)], const[:, C_ID:C_ID + P])
                last.then_inc(ot_full, 1)

            for u in range(2 * B):
                for pg in range(HALF):
                    turn_page(u, pg)
                scores(u)
                if u == 2 * BG:
                    turn_weights(0)
                elif 2 * BG < u <= 3 * BG:
                    output(u - 2 * BG - 1)
                elif u == 3 * BG + 1:
                    turn_output(0)
            turn_weights(1)
            for b in range(BG, B):
                output(b)
            turn_output(1)

        @block.scalar
        def _(act):
            for b in range(BG):
                for h in range(HA):
                    r = 32 * b + TS * h
                    act.dma_start(biasR[r:r + TS, 0:1], d["sb_bias"][:, h:h + 1].to_broadcast([TS, 1])).then_inc(bias_in, 16)
            cache_v = d["cache_sb_v"].rearrange("l n p h c -> (l n) p (h c)")
            act.wait_ge(bias_set, 1)
            for g in range(G):
                act.wait_ge(z_full, 2 * BG * (g + 1))
                if g >= 1:
                    act.wait_ge(a_done, g)
                z = ps[:, 0:2, :].rearrange("p a n -> p (a n)")
                act.activation(pos[:, 0:PAST], z, ACT.Sigmoid, bias=biasR[:, 0:1])
                act.activation(neg[:, 0:PAST], z, ACT.Sigmoid, bias=biasR[:, 1:2], scale=-1.0)
                act.wait_ge(zn_set, g + 1)
                act.activation(pos[:, PAST:LK], zn[:, :], ACT.Sigmoid, bias=biasR[:, 0:1])
                act.activation(neg[:, PAST:LK], zn[:, :], ACT.Sigmoid, bias=biasR[:, 1:2], scale=-1.0).then_inc(sig_done, 1)
                for m in range(3):
                    act.wait_ge(t_full, 3 * g + m + 1)
                    if g >= 1 and m == 0:
                        act.wait_ge(o_full, BG * g)
                    if m < 2:
                        act.activation(aT[:, 4 * m:4 * m + 4, :], ps[:, 6, :].rearrange("p (j r) -> p j r", r=P), ACT.Copy).then_inc(t_done, 1)
                    else:
                        act.activation(aN[S0:R8, :], ps[0:NS, 6, 0:P], ACT.Copy).then_inc(t_done, 1)
                for b in range(BG * (g + 1), B):
                    act.wait_ge(o_full, b - BG + 1)
                    load_pages(act, table, cache_v, b, 0, PAGES, vp[:, b % BG], v_in[b % BG])

        @block.vector
        def _(dve):
            link = chain(dve, link_s)
            dve.wait_ge(q_zero, 1)
            for c in range(PAIRS):
                for j in range(2):
                    dst = qB[DA * j:DA * (j + 1), c, :, 8 * c + TS * j:8 * c + TS * (j + 1)]
                    last = dve.tensor_copy(dst, qS[DA * j:DA * (j + 1), c, :].rearrange("p (b t) -> p b t", t=TS))
            last.then_inc(q_set, 1)
            dve.wait_ge(bias_in, 16 * BG * HA)
            dve.tensor_scalar(biasR[:, 1:2], biasR[:, 0:1], -1.0, None, ALU.mult).then_inc(bias_set, 1)
            def copy_keys(u):
                for pg in range(HALF):
                    n = HALF * u + pg
                    dve.wait_ge(kt_full, n + 1)
                    if u >= 2 and pg == 0:
                        dve.wait_ge(z_full, u - 1)
                    dve.tensor_copy(kT[:, u % 2, :, P * pg:P * (pg + 1)], ps[:, 4 + n % 2, :].rearrange("p (c r) -> p c r", r=P)).then_inc(kt_done, 1)

            def weights(g):
                dve.wait_ge(z_full, 2 * BG * (g + 1))
                if g >= 1:
                    dve.wait_ge(sig_done, g)
                dve.tensor_tensor(zn[:, :], ps[:, 2, 0:NS], const[:, C_DEC + NS * g:C_DEC + NS * (g + 1)], ALU.add).then_inc(zn_set, 1)
                if g == 0:
                    link(dve.memset(rest[:, LK:LK + 1], 1.0))
                dve.wait_ge(sig_done, g + 1)
                link(dve.tensor_tensor_scan(rest[:, 0:LK][:, ::-1], neg[:, ::-1], neg[:, ::-1], 1.0, ALU.mult, ALU.bypass))
                if g >= 1:
                    dve.wait_ge(t_full, 3 * g)
                dve.tensor_tensor(a[:, :], pos[:, :], rest[:, 1:LK + 1], ALU.mult).then_inc(a_done, 1)

            def save(g):
                dve.wait_ge(o_full, BG * (g + 1))
                dve.tensor_copy(oS[:, :], ps[:, 7, :]).then_inc(o_saved, 1)

            def outputs(g):
                dve.wait_ge(ot_full, g + 1)
                for c in range(PAIRS):
                    for j in range(2):
                        r = slice(DA * j, DA * (j + 1))
                        rows = ps[r, 3, P * c:P * (c + 1)].rearrange("p (b x) -> p b x", b=BG)[:, :, 8 * c + TS * j:8 * c + TS * (j + 1)]
                        c0 = TS * BG * g
                        last = dve.tensor_tensor(mixT[r, c, SC + c0:SC + c0 + TS * BG].rearrange("p (b t) -> p b t", t=TS), rows,
                                                 gS[r, c, c0:c0 + TS * BG].rearrange("p (b t) -> p b t", t=TS), ALU.mult)
                last.then_inc(o_done, 1)

            for u in range(2 * BG):
                copy_keys(u)
            weights(0)
            for u in range(2 * BG, 4 * BG):
                copy_keys(u)
                if u == 3 * BG:
                    save(0)
            outputs(0)
            weights(1)
            save(1)
            outputs(1)


_OUTS = {
    "out_yp": (1, SEQ, D), "out_ys": (B, TS, D),
    "out_kp": (1, 1, PROMPT, HA, DA), "out_vp": (1, 1, PROMPT, HA, DA),
    "out_ks": (1, B, TS, HA, DA), "out_vs": (1, B, TS, HA, DA),
    "out_pool_p": (1, 1, PRE, WA), "out_pool_s": (1, B, PRE, WA),
    "out_C_p": (1, 1, HC, DH, DH), "out_C_s": (1, B, HC, DH, DH),
    "out_n_p": (1, 1, HC, DH), "out_n_s": (1, B, HC, DH),
    "out_m_p": (1, 1, HC), "out_m_s": (1, B, HC),
    "out_conv_p": (1, 1, CP, INNER), "out_conv_s": (1, B, CP, INNER),
}
_RETURNS = ("out_yp", "out_ys", "out_kp", "out_vp", "out_ks", "out_vs", "out_pool_p", "out_pool_s", "out_C_p", "out_C_s",
            "out_n_p", "out_n_s", "out_m_p", "out_m_s", "out_conv_p", "out_conv_s")


Q_G, Q_INTER, Q_FLOOR, Q_STATE = range(4)


def load_unit(sp, w, w_in, slot, src):
    sp.dma_start(w[:, slot], src).then_inc(w_in[slot], 16)


def x_weights(d, e, half):
    return d["w_in_c"].rearrange("l (k p) c -> p (l k) c", p=P)[:, KH * half:KH * (half + 1), bass.ds(DH * e, DH)]


def square(d, name, e):
    return d[name].rearrange("l h (k p) c -> (l h) p k c", p=P)[bass.ds(e, 1)].rearrange("o p k c -> (o p) k c")


def gate_stage(nc, d, const, xnT, cols, decay8, preC, gate_dram, w, w_in):
    with ExitStack() as ctx:
        s = Space(nc, ctx, "gate")
        wg = s.sb("wg", [P, KD, S0 + HC])
        gb = s.sb("gb", [HC, 2])
        m0 = s.sb("m0", [HC, B])
        carry = s.sb("carry", [HC, T])
        li, f, e, lf, b, m, u, mp = (s.sb(n, [HC, T]) for n in ("li", "f", "e", "lf", "b", "m", "u", "mp"))
        q = s.sb("q", [HC, 4, T])
        dec = s.sb("dec", [HC, NT + 1 + B])
        crow = s.sb("crow", [B * CP, INNER])
        ps = s.ps("ps", [P, 8, BANK])
        landed, zeroed, g_full, raw, vs, act_s, rows_set, t_full, done, out = (
            s.sem(n) for n in ("landed", "zeroed", "g_full", "raw", "vs", "act_s", "rows_set", "t_full", "done", "out"))
        pre_done = s.sem("pre_done")
        block = ctx.enter_context(nc.Block())

        @block.gpsimd
        def _(pool):
            pool.memset(wg[:, :, :], 0.0).then_inc(zeroed, 1)

        @block.sync
        def _(sp):
            win = d["w_in_c"].rearrange("l (k p) c -> p (l k) c", p=P)
            with nc.allow_non_contiguous_dma(reason="gate weights, biases and states are a few words per row"):
                sp.wait_ge(zeroed, 1)
                for g in range(2):
                    c0 = 2 * INNER + HC * g
                    sp.dma_start(wg[:, :, S0 * g:S0 * g + HC], win[:, :, c0:c0 + HC]).then_inc(landed, 16)
                    sp.dma_start(gb[:, g:g + 1], d["b_gate_c"][:, HC * g:HC * (g + 1)].rearrange("l h -> h l")).then_inc(landed, 16)
                sp.dma_start(m0[:, :], d["state_m"].rearrange("l b h -> h (l b)")).then_inc(landed, 16)
                sp.dma_start(carry[:, :], d["carry"]).then_inc(landed, 16)
                sp.dma_start(crow[:, :], d["state_conv"].rearrange("l b r c -> (l b r) c")).then_inc(landed, 16)
                for half in range(2):
                    load_unit(sp, w, w_in, half, x_weights(d, 0, half))
                load_unit(sp, w, w_in, 2, square(d, "w_v", 0))
                sp.wait_ge(rows_set, 3)
                sp.dma_start(gate_dram[:, 0:T], u[:, :]).then_inc(out, 16)
                sp.dma_start(gate_dram[:, T:T + NT + 1 + B], dec[:, :]).then_inc(out, 16)
                sp.dma_start(d["out_m_p"].rearrange("l b h -> h (l b)"), m[:, PROMPT - 1:PROMPT]).then_inc(out, 16)
                sp.dma_start(d["out_m_s"].rearrange("l b h -> h (l b)"), m[:, SC + TS - 1:T:TS]).then_inc(out, 16)
                sp.wait_ge(out, 64)

        @block.tensor
        def _(pe):
            pe.wait_ge(landed, 16 * 7)
            for c, (c0, c1) in enumerate(CHUNKS):
                for k in range(KD):
                    last = pe.matmul(ps[0:S0 + HC, c, 0:c1 - c0], wg[:, k, :], xnT[:, k, c0:c1], start=(k == 0), stop=(k == KD - 1))
            last.then_inc(g_full, 1)
            for j in range(16):
                last = pe.transpose(ps[:, 4, 24 * j:24 * (j + 1)], crow[:, P * j:P * (j + 1)], const[0:24, C_ID:C_ID + 24])
            last.then_inc(t_full, 1)
            pe.wait_ge(rows_set, 3)
            for i in range(NT + 1):
                rows = P if i < NT else R8
                for n in range(4):
                    pe.transpose(ps[0:rows, 5, 16 * i + HC * n:16 * i + HC * (n + 1)], tok(q[:, n, :], i), const[0:HC, C_ID:C_ID + HC])
            pe.transpose(ps[0:B, 6, 0:HC], dec[:, NT + 1:NT + 1 + B], const[0:HC, C_ID:C_ID + HC]).then_inc(t_full, 1)

        @block.scalar
        def _(act):
            act.wait_ge(landed, 16 * 7)
            act.wait_ge(g_full, 1)
            flat = ps[:, 0:3, :].rearrange("p a n -> p (a n)")
            act.activation(li[:, :], flat[0:HC, 0:T], ACT.Identity, bias=gb[:, 0:1]).then_inc(raw, 1)
            act.activation(f[:, :], flat[S0:S0 + HC, 0:T], ACT.Identity, bias=gb[:, 1:2]).then_inc(raw, 1)
            act.wait_ge(vs, 1)
            act.activation(e[:, :], e[:, :], ACT.Exp, scale=-1.0).then_inc(act_s, 1)
            act.wait_ge(act_s, 1)
            act.activation(e[:, :], e[:, :], ACT.Ln, bias=const[0:HC, C_ONE:C_ONE + 1]).then_inc(act_s, 1)
            act.wait_ge(rows_set, 2)
            act.activation(q[:, Q_FLOOR, :], m[:, :], ACT.Exp, scale=-1.0).then_inc(act_s, 1)
            act.activation(q[:, Q_INTER, :], q[:, Q_INTER, :], ACT.Exp).then_inc(act_s, 1)
            act.activation(q[:, Q_STATE, :], q[:, Q_STATE, :], ACT.Exp).then_inc(act_s, 1)
            act.activation(dec[:, :], dec[:, :], ACT.Exp).then_inc(act_s, 1)
            act.wait_ge(act_s, 6)
            act.sem_inc(rows_set, 0 + 1)

        @block.vector
        def _(dve):
            link = chain(dve, vs)
            dve.wait_ge(raw, 2)
            link(dve.scalar_tensor_tensor(e[:, :], f[:, :], -1.0, f[:, :], ALU.mult, ALU.max))
            dve.wait_ge(act_s, 2)
            link(dve.scalar_tensor_tensor(lf[:, :], f[:, :], 0.0, e[:, :], ALU.min, ALU.subtract))
            link(dve.tensor_tensor_scan(b[:, :], carry[:, :], lf[:, :], 0.0, ALU.mult, ALU.add))
            dve.tensor_tensor_scan(m[:, 0:PROMPT], lf[:, 0:PROMPT], li[:, 0:PROMPT], 0.0, ALU.add, ALU.max)
            dve.tensor_tensor_scan(m[:, PROMPT:SC], lf[:, PROMPT:SC], li[:, PROMPT:SC], 0.0, ALU.add, ALU.max)
            for j in range(B):
                c = slice(SC + TS * j, SC + TS * (j + 1))
                last = dve.tensor_tensor_scan(m[:, c], lf[:, c], li[:, c], m0[:, j:j + 1], ALU.add, ALU.max)
            link(last)
            link(dve.tensor_tensor(u[:, :], b[:, :], m[:, :], ALU.subtract))
            link(dve.tensor_tensor(q[:, Q_G, :], li[:, :], b[:, :], ALU.subtract))

            def spread(dst, src, c0, step, n, width, first):
                a, z = dst[:, c0:c0 + 1], src[:, first:first + 1]
                link(dve.tensor_copy(bass.AP(a.tensor, a.offset, [a.ap[0], [step, n], [1, width]]),
                                     bass.AP(z.tensor, z.offset, [z.ap[0], [step, n], [0, width]])))

            link(dve.memset(mp[:, :], 0.0))
            spread(mp, m, META, P, NT, P, META - 1)
            a = mp[:, SC:SC + 1]
            z = m0[:, 0:1]
            link(dve.tensor_copy(bass.AP(a.tensor, a.offset, [a.ap[0], [TS, B], [1, TS]]), bass.AP(z.tensor, z.offset, [z.ap[0], [1, B], [0, TS]])))
            link(dve.tensor_tensor(q[:, Q_INTER, :], u[:, :], mp[:, :], ALU.add))
            spread(mp, u, 0, P, 1, META, META - 1)
            spread(mp, u, META, P, NT, P, META + P - 1)
            spread(mp, u, PROMPT, P, 1, S0, PROMPT + META - 1)
            spread(mp, u, SC, TS, B, TS, SC + TS - 1)
            link(dve.tensor_tensor(q[:, Q_STATE, :], q[:, Q_G, :], mp[:, :], ALU.add))
            link(dve.tensor_scalar(q[:, Q_STATE, :], q[:, Q_STATE, :], 0.0, None, ALU.min))
            link(dve.tensor_copy(dec[:, 0:NT + 1], q[:, Q_INTER, META - 1:PROMPT:P]))
            link(dve.tensor_copy(dec[:, NT + 1:NT + 1 + B], q[:, Q_INTER, SC + TS - 1:T:TS]))
            dve.sem_inc(rows_set, 2)
            dve.wait_ge(t_full, 1)
            dve.tensor_copy(preC[:, :, :], ps[:, 4, 0:384].rearrange("p (k r) -> p k r", r=24)).then_inc(pre_done, 1)
            dve.wait_ge(t_full, 2)
            n = 16 * NT
            dve.tensor_copy(cols[:, 0:NT], ps[:, 5, 0:n].rearrange("p (i n h) -> p i n h", i=NT, n=4))
            dve.tensor_copy(cols[0:R8, NT], ps[0:R8, 5, n:n + 16].rearrange("p (n h) -> p n h", n=4))
            dve.tensor_copy(decay8[:, :], ps[0:B, 6, 0:HC]).then_inc(done, 1)


def head_loop(nc, d, const, wcol, cols, decay8, preC, gate_dram, h_dram, xnT, w, w_in, w_place):
    NP = 16
    NV = NT + 1 + 2
    NCH = NT + 1
    assert B <= NT
    NKV = KH * (1 + B + NT)
    NY = 2 * (NT + 1)
    YB = 6
    assert NY % YB == 0
    GW = T + NT + 1 + B
    with ExitStack() as ctx:
        s = Space(nc, ctx, "head")
        s.place["w"] = w_place
        xq = s.sb("xq", [P, KH, T])
        ca = s.sb("ca", [P, KH, T])
        kz = s.sb("kz", [P, KH, T])
        hT = s.sb("hT", [P, KH, T])
        v = s.sb("v", [P, NT + 1, DH])
        C = s.sb("C", [P, KH, DH])
        Cs = s.sb("Cs", [P, 2, KH, DH])
        x8 = s.sb("x8", [P, KH, R8])
        xc = s.sb("xc", [P, KH, B * CP])
        qm = s.sb("qm", [P, KH, B, NS])
        kw = hT[:, 3, 0:2 * DH].rearrange("p (j c) -> p j c", j=2)
        ks, vs = s.sb("ks", [P, DH], F32R), s.sb("vs", [P, DH], F32R)
        kb = s.sb("kb", [P, 2, DH], F32R)
        vm = s.sb("vm", [P, DH], F32R)
        t1 = hT[:, 2, 0:DH]
        arg, ex, sT = s.sb("arg", [P, P]), s.sb("ex", [P, P]), s.sb("sT", [P, 2, P])
        ub = s.sb("ub", [P, GW])
        ys = Cs.rearrange("p j k c -> p (j k) c")[:, 0:YB]
        crow = s.sb("crow", [R8, DH])
        nrow = s.sb("nrow", [B, DH])
        n0 = s.sb("n0", [P, KH, B])
        n = s.sb("n", [P, KH])
        hv = s.sb("hv", [P, W_KINDS, KH])
        hc = s.sb("hc", [P, NT + 1, 4])
        d8 = s.sb("d8", [B, 1])
        bn = s.sb("bn", [P, NT + 1, 6])
        mv = s.sb("mv", [P, NT + 1, 2])
        den, r1, r2 = s.sb("den", [P, NT + 1]), s.sb("r1", [P, NT + 1]), s.sb("r2", [P, NT + 1])
        oh, ol = s.over("ca", "oh", [P, KH, T], F32R), s.over("xq", "ol", [P, KH, T], F32R)
        wh, wl = s.over("v", "wh", [P, 2 * KH, DH], F32R), s.over("w", "wl", [P, 3, KH, DH], F32R)
        ps = s.ps("ps", [P, 8, BANK])
        ub_in, n_in, n_out = s.sem("ub_in"), s.sem("n_in"), s.sem("n_out")
        cs_in, cs_out = [s.sem("cs_in0"), s.sem("cs_in1")], [s.sem("cs_out0"), s.sem("cs_out1")]
        y_in, y_out = [s.sem(f"y_in{j}") for j in range(YB)], [s.sem(f"y_out{j}") for j in range(YB)]
        rows_out, cp_out = s.sem("rows_out"), s.sem("cp_out")
        proj_full, proj_done, pads, conv0, conv, ca_done, v_full, v_done, skipped = (
            s.sem(x) for x in ("proj_full", "proj_done", "pads", "conv0", "conv", "ca_done", "v_full", "v_done", "skipped"))
        s_full, s_done, arg_done, ex_done, kt_full, kt_done, i_full, i_done, h_full, h_done = (
            s.sem(x) for x in ("s_full", "s_done", "arg_done", "ex_done", "kt_full", "kt_done", "i_full", "i_done", "h_full", "h_done"))
        kv_full, kv_done, n_done, kb_done, n0_full, n0_done, ns_full, ns_done, qm_done = (
            s.sem(x) for x in ("kv_full", "kv_done", "n_done", "kb_done", "n0_full", "n0_done", "ns_full", "ns_done", "qm_done"))
        var_done, root_done, scale_done, hn_done, ht_full, ht_done, out_done, y_full, y_done = (
            s.sem(x) for x in ("var_done", "root_done", "scale_done", "hn_done", "ht_full", "ht_done", "out_done", "y_full", "y_done"))
        all_stored = s.sem("all_stored")
        gated, oh_done, wh_done, wl_done = (s.sem(x) for x in ("gated", "oh_done", "wh_done", "wl_done"))
        km_high, km_done, vm_done = s.sem("km_high"), s.sem("km_done"), s.sem("vm_done")
        vs_done, kh_done, ks_done, e_done = (s.sem(x) for x in ("vs_done", "kh_done", "ks_done", "e_done"))
        vec, head_set, zero_set, passed = s.sem("vec"), s.sem("head_set"), s.sem("zero_set"), s.sem("passed")
        block = ctx.enter_context(nc.Block())
        X_, K_, Q_, Z_ = 0, 4, 8, 12

        def flat(b0, b1, c0, c1, rows=P):
            return ps[0:rows, b0:b1, :].rearrange("p a n -> p (a n)")[:, c0:c1]

        def kv_unit(c, m):
            if c == -1:
                return m
            return KH * (2 + 2 * c[1]) + m if isinstance(c, tuple) else KH * (1 + 2 * c) + m

        def met(eng, sem, value):
            eng.wait_ge(sem, value)
            eng.sem_inc(passed, 1)

        @block.sync
        def _(sp):
            win = d["w_in_c"].rearrange("l (k p) c -> p (l k) c", p=P)
            wo = d["w_out_c"].rearrange("l (k p) c -> p (l k) c", p=P)

            def unit(slot, src):
                load_unit(sp, w, w_in, slot, src)

            def first(e):
                later = not isinstance(e, int)
                if later:
                    met(sp, proj_full, NP * e)
                    unit(0, x_weights(d, e, 0))
                    met(sp, y_full, NY * e - NT - 1)
                    unit(1, x_weights(d, e, 1))
                    met(sp, h_done, NCH * e)
                sp.dma_start(ub[:, :], gate_dram[bass.ds(e, 1)].to_broadcast([P, GW])).then_inc(ub_in, 16)
                if later:
                    met(sp, n_out, 16 * e)
                sp.dma_start(nrow[:, :], d["state_n"].rearrange("l b h c -> (l b) (h c)")[:, bass.ds(DH * e, DH)]).then_inc(n_in, 16)
                if later:
                    met(sp, y_full, NY * e)
                    unit(2, square(d, "w_v", e))

            def rest(e):
                met(sp, proj_full, NP * e + K_)
                unit(0, square(d, "w_k", e))
                unit(1, square(d, "w_q", e))
                met(sp, v_full, NV * e + NT + 1)
                unit(2, win[:, 0:KH, bass.ds(INNER + DH * e, DH)])
                met(sp, proj_full, NP * e + Q_)
                unit(0, win[:, KH:KD, bass.ds(INNER + DH * e, DH)])
                met(sp, ns_done, e + 1)
                sp.dma_start(d["out_n_s"].rearrange("l b h c -> (l b) (h c)")[:, bass.ds(DH * e, DH)], nrow[:, :]).then_inc(n_out, 16)
                met(sp, proj_full, NP * e + Z_)
                unit(1, wo[:, bass.ds(KH * e, KH), 0:DH])
                met(sp, proj_full, NP * e + NP)
                unit(2, wo[:, bass.ds(KH * e, KH), DH:D])

            first(0)
            with sp.Fori(0, HC - 1) as e:
                rest(e)
                first(e + 1)
            rest(HC - 1)
            met(sp, n_out, 16 * HC)

        @block.gpsimd
        def _(pool):
            with pool.Fori(0, HC) as e:
                old = d["state_C"].rearrange("l b h (k p) c -> (l b) h p k c", p=P)
                new = d["out_C_s"].rearrange("l b h (k p) c -> (l b) h p k c", p=P)

                def state(t, b):
                    return t[b][bass.ds(e, 1)].rearrange("o p k c -> (o p) k c")

                def load(b):
                    pool.dma_start(Cs[:, b % 2], state(old, b)).then_inc(cs_in[b % 2], 16)

                for b in range(2):
                    load(b)
                met(pool, v_done, NV * e + NV)
                cc = bass.ds(DH * e, DH)
                pool.dma_start(d["out_conv_s"].rearrange("l b r c -> (l b r) c")[:, cc], crow[0:B * CP, :]).then_inc(rows_out, 16)
                pool.dma_start(d["out_conv_p"].rearrange("l b r c -> (l b r) c")[:, cc], crow[S0:S0 + CP, :]).then_inc(rows_out, 16)
                for b in range(B):
                    met(pool, kv_done, NKV * e + kv_unit(("s", b), KH - 1) + 1)
                    pool.dma_start(state(new, b), Cs[:, b % 2]).then_inc(cs_out[b % 2], 16)
                    if b + 2 < B:
                        met(pool, cs_out[b % 2], 64 * e + 16 * (b // 2) + 16)
                        load(b + 2)
                met(pool, h_done, NCH * e + NCH)
                pool.dma_start(d["out_C_p"].rearrange("l b h (k p) c -> (l b h) p k c", p=P)[bass.ds(e, 1)].rearrange("o p k c -> (o p) k c"),
                               C[:, :, :]).then_inc(cp_out, 16)
                with nc.allow_non_contiguous_dma(reason="512 words"):
                    for m in range(KH):
                        pool.dma_start(d["out_n_p"].rearrange("l b h (k p o) -> (l b h) p k o", p=P, o=1)[bass.ds(e, 1), :, m]
                                       .rearrange("a p o -> (a p) o"), n[:, m:m + 1]).then_inc(cp_out, 16)

                def tile(u):
                    half, i = divmod(u, NT + 1)
                    rows = P if i < NT else R8
                    return h_dram[i, 0:rows, DH * half:DH * (half + 1)], ys[0:rows, u % YB, :]

                def load_sum(u):
                    src, dst = tile(u)
                    pool.dma_start(dst, src).then_inc(y_in[u % YB], 16)

                for j in range(2):
                    met(pool, cs_out[j], 64 * e + 64)
                for u in range(YB - 1):
                    load_sum(u)
                for u in range(NY):
                    dst, src = tile(u)
                    met(pool, y_done, NY * e + u + 2)
                    pool.dma_start(dst, src).then_inc(y_out[u % YB], 16)
                    if u + YB - 1 < NY:
                        if u >= 1:
                            met(pool, y_out[(u - 1) % YB], 16 * (NY // YB) * e + 16 * ((u - 1) // YB + 1))
                        load_sum(u + YB - 1)
                for j in range(YB):
                    met(pool, y_out[j], 16 * (NY // YB) * (e + 1))
                met(pool, rows_out, 32 * e + 32)
                met(pool, cp_out, 80 * e + 80)
                pool.sem_inc(all_stored, 1)

        @block.tensor
        def _(pe):
            def landed(slot, k):
                pe.wait_ge(w_in[slot], 16 * 3 * e + 16 * (k + 1))

            def project(j, lhs, rhs, kk, banks_free=()):
                if j % 4 >= 2 or j >= 4:
                    pe.wait_ge(proj_done, NP * e + j - 1)
                for c, (c0, c1) in enumerate(CHUNKS):
                    for sem, value in banks_free[c:c + 1]:
                        pe.wait_ge(sem, value)
                    for k in range(kk):
                        last = pe.matmul(ps[:, 3 * (j % 2) + c, 0:c1 - c0], lhs(k, j % 4), rhs[:, k, c0:c1], start=(k == 0), stop=(k == kk - 1))
                last.then_inc(proj_full, 1)

            def scores(i):
                x = 0 if i == NT else i + 1
                rows = P if i < NT else R8
                if x >= 1:
                    pe.wait_ge(s_done, NCH * e + x)
                if x == 1:
                    pe.wait_ge(ns_done, e + 1)
                for k in range(KH):
                    last = pe.matmul(ps[0:rows, 4, 0:rows], tok(kz[:, k, :], i), tok(xq[:, k, :], i), start=(k == 0), stop=(k == KH - 1))
                last.then_inc(s_full, 1)
                if x >= 1:
                    pe.wait_ge(kt_done, NCH * e + x)
                for k in range(KH):
                    last = pe.transpose(ps[0:rows, 5, P * k:P * (k + 1)], tok(kz[:, k, :], i), const[:, C_ID:C_ID + P])
                last.then_inc(kt_full, 1)

            def state_products(c, lhs, rhs):
                for m in range(KH):
                    u = kv_unit(c, m)
                    if u >= 2:
                        pe.wait_ge(kv_done, NKV * e + u - 1)
                    pe.matmul(ps[:, 2 + u % 2, :], lhs[:, P * m:P * (m + 1)], rhs, start=True, stop=True).then_inc(kv_full, 1)

            def one(r0, r1):
                return const[r0:r1, C_ONE:C_ONE + 1]

            with pe.Fori(0, HC) as e:
                pe.wait_ge(y_done, NY * e + 1)
                landed(0, 0)
                landed(1, 0)
                for m in range(4):
                    project(X_ + m, lambda k, t: w[:, k // KH, k % KH, P * t:P * (t + 1)], xnT, KD)
                pe.wait_ge(proj_done, NP * e + K_)
                landed(2, 0)
                for i in range(NT + 1):
                    if i >= 2:
                        pe.wait_ge(v_done, NV * e + i - 1)
                    rows = P if i < NT else R8
                    for k in range(KH):
                        x = xq[:, k, CP + META + P * i:CP + META + P * (i + 1)] if i < NT else x8[:, k, :]
                        last = pe.matmul(ps[0:rows, 6 + i % 2, :], x, w[:, 2, k, :], start=(k == 0), stop=(k == KH - 1))
                    last.then_inc(v_full, 1)
                for j, (rows, src) in enumerate(((CP, lambda k: xq[:, k, XS - CP:XS]), (B * CP, lambda k: xc[:, k, :]))):
                    pe.wait_ge(v_done, NV * e + NT + j)
                    pe.sem_inc(passed, 1)
                    for k in range(KH):
                        last = pe.transpose(ps[0:rows, 7 - j, P * k:P * (k + 1)], src(k), const[:, C_ID:C_ID + P])
                    last.then_inc(v_full, 1)
                pe.wait_ge(ca_done, KH * e + KH)
                landed(0, 1)
                for m in range(4):
                    project(K_ + m, lambda k, t: w[:, 0, k, P * t:P * (t + 1)], ca, KH)
                landed(1, 1)
                for m in range(4):
                    project(Q_ + m, lambda k, t: w[:, 1, k, P * t:P * (t + 1)], ca, KH)
                pe.wait_ge(proj_done, NP * e + Z_)
                pe.wait_ge(v_done, NV * e + NV)

                scores(NT)
                pe.wait_ge(n_in, 16 * e + 16)
                pe.sem_inc(passed, 1)
                for k in range(KH):
                    last = pe.transpose(ps[:, 7, B * k:B * (k + 1)], nrow[:, P * k:P * (k + 1)], const[0:B, C_ID:C_ID + B])
                last.then_inc(n0_full, 1)
                pe.wait_ge(kt_done, NCH * e + 1)
                pe.wait_ge(s_done, NCH * e + 1)
                pe.sem_inc(passed, 1)
                pe.matmul(ps[0:R8, 1, :], sT[0:R8, 0, 0:R8], v[0:R8, NT, :], start=True, stop=True)
                pe.matmul(ps[0:R8, 6, 1:2], sT[0:R8, 0, 0:R8], one(0, R8), start=True, stop=True)
                pe.wait_ge(n0_done, e + 1)
                pe.wait_ge(qm_done, e + 1)
                pe.sem_inc(passed, 1)
                for b in range(B):
                    for k in range(KH):
                        pe.matmul(ps[S0:R8, 6, 0:1], qm[:, k, b, :], n0[:, k, b:b + 1], start=(b == 0 and k == 0), stop=(b == B - 1 and k == KH - 1))
                for m in range(KH):
                    last = pe.matmul(ps[:, 6, 2 + m:3 + m], kw[0:META, 0, P * m:P * (m + 1)], one(0, META), start=True, stop=True)
                last.then_inc(h_full, 1)
                pe.matmul(ps[0:B, 4, :], const[S0:R8, C_OWN:C_OWN + B], kw[S0:R8, 0, :], start=True, stop=True).then_inc(ns_full, 1)
                pe.wait_ge(km_done, e + 1)
                pe.wait_ge(vm_done, e + 1)
                state_products(-1, kb[:, 1, :], vm[:, :])

                def sample(b):
                    pe.wait_ge(cs_in[b % 2], 64 * e + 16 * (b // 2) + 16)
                    pe.sem_inc(passed, 1)
                    for k in range(KH):
                        last = pe.matmul(ps[S0:R8, 7, :], qm[:, k, b, :], Cs[:, b % 2, k, :], start=(b == 0 and k == 0), stop=(b == B - 1 and k == KH - 1))
                    if b == B - 1:
                        last.then_inc(i_full, 1)
                    if b == 0:
                        pe.wait_ge(vs_done, e + 1)
                    pe.wait_ge(kb_done, B * e + b + 1)
                    state_products(("s", b), kb[:, b % 2, :], vs[:, :])

                for c in range(NT):
                    x = c + 1
                    scores(c)
                    if c >= 1:
                        pe.wait_ge(i_done, NCH * e + c)
                    for k in range(KH):
                        pe.wait_ge(kv_done, NKV * e + (kv_unit(c - 1, k)) + 1)
                        last = pe.matmul(ps[:, 0, :], tok(xq[:, k, :], c), C[:, k, :], start=(k == 0), stop=(k == KH - 1))
                    last.then_inc(i_full, 1)
                    if c == 0:
                        pe.wait_ge(e_done, e + 1)
                    else:
                        pe.wait_ge(h_done, NCH * e + c)
                    for k in range(KH):
                        pe.matmul(ps[:, 6, 0:1], tok(xq[:, k, :], c), n[:, k:k + 1], start=(k == 0), stop=(k == KH - 1))
                    pe.wait_ge(s_done, NCH * e + x + 1)
                    pe.matmul(ps[:, 1, :], sT[:, x % 2, :], v[:, c, :], start=True, stop=True)
                    pe.matmul(ps[:, 6, 1:2], sT[:, x % 2, :], one(0, P), start=True, stop=True)
                    pe.wait_ge(kt_done, NCH * e + x + 1)
                    for m in range(KH):
                        last = pe.matmul(ps[:, 6, 2 + m:3 + m], kw[:, x % 2, P * m:P * (m + 1)], one(0, P), start=True, stop=True)
                    last.then_inc(h_full, 1)
                    state_products(c, kw[:, x % 2, :], v[:, c, :])
                    if c < B:
                        sample(c)

                landed(2, 1)
                landed(0, 2)
                zw = (lambda k, t: w[:, 2 if k < KH else 0, k % KH, P * t:P * (t + 1)])
                project(Z_, zw, xnT, KD, ((i_done, NCH * e + NT), (h_done, NCH * e + NT), (kv_done, NKV * (e + 1))))
                for i in range(NT + 1):
                    rows = P if i < NT else R8
                    pe.wait_ge(hn_done, NCH * e + i + 1)
                    if i >= 2:
                        pe.wait_ge(ht_done, NCH * e + i - 1)
                    if i == NT:
                        pe.sem_inc(passed, 1)
                    for k in range(KH):
                        last = pe.transpose(ps[:, 6 + i % 2, P * k:P * k + rows], v[0:rows, i, P * k:P * (k + 1)], const[0:rows, C_ID:C_ID + rows])
                    last.then_inc(ht_full, 1)
                for m in range(1, 4):
                    project(Z_ + m, zw, xnT, KD)

                def output(u, ks):
                    half, i = divmod(u, NT + 1)
                    rows = P if i < NT else R8
                    for k in ks:
                        whk, wlk = wh[:, KH * half + k, :], wl[:, 1 + half, k, :]
                        pe.matmul(ps[0:rows, u % 4, :], tok(oh[:, k, :], i), whk, start=(k == 0), stop=False)
                        pe.matmul(ps[0:rows, u % 4, :], tok(oh[:, k, :], i), wlk, start=False, stop=False)
                        last = pe.matmul(ps[0:rows, u % 4, :], tok(ol[:, k, :], i), whk, start=False, stop=(k == KH - 1))
                    if ks[-1] == KH - 1:
                        last.then_inc(y_full, 1)

                pe.wait_ge(proj_done, NP * e + NP - 1)
                pe.wait_ge(wl_done, 2 * e + 1)
                pe.wait_ge(out_done, KH * e + KH - 1)
                for u in range(3):
                    output(u, range(KH - 1))
                pe.wait_ge(out_done, KH * e + KH)
                for u in range(3):
                    output(u, (KH - 1,))
                pe.wait_ge(proj_done, NP * e + NP)
                for u in range(3, NY):
                    if u == NT + 1:
                        pe.wait_ge(wl_done, 2 * e + 2)
                    if u >= 4:
                        pe.wait_ge(y_done, NY * e + u - 2)
                    output(u, range(KH))

        @block.scalar
        def _(act):
            act.wait_ge(zero_set, 1)
            with act.Fori(0, HC) as e:
                for m in range(4):
                    act.wait_ge(proj_full, NP * e + X_ + m + 1)
                    if m == 0:
                        act.wait_ge(pads, e + 1)
                    b0 = 3 * (m % 2)
                    act.activation(xq[:, m, CP:CP + PROMPT], flat(b0, b0 + 3, 0, PROMPT), ACT.Copy)
                    new = flat(b0, b0 + 3, SC, T).rearrange("p (b t) -> p b t", t=TS)
                    a = xq[:, m, XS + CP:XS + CP + 1]
                    act.activation(bass.AP(a.tensor, a.offset, [a.ap[0], [CP + TS, B], [1, TS]]), new, ACT.Copy)
                    act.activation(xc[:, m, :].rearrange("p (b t) -> p b t", t=CP), new[:, :, TS - CP:TS], ACT.Copy)
                    act.activation(x8[:, m, :], flat(b0, b0 + 3, PROMPT, T), ACT.Copy).then_inc(proj_done, 1)
                    act.wait_ge(proj_done, NP * e + m + 1)
                    if m >= 2:
                        act.wait_ge(ca_done, KH * e + m - 1)
                    act.activation(hT[:, m % 2, 0:XW - CP], xq[:, m, 0:XW - CP], ACT.Identity,
                                   bias=hv[:, W_BIAS, m:m + 1], scale=hv[:, W_TAP, m:m + 1]).then_inc(conv0, 1)

                    def silu(m):
                        act.wait_ge(conv, 3 * KH * e + 3 * m + 3)
                        c = hT[:, m % 2, :]
                        act.activation(ca[:, m, 0:PROMPT], c[:, 0:PROMPT], ACT.Silu)
                        act.activation(ca[:, m, PROMPT:PROMPT + META], c[:, 0:META], ACT.Silu)
                        a = c[:, XS:XS + 1]
                        act.activation(ca[:, m, SC:T].rearrange("p (b t) -> p b t", t=TS),
                                       bass.AP(a.tensor, a.offset, [a.ap[0], [CP + TS, B], [1, TS]]), ACT.Silu).then_inc(ca_done, 1)
                    if m >= 1:
                        silu(m - 1)
                silu(3)
                def exponent(x, rows):
                    act.wait_ge(arg_done, NCH * e + x + 1)
                    act.activation(ex[0:rows, 0:rows], arg[0:rows, 0:rows], ACT.Exp).then_inc(ex_done, 1)

                for j in range(K_, Z_):
                    if j == Z_ - 1:
                        exponent(0, R8)
                    act.wait_ge(proj_full, NP * e + j + 1)
                    b0 = 3 * (j % 2)
                    dst, scale = (kz, DH ** -0.5) if j < Q_ else (xq, 1.0)
                    act.activation(dst[:, j % 4, :], flat(b0, b0 + 3, 0, T), ACT.Copy, scale=scale).then_inc(proj_done, 1)

                act.wait_ge(kt_full, NCH * e + 1)
                act.activation(kw[S0:R8, 0, :], ps[S0:R8, 5, :], ACT.Copy, scale=hc[S0:R8, NT, Q_STATE:Q_STATE + 1])
                act.activation(kw[0:S0, 0, :], ps[0:S0, 5, :], ACT.Copy, scale=hc[0:S0, NT, Q_STATE:Q_STATE + 1]).then_inc(kt_done, 1)
                act.wait_ge(kt_done, NCH * e + 1)
                for q in range(2):
                    last = act.activation(kb[S0 * q:S0 * (q + 1), 1, :], kw[0:S0, 0, :], ACT.Copy)
                last.then_inc(km_high, 1)
                for q in range(2):
                    last = act.activation(ks[NS * q:NS * (q + 1), :], kw[S0:R8, 0, :], ACT.Copy)
                last.then_inc(kh_done, 1)
                for c in range(NT):
                    x = c + 1
                    exponent(x, P)
                    act.wait_ge(kt_full, NCH * e + x + 1)
                    if c >= 1:
                        act.wait_ge(kv_full, NKV * e + kv_unit(c - 2, KH - 1) + 1)
                    act.activation(kw[:, x % 2, :], ps[:, 5, :], ACT.Copy, scale=hc[:, c, Q_STATE:Q_STATE + 1]).then_inc(kt_done, 1)
                    if c < B:
                        if c == 0:
                            act.wait_ge(ks_done, e + 1)
                        if c >= 1:
                            act.wait_ge(kv_full, NKV * e + (kv_unit(("s", c - 2), KH - 1) if c >= 2 else kv_unit(-1, KH - 1)) + 1)
                        act.activation(kb[:, c % 2, :], ks[:, :], ACT.Copy, scale=const[:, C_OWN + c:C_OWN + c + 1]).then_inc(kb_done, 1)
                    if c < KH:
                        last = act.activation(ca[:, c, :], ca[:, c, :], ACT.Copy, scale=hv[:, W_SKIP, c:c + 1])
                        if c == KH - 1:
                            last.then_inc(skipped, 1)
                    act.wait_ge(i_full, NCH * e + x)
                    if c >= 1:
                        act.wait_ge(h_done, NCH * e + c)
                    act.activation(t1, ps[:, 0, :], ACT.Copy, scale=hc[:, c, Q_INTER:Q_INTER + 1]).then_inc(i_done, 1)
                act.wait_ge(i_full, NCH * e + NCH)
                act.wait_ge(h_done, NCH * e + NT)
                act.activation(t1[S0:R8, :], ps[S0:R8, 7, :], ACT.Copy, scale=hc[S0:R8, NT, Q_INTER:Q_INTER + 1]).then_inc(i_done, 1)
                act.wait_ge(var_done, e + 1)
                act.activation(r2[:, :], r2[:, :], ACT.Sqrt).then_inc(root_done, 1)
                act.wait_ge(scale_done, e + 1)
                for i in range(NT + 1):
                    rows = P if i < NT else R8
                    act.activation(v[0:rows, i, :], v[0:rows, i, :], ACT.Identity, scale=r1[0:rows, i:i + 1], bias=r2[0:rows, i:i + 1]).then_inc(hn_done, 1)
                def high_output(k):
                    act.wait_ge(gated, KH * e + k + 1)
                    act.activation(oh[:, k, META:T], hT[:, k, META:T], ACT.Copy).then_inc(oh_done, 1)

                def high_weights(half):
                    act.wait_ge(w_in[1 + half], 48 * e + 48)
                    act.activation(wh[:, KH * half:KH * (half + 1), :], w[:, 1 + half], ACT.Copy).then_inc(wh_done, 1)

                for m in range(4):
                    act.wait_ge(proj_full, NP * e + Z_ + m + 1)
                    b0 = 3 * (m % 2)
                    act.activation(kz[:, m, :], flat(b0, b0 + 3, 0, T), ACT.Silu).then_inc(proj_done, 1)
                    if m == 1:
                        act.wait_ge(ht_full, NCH * (e + 1))
                        high_weights(0)
                    high_output(m)
                high_weights(1)

        @block.vector
        def _(dve):
            V = 25
            dve.memset(den[:, :], 1.0)
            dve.memset(hc[:, :, :], 1.0)
            dve.memset(mv[:, :, :], 0.0)
            dve.memset(qm[:, :, :, :], 0.0).then_inc(zero_set, 1)
            for sem, k in ((y_done, 1), (all_stored, 1)):
                dve.sem_inc(sem, k)
            dve.wait_ge(zero_set, 1)
            with dve.Fori(0, HC) as e:
                count = [0]

                def link(ins):
                    count[0] += 1
                    ins.then_inc(vec, 1)
                    dve.wait_ge(vec, V * e + count[0])

                dve.wait_ge(y_done, NY * e + 1)
                dve.tensor_scalar(hv[:, :, :], wcol[:, :, bass.ds(KH * e, KH)], 1.0, None, ALU.mult)
                dve.tensor_scalar(hc[:, 0:NT, :], cols[:, 0:NT, :, bass.ds(e, 1)].rearrange("p i n o -> p i (n o)"), 1.0, None, ALU.mult)
                dve.tensor_scalar(hc[0:R8, NT, :], cols[0:R8, NT, :, bass.ds(e, 1)].rearrange("p n o -> p (n o)"), 1.0, None, ALU.mult)
                dve.tensor_scalar(d8[:, :], decay8[:, bass.ds(e, 1)], 1.0, None, ALU.mult).then_inc(head_set, 1)
                dve.wait_ge(head_set, e + 1)
                dve.memset(xq[:, :, 0:CP], 0.0)
                dve.memset(ca[:, :, PROMPT + META:SC], 0.0)
                for k in range(KH):
                    a = xq[:, k, XS:XS + 1]
                    last = dve.tensor_scalar(bass.AP(a.tensor, a.offset, [a.ap[0], [CP + TS, B], [1, CP]]),
                                             preC[:, bass.ds(KH * e + k, 1), :].rearrange("p o (b r) -> p (o b) r", r=CP), 1.0, None, ALU.mult)
                last.then_inc(pads, 1)
                for m in range(KH):
                    dve.wait_ge(conv0, KH * e + m + 1)
                    c = hT[:, m % 2, 0:XW - CP]
                    for j in range(1, CW):
                        dve.scalar_tensor_tensor(c, xq[:, m, j:j + XW - CP], hv[:, W_TAP + j, m:m + 1], c, ALU.mult, ALU.add).then_inc(conv, 1)
                        if j < CW - 1:
                            dve.wait_ge(conv, 3 * KH * e + 3 * m + j)
                for i in range(NT + 1):
                    rows = P if i < NT else R8
                    dve.wait_ge(v_full, NV * e + i + 1)
                    dve.tensor_copy(v[0:rows, i, :], ps[0:rows, 6 + i % 2, :]).then_inc(v_done, 1)
                dve.wait_ge(all_stored, e + 1)
                dve.wait_ge(v_full, NV * e + NT + 2)
                dve.tensor_copy(crow[S0:S0 + CP, :], ps[0:CP, 7, :]).then_inc(v_done, 1)
                dve.wait_ge(v_full, NV * e + NT + 3)
                dve.tensor_copy(crow[0:B * CP, :], ps[0:B * CP, 6, :]).then_inc(v_done, 1)

                dve.wait_ge(ub_in, 16 * e + 16)

                def log_weights(x, rows, c0, g, mask):
                    if x >= 1:
                        dve.wait_ge(ex_done, NCH * e + x)
                    dve.scalar_tensor_tensor(arg[0:rows, 0:rows], ub[0:rows, c0:c0 + rows], g, const[0:rows, mask:mask + rows],
                                             ALU.add, ALU.min).then_inc(arg_done, 1)

                def weigh(x, rows):
                    dve.wait_ge(ex_done, NCH * e + x + 1)
                    dve.wait_ge(s_full, NCH * e + x + 1)
                    dve.tensor_tensor(sT[0:rows, x % 2, 0:rows], ps[0:rows, 4, 0:rows], ex[0:rows, 0:rows], ALU.mult).then_inc(s_done, 1)

                def chunk_weights(c):
                    log_weights(c + 1, P, META + P * c, hc[:, c, Q_G:Q_G + 1], C_CAUSAL)

                log_weights(0, R8, PROMPT, hc[0:R8, NT, Q_G:Q_G + 1], C_BLOCK8)
                dve.wait_ge(v_done, NV * e + NT + 1)
                for q in (2, 0, 1):
                    last = dve.tensor_copy(vs[NS * q:NS * (q + 1), :], v[S0:R8, NT, :])
                link(last)
                link(dve.tensor_tensor(vs[S0:R8, :], v[S0:R8, NT, :], vs[S0:R8, :].bitcast(F32), ALU.subtract))
                dve.tensor_copy(vs[96:P, :], vs[S0:R8, :]).then_inc(vs_done, 1)
                for q in (0, 2):
                    last = dve.tensor_copy(vm[S0 * q:S0 * (q + 1), :], v[0:S0, NT, :])
                link(last)
                link(dve.tensor_tensor(vm[S0:R8, :], v[0:S0, NT, :], vm[0:S0, :].bitcast(F32), ALU.subtract))
                dve.tensor_copy(vm[96:P, :], vm[S0:R8, :]).then_inc(vm_done, 1)
                dve.wait_ge(proj_done, NP * e + Z_)
                for k in range(KH):
                    a = qm[:, k, 0, 0:1]
                    last = dve.tensor_copy(bass.AP(a.tensor, a.offset, [a.ap[0], [NS + TS, B], [1, TS]]), xq[:, k, SC:T].rearrange("p (b t) -> p b t", t=TS))
                last.then_inc(qm_done, 1)
                weigh(0, R8)
                dve.wait_ge(n0_full, e + 1)
                dve.tensor_copy(n0[:, :, :], ps[:, 7, 0:KH * B].rearrange("p (k b) -> p k b", b=B)).then_inc(n0_done, 1)
                chunk_weights(0)
                dve.wait_ge(km_high, e + 1)
                link(dve.tensor_tensor(kb[R8:96, 1, :], kw[0:S0, 0, :], kb[0:S0, 1, :].bitcast(F32), ALU.subtract))
                dve.tensor_copy(kb[96:P, 1, :], kb[R8:96, 1, :]).then_inc(km_done, 1)
                dve.wait_ge(kh_done, e + 1)
                link(dve.tensor_tensor(ks[R8:96, :], kw[S0:R8, 0, :], ks[S0:R8, :].bitcast(F32), ALU.subtract))
                dve.tensor_copy(ks[96:P, :], ks[R8:96, :]).then_inc(ks_done, 1)
                dve.wait_ge(h_full, NCH * e + 1)
                dve.tensor_copy(n[:, :], ps[:, 6, 2:2 + KH]).then_inc(n_done, 1)
                dve.wait_ge(ns_full, e + 1)
                dve.scalar_tensor_tensor(nrow[:, :], nrow[:, :], d8[:, 0:1], ps[0:B, 4, :], ALU.mult, ALU.add).then_inc(ns_done, 1)
                for m in range(KH):
                    dve.wait_ge(kv_full, NKV * e + m + 1)
                    dve.tensor_copy(C[:, m, :], ps[:, 2 + m % 2, :]).then_inc(kv_done, 1)
                dve.tensor_copy(v[0:R8, NT, :], ps[0:R8, 1, :])
                dve.tensor_copy(den[0:S0, NT:NT + 1], ps[0:S0, 6, 1:2])
                dve.tensor_copy(r1[S0:R8, NT:NT + 1], ps[S0:R8, 6, 1:2])
                link(dve.tensor_scalar(r2[S0:R8, NT:NT + 1], ps[S0:R8, 6, 0:1], hc[S0:R8, NT, Q_INTER:Q_INTER + 1], None, ALU.mult))
                dve.tensor_tensor(den[S0:R8, NT:NT + 1], r2[S0:R8, NT:NT + 1], r1[S0:R8, NT:NT + 1], ALU.add).then_inc(e_done, 1)
                for c in range(NT):
                    x = c + 1
                    weigh(x, P)
                    if c + 1 < NT:
                        chunk_weights(c + 1)
                    for m in range(KH):
                        u = kv_unit(c, m)
                        dve.wait_ge(kv_full, NKV * e + u + 1)
                        dve.scalar_tensor_tensor(C[:, m, :], C[:, m, :], ub[:, T + 1 + c:T + 2 + c], ps[:, 2 + u % 2, :], ALU.mult, ALU.add).then_inc(kv_done, 1)
                    for m in range(KH if c < B else 0):
                        u = kv_unit(("s", c), m)
                        dve.wait_ge(kv_full, NKV * e + u + 1)
                        dve.scalar_tensor_tensor(Cs[:, c % 2, m, :], Cs[:, c % 2, m, :], ub[:, T + NT + 1 + c:T + NT + 2 + c],
                                                 ps[:, 2 + u % 2, :], ALU.mult, ALU.add).then_inc(kv_done, 1)
                    dve.wait_ge(i_done, NCH * e + x)
                    dve.scalar_tensor_tensor(n[:, :], n[:, :], ub[:, T + 1 + c:T + 2 + c], ps[:, 6, 2:2 + KH], ALU.mult, ALU.add)
                    dve.tensor_tensor(v[:, c, :], t1, ps[:, 1, :], ALU.add)
                    dve.tensor_copy(r1[:, c:c + 1], ps[:, 6, 1:2])
                    link(dve.tensor_scalar(r2[:, c:c + 1], ps[:, 6, 0:1], hc[:, c, Q_INTER:Q_INTER + 1], None, ALU.mult))
                    dve.tensor_tensor(den[:, c:c + 1], r2[:, c:c + 1], r1[:, c:c + 1], ALU.add).then_inc(h_done, 1)
                    dve.wait_ge(h_done, NCH * e + x)
                    dve.bn_stats(bn[:, c, :], v[:, c, :])
                dve.wait_ge(i_done, NCH * e + NCH)
                dve.tensor_tensor(v[S0:R8, NT, :], v[S0:R8, NT, :], t1[S0:R8, :], ALU.add).then_inc(h_done, 1)
                dve.wait_ge(h_done, NCH * e + NCH)
                last = dve.bn_stats(bn[0:R8, NT, :], v[0:R8, NT, :])
                link(last)
                dve.sem_inc(passed, 1)
                for i in range(NT + 1):
                    rows = P if i < NT else R8
                    last = dve.bn_aggr(mv[0:rows, i, :], bn[0:rows, i, :])
                link(last)
                link(dve.scalar_tensor_tensor(den[:, :], den[:, :], -1.0, den[:, :], ALU.mult, ALU.max))
                link(dve.tensor_tensor(den[:, :], den[:, :], hc[:, :, Q_FLOOR:Q_FLOOR + 1].rearrange("p i o -> p (i o)"), ALU.max))
                link(dve.reciprocal(r1[:, :], den[:, :]))
                link(dve.tensor_tensor(r2[:, :], r1[:, :], r1[:, :], ALU.mult))
                link(dve.tensor_tensor(r2[:, :], r2[:, :], mv[:, :, 1], ALU.mult))
                dve.tensor_scalar(r2[:, :], r2[:, :], EPS, None, ALU.add).then_inc(var_done, 1)
                dve.wait_ge(root_done, e + 1)
                link(dve.reciprocal(den[:, :], r2[:, :]))
                link(dve.tensor_tensor(r1[:, :], r1[:, :], den[:, :], ALU.mult))
                dve.scalar_tensor_tensor(r2[:, :], mv[:, :, 0], -1.0, r1[:, :], ALU.mult, ALU.mult).then_inc(scale_done, 1)
                for i in range(NT + 1):
                    rows = P if i < NT else R8
                    dve.wait_ge(ht_full, NCH * e + i + 1)
                    src = ps[:, 6 + i % 2, :].rearrange("p (k r) -> p k r", r=P)[:, :, 0:rows]
                    c0 = META + P * i if i < NT else PROMPT
                    dve.tensor_copy(hT[:, :, c0:c0 + rows], src).then_inc(ht_done, 1)
                dve.wait_ge(skipped, e + 1)
                dve.wait_ge(ht_done, NCH * e + NCH)
                H = slice(META, T)
                for k in range(KH):
                    last = dve.scalar_tensor_tensor(hT[:, k, H], hT[:, k, H], hv[:, W_GAMMA, k:k + 1], ca[:, k, H], ALU.mult, ALU.add)
                link(last)

                def low_weights(half):
                    dve.wait_ge(wh_done, 2 * e + half + 1)
                    dve.tensor_tensor(wl[:, 1 + half], w[:, 1 + half], wh[:, KH * half:KH * (half + 1), :].bitcast(F32), ALU.subtract).then_inc(wl_done, 1)

                def low_output(k):
                    dve.wait_ge(oh_done, KH * e + k + 1)
                    dve.tensor_tensor(ol[:, k, H], hT[:, k, H], oh[:, k, H].bitcast(F32), ALU.subtract).then_inc(out_done, 1)

                for k in range(KH):
                    dve.wait_ge(proj_done, NP * e + Z_ + k + 1)
                    dve.tensor_tensor(hT[:, k, H], hT[:, k, H], kz[:, k, H], ALU.mult).then_inc(gated, 1)
                    if k == 1:
                        low_weights(0)
                    low_output(k)
                for u in range(NY):
                    rows = P if u % (NT + 1) < NT else R8
                    if u == 4:
                        low_weights(1)
                    dve.wait_ge(y_full, NY * e + u + 1)
                    dve.wait_ge(y_in[u % YB], 16 * (NY // YB) * e + 16 * (u // YB) + 16)
                    dve.tensor_tensor(ys[0:rows, u % YB, :], ys[0:rows, u % YB, :], ps[0:rows, u % 4, :], ALU.add).then_inc(y_done, 1)
                assert count[0] == V, count[0]


def final_stage(nc, d, h_dram):
    HS = 4
    with ExitStack() as ctx:
        s = Space(nc, ctx, "fin")
        h, sq, y = s.sb("h", [P, HS, D]), s.sb("sq", [P, 2, D]), s.sb("y", [P, 2, D])
        g = s.sb("g", [P, D])
        stat = s.sb("stat", [P, 2, 2])
        h_in, y_out = [s.sem(f"h_in{j}") for j in range(HS)], [s.sem("y_out0"), s.sem("y_out1")]
        g_in, ss_ready, msq_ready, rms_ready, rstd_ready, y_ready = (
            s.sem(n) for n in ("g_in", "ss_ready", "msq_ready", "rms_ready", "rstd_ready", "y_ready"))
        block = ctx.enter_context(nc.Block())
        rows_of = [P] * NT + [R8]

        @block.sync
        def _(sp):
            for i in range(NT + 1):
                if i >= HS:
                    sp.wait_ge(y_ready, i - HS + 1)
                sp.dma_start(h[0:rows_of[i], i % HS, :], h_dram[i, 0:rows_of[i]]).then_inc(h_in[i % HS], 16)
                if i == 0:
                    sp.dma_start(g[:, :], d["final_norm_g"].rearrange("(o c) -> o c", o=1).to_broadcast([P, D])).then_inc(g_in, 16)

        @block.gpsimd
        def _(pool):
            yp = d["out_yp"].rearrange("b (i p) c -> (b i) p c", p=P)
            for i in range(NT + 1):
                pool.wait_ge(y_ready, i + 1)
                if i < NT:
                    pool.dma_start(yp[i], y[:, i % 2, :]).then_inc(y_out[i % 2], 16)
                else:
                    pool.dma_start(d["out_ys"].rearrange("b t c -> (b t) c"), y[S0:R8, i % 2, :]).then_inc(y_out[i % 2], 16)
            pool.wait_ge(y_out[0], 16 * (NT // 2 + 1))
            pool.wait_ge(y_out[1], 16 * (NT // 2))

        @block.scalar
        def _(act):
            def squares(i):
                act.wait_ge(h_in[i % HS], 16 * (i // HS + 1))
                if i >= 2:
                    act.wait_ge(rstd_ready, i - 1)
                act.activation(sq[0:rows_of[i], i % 2, :], h[0:rows_of[i], i % HS, :], ACT.Square, accum_out=stat[0:rows_of[i], i % 2, 0:1]).then_inc(ss_ready, 1)

            squares(0)
            for i in range(NT + 1):
                if i < NT:
                    squares(i + 1)
                act.wait_ge(msq_ready, i + 1)
                act.activation(stat[0:rows_of[i], i % 2, 0:1], stat[0:rows_of[i], i % 2, 1:2], ACT.Sqrt).then_inc(rms_ready, 1)

        @block.vector
        def _(dve):
            def mean(i):
                dve.wait_ge(ss_ready, i + 1)
                if i >= 2:
                    dve.wait_ge(y_ready, i - 1)
                dve.tensor_scalar(stat[0:rows_of[i], i % 2, 1:2], stat[0:rows_of[i], i % 2, 0:1], 1.0 / D, EPS, ALU.mult, ALU.add).then_inc(msq_ready, 1)

            mean(0)
            dve.wait_ge(g_in, 16)
            for i in range(NT + 1):
                q, rows = i % 2, rows_of[i]
                if i < NT:
                    mean(i + 1)
                dve.wait_ge(rms_ready, i + 1)
                dve.reciprocal(stat[0:rows, q, 1:2], stat[0:rows, q, 0:1]).then_inc(rstd_ready, 1)
                dve.wait_ge(rstd_ready, i + 1)
                if i >= 2:
                    dve.wait_ge(y_out[q], 16 * (i // 2))
                dve.scalar_tensor_tensor(y[0:rows, q, :], h[0:rows, i % HS, :], stat[0:rows, q, 1:2], g[0:rows, :], ALU.mult, ALU.mult).then_inc(y_ready, 1)


def program(nc, d, h_dram, gate_dram):
    with ExitStack() as ctx:
        s = Space(nc, ctx, "all")
        const = s.sb("const", [P, C_W])
        vcol, wcol, biasB = s.sb("vcol", [P, V_ROWS]), s.sb("wcol", [P, W_KINDS, 16]), s.sb("biasB", [P, HA])
        xnT = s.sb("xnT", [P, KD, T])
        with ExitStack() as ctx0:
            s0 = Space(nc, ctx0, "even")
            mixT = s0.sb("mixT", [P, KD, T])
            prefT = s0.sb("prefT", [P, 4, B * PRE])
            qS, kS, gS = (s0.sb(n, [P, PAIRS, NS]) for n in ("qS", "kS", "gS"))
            vS = s0.sb("vS", [R8, WA])
            load_constants(nc, d, const, vcol, wcol, biasB, prefT)
            norm_stage(nc, d, "norm0", const, vcol, V_NORM, xnT, None, None)
            attention_pairs(nc, d, const, biasB, xnT, mixT, qS, kS, gS, vS)
            with ExitStack() as ctx2:
                s2 = Space(nc, ctx2, "paged")
                table = s2.sb("table", [1, B * PAGES], I32)
                vp = s2.sb("vp", [P, B // 2, PAGES, WA])
                v_in = [s2.sem(f"v_in{j}") for j in range(B // 2)]
                pool_groups(nc, d, const, vcol, prefT, xnT, mixT, table, vp, v_in)
                decode_attention(nc, d, const, xnT, mixT, qS, kS, gS, vS, table, vp, v_in)
            norm_stage(nc, d, "norm1", const, vcol, V_NORM + KD, xnT, mixT, h_dram)
        with ExitStack() as ctx1:
            s1 = Space(nc, ctx1, "odd")
            cols = s1.sb("cols", [P, NT + 1, 4, HC])
            decay8 = s1.sb("decay8", [B, HC])
            preC = s1.sb("preC", [P, INNER // P, B * CP])
            w = s1.sb("w", [P, 3, KH, DH])
            w_in = [s1.sem(f"w_in{j}") for j in range(3)]
            gate_stage(nc, d, const, xnT, cols, decay8, preC, gate_dram, w, w_in)
            head_loop(nc, d, const, wcol, cols, decay8, preC, gate_dram, h_dram, xnT, w, w_in, s1.place["w"])
        final_stage(nc, d, h_dram)


def kernel(**inputs):
    import concourse.bacc as _bacc
    from concourse.bass_utils import run_bass_kernel_spmd as _run

    nc = _bacc.Bacc("TRN2", target_bir_lowering=False, num_devices=1)
    arrays = {n: np.ascontiguousarray(a) for n, a in inputs.items()}
    arrays["consts"], arrays["carry"] = constant_table(), carry_table()
    d = {n: nc.dram_tensor(f"in_{n}", a.shape, mybir.dt.from_np(a.dtype), kind="ExternalInput").ap() for n, a in arrays.items()}
    d.update({n: nc.dram_tensor(n, shape, F32, kind="ExternalOutput").ap() for n, shape in _OUTS.items()})
    h_dram = nc.dram_tensor("h_dram", (NT + 1, P, D), F32, kind="Internal").ap()
    gate_dram = nc.dram_tensor("gate_dram", (HC, T + NT + 1 + B), F32, kind="Internal").ap()
    program(nc, d, h_dram, gate_dram)
    r = _run(nc, [{f"in_{n}": a for n, a in arrays.items()}], core_ids=[0]).results[0]
    return tuple(r[n] for n in _RETURNS)
```
